# Optimizing a Trainium2 kernel written in Bass

```python
import math
import jax, jax.numpy as jnp
from jax import lax
import numpy as np

D_MODEL = 1024
BATCH = 1
SEQ = 256
DEPTH = 2

GRID_W = 64
ROPE_THETA = 10000.0
Q_BLOCK = 128
EPS = 1e-6
PLE_DIM = 256

MLA_HEADS = 8
MLA_Q_LORA = 256
MLA_KV_LORA = 128
MLA_NOPE = 64
MLA_ROPE = 32
MLA_V = 64

GLA_HEADS = 4
GLA_DK = 64
GLA_DV = 128
GLA_GATE_RANK = 16
GLA_GATE_NORM = 16.0
GLA_CHUNK = 64

GQA_HEADS = 16
GQA_KV_HEADS = 4
GQA_HEAD_DIM = 64

N_EXPERTS = 16
EC_CAPACITY_FACTOR = 2
EXPERT_FF = 1024

D_MIX = MLA_HEADS * MLA_V + GLA_HEADS * GLA_DV
EVEN_SPLITS = (MLA_Q_LORA, MLA_KV_LORA, MLA_ROPE,
               GLA_HEADS * GLA_DK, GLA_HEADS * GLA_DK, GLA_HEADS * GLA_DV,
               2 * GLA_GATE_RANK, GLA_HEADS * GLA_DV)
ODD_SPLITS = (GQA_HEADS * GQA_HEAD_DIM, GQA_KV_HEADS * GQA_HEAD_DIM, GQA_KV_HEADS * GQA_HEAD_DIM)
N_EVEN = (DEPTH + 1) // 2
N_ODD = DEPTH // 2
DEEPNORM_ALPHA = (2.0 * DEPTH) ** 0.25
DEEPNORM_BETA = (8.0 * DEPTH) ** -0.25


def _split(h, sizes):
    offs = np.cumsum(sizes)[:-1].tolist()
    return jnp.split(h, offs, axis=-1)

def rms_norm(x, g):
    x32 = x.astype(jnp.float32)
    y = x32 * lax.rsqrt(jnp.mean(x32 * x32, axis=-1, keepdims=True) + EPS)
    return (y * g.astype(jnp.float32)).astype(x.dtype)

def layer_norm(x, g, b):
    x32 = x.astype(jnp.float32)
    mu = jnp.mean(x32, axis=-1, keepdims=True)
    xc = x32 - mu
    var = jnp.mean(xc * xc, axis=-1, keepdims=True)
    y = xc * lax.rsqrt(var + EPS) * g.astype(jnp.float32) + b.astype(jnp.float32)
    return y.astype(x.dtype)

def axial_rope(seq, rot_dim):
    rows = seq // GRID_W
    row = jnp.repeat(jnp.arange(rows, dtype=jnp.float32), GRID_W)
    col = jnp.tile(jnp.arange(GRID_W, dtype=jnp.float32), rows)
    axis_dim = rot_dim // 2
    inv = ROPE_THETA ** (-jnp.arange(0, axis_dim, 2, dtype=jnp.float32) / axis_dim)
    ang = jnp.concatenate([row[:, None] * inv, col[:, None] * inv], axis=-1)
    return jnp.cos(ang), jnp.sin(ang)

def apply_rope(x, cos, sin):
    half = x.shape[-1] // 2
    c = cos.astype(x.dtype)
    s = sin.astype(x.dtype)
    x1, x2 = x[..., :half], x[..., half:]
    return jnp.concatenate([x1 * c - x2 * s, x1 * s + x2 * c], axis=-1)

def _to_blocks(t):
    b, s = t.shape[:2]
    nb = s // Q_BLOCK
    return t.reshape((b, nb, Q_BLOCK) + t.shape[2:]).swapaxes(0, 1)

def _from_blocks(t):
    nb, b, qb = t.shape[:3]
    return t.swapaxes(0, 1).reshape((b, nb * qb) + t.shape[3:])

def mla_attention(q_nope, q_pe, k_nope, k_pe, v):
    scale = (MLA_NOPE + MLA_ROPE) ** -0.5

    def block(args):
        qn, qp = args
        s = (jnp.einsum('bqhd,bkhd->bhqk', qn, k_nope)
             + jnp.einsum('bqhd,bkd->bhqk', qp, k_pe)) * scale
        pr = jax.nn.softmax(s.astype(jnp.float32), axis=-1).astype(v.dtype)
        return jnp.einsum('bhqk,bkhd->bqhd', pr, v)

    o = lax.map(block, (_to_blocks(q_nope), _to_blocks(q_pe)))
    return _from_blocks(o)

def gla_chunked(q, k, v, log_a):
    b, s, h, dk = q.shape
    dv = v.shape[-1]
    n = s // GLA_CHUNK
    L = GLA_CHUNK

    def chunk(t):
        return t.astype(jnp.float32).reshape(b, n, L, h, t.shape[-1]).transpose(0, 3, 1, 2, 4)

    qc, kc, vc, lac = chunk(q), chunk(k), chunk(v), chunk(log_a)
    cum = jnp.cumsum(lac, axis=-2)
    qg = qc * jnp.exp(cum)
    kg = kc * jnp.exp(-cum)
    tri = jnp.tril(jnp.ones((L, L), dtype=bool))
    att = jnp.where(tri, jnp.einsum('bhnld,bhnmd->bhnlm', qg, kg), 0.0)
    o_intra = jnp.einsum('bhnlm,bhnme->bhnle', att, vc)
    last = cum[..., -1:, :]
    u = jnp.einsum('bhnld,bhnle->bhnde', kc * jnp.exp(last - cum), vc)
    decay = jnp.exp(last[..., 0, :])

    def step(state, inp):
        d, du = inp
        return d[..., None] * state + du, state

    init = jnp.zeros((b, h, dk, dv), jnp.float32)
    _, s_prev = lax.scan(step, init, (jnp.moveaxis(decay, 2, 0), jnp.moveaxis(u, 2, 0)))
    o_inter = jnp.einsum('bhnld,nbhde->bhnle', qg, s_prev)
    o = (o_intra + o_inter).transpose(0, 2, 3, 1, 4).reshape(b, s, h, dv)
    return o.astype(v.dtype)

def even_mixer(x, w_in, mla_q_norm, w_uq, mla_kv_norm, w_ukv,
               gla_gate_w_fwd, gla_gate_b_fwd, gla_gate_w_bwd, gla_gate_b_bwd, gla_norm,
               cos_a, sin_a):
    b, s, _ = x.shape
    h = x @ w_in
    c_q, c_kv, k_pe, gq, gk, gv, g_lr, gr = _split(h, EVEN_SPLITS)

    q = (rms_norm(c_q, mla_q_norm) @ w_uq).reshape(b, s, MLA_HEADS, MLA_NOPE + MLA_ROPE)
    q_nope = q[..., :MLA_NOPE]
    q_pe = apply_rope(q[..., MLA_NOPE:], cos_a[:, None, :], sin_a[:, None, :])
    kv = (rms_norm(c_kv, mla_kv_norm) @ w_ukv).reshape(b, s, MLA_HEADS, MLA_NOPE + MLA_V)
    k_nope, v_mla = kv[..., :MLA_NOPE], kv[..., MLA_NOPE:]
    k_pe = apply_rope(k_pe, cos_a, sin_a)
    o_mla = mla_attention(q_nope, q_pe, k_nope, k_pe, v_mla).reshape(b, s, MLA_HEADS * MLA_V)

    qh = (gq * (GLA_DK ** -0.5)).reshape(b, s, GLA_HEADS, GLA_DK)
    kh = gk.reshape(b, s, GLA_HEADS, GLA_DK)
    vh = gv.reshape(b, s, GLA_HEADS, GLA_DV)
    lr_f, lr_b = g_lr[..., :GLA_GATE_RANK], g_lr[..., GLA_GATE_RANK:]
    la_f = (jax.nn.log_sigmoid((lr_f @ gla_gate_w_fwd + gla_gate_b_fwd).astype(jnp.float32))
            / GLA_GATE_NORM).reshape(b, s, GLA_HEADS, GLA_DK)
    la_b = (jax.nn.log_sigmoid((lr_b @ gla_gate_w_bwd + gla_gate_b_bwd).astype(jnp.float32))
            / GLA_GATE_NORM).reshape(b, s, GLA_HEADS, GLA_DK)
    o_f = gla_chunked(qh, kh, vh, la_f)
    flip = lambda t: jnp.flip(t, axis=1)
    o_b = flip(gla_chunked(flip(qh), flip(kh), flip(vh), flip(la_b)))
    o_gla = rms_norm(o_f + o_b, gla_norm).reshape(b, s, GLA_HEADS * GLA_DV) * jax.nn.silu(gr)

    return jnp.concatenate([o_mla, o_gla], axis=-1)

def odd_mixer(x, w_in, gqa_q_norm, gqa_k_norm, cos_c, sin_c):
    b, s, _ = x.shape
    g = GQA_HEADS // GQA_KV_HEADS
    q, k, v = _split(x @ w_in, ODD_SPLITS)
    q = rms_norm(q.reshape(b, s, GQA_HEADS, GQA_HEAD_DIM), gqa_q_norm)
    k = rms_norm(k.reshape(b, s, GQA_KV_HEADS, GQA_HEAD_DIM), gqa_k_norm)
    v = v.reshape(b, s, GQA_KV_HEADS, GQA_HEAD_DIM)
    q = apply_rope(q, cos_c[:, None, :], sin_c[:, None, :]).reshape(b, s, GQA_KV_HEADS, g, GQA_HEAD_DIM)
    k = apply_rope(k, cos_c[:, None, :], sin_c[:, None, :])
    scale = GQA_HEAD_DIM ** -0.5

    def block(qb):
        sc = jnp.einsum('bqkgd,bskd->bkgqs', qb, k) * scale
        pr = jax.nn.softmax(sc.astype(jnp.float32), axis=-1).astype(v.dtype)
        return jnp.einsum('bkgqs,bskd->bqkgd', pr, v)

    o = _from_blocks(lax.map(block, _to_blocks(q)))
    return o.reshape(b, s, GQA_HEADS * GQA_HEAD_DIM)

def expert_choice_moe(x, router_w, w1, w3, w2):
    b, s, d = x.shape
    cap = EC_CAPACITY_FACTOR * s // N_EXPERTS
    aff = jax.nn.softmax(jnp.einsum('bsd,de->bse', x, router_w).astype(jnp.float32), axis=-1)
    gates, idx = lax.top_k(aff.transpose(0, 2, 1), cap)
    xg = jax.vmap(lambda xb, ib: xb[ib])(x, idx)
    hid = jax.nn.silu(jnp.einsum('becd,edf->becf', xg, w1)) * jnp.einsum('becd,edf->becf', xg, w3)
    ye = jnp.einsum('becf,efd->becd', hid, w2) * gates[..., None].astype(x.dtype)
    return jax.vmap(lambda yb, ib: jnp.zeros((s, d), x.dtype).at[ib.reshape(-1)].add(yb.reshape(-1, d)))(ye, idx)

def first_inputs(seed: int = 0) -> dict:
    key = jax.random.key(seed)
    ks = iter(jax.random.split(key, 40))
    f32 = jnp.float32

    def nrm(shape, scale):
        return jax.random.normal(next(ks), shape, f32) * scale

    def gain(shape):
        return 1.0 + 0.02 * jax.random.normal(next(ks), shape, f32)

    d_even_in = sum(EVEN_SPLITS)
    d_odd_in = sum(ODD_SPLITS)
    NE, NO = N_EVEN, N_ODD
    return {
        "x": nrm((BATCH, SEQ, D_MODEL), 1.0),
        "p": nrm((DEPTH, BATCH, SEQ, PLE_DIM), 1.0),
        "w_in_even": nrm((NE, D_MODEL, d_even_in), D_MODEL ** -0.5),
        "mla_q_norm": gain((NE, MLA_Q_LORA)),
        "w_uq": nrm((NE, MLA_Q_LORA, MLA_HEADS * (MLA_NOPE + MLA_ROPE)), MLA_Q_LORA ** -0.5),
        "mla_kv_norm": gain((NE, MLA_KV_LORA)),
        "w_ukv": nrm((NE, MLA_KV_LORA, MLA_HEADS * (MLA_NOPE + MLA_V)), MLA_KV_LORA ** -0.5),
        "gla_gate_w_fwd": nrm((NE, GLA_GATE_RANK, GLA_HEADS * GLA_DK), GLA_GATE_RANK ** -0.5),
        "gla_gate_b_fwd": nrm((NE, GLA_HEADS * GLA_DK), 0.1),
        "gla_gate_w_bwd": nrm((NE, GLA_GATE_RANK, GLA_HEADS * GLA_DK), GLA_GATE_RANK ** -0.5),
        "gla_gate_b_bwd": nrm((NE, GLA_HEADS * GLA_DK), 0.1),
        "gla_norm": gain((NE, GLA_DV)),
        "w_in_odd": nrm((NO, D_MODEL, d_odd_in), D_MODEL ** -0.5),
        "gqa_q_norm": gain((NO, GQA_HEAD_DIM)),
        "gqa_k_norm": gain((NO, GQA_HEAD_DIM)),
        "w_o": nrm((DEPTH, D_MIX, D_MODEL), D_MIX ** -0.5 * DEEPNORM_BETA),
        "ln1_g": gain((DEPTH, D_MODEL)),
        "ln1_b": nrm((DEPTH, D_MODEL), 0.02),
        "router_w": nrm((DEPTH, D_MODEL, N_EXPERTS), D_MODEL ** -0.5),
        "w1": nrm((DEPTH, N_EXPERTS, D_MODEL, EXPERT_FF), D_MODEL ** -0.5),
        "w3": nrm((DEPTH, N_EXPERTS, D_MODEL, EXPERT_FF), D_MODEL ** -0.5),
        "w2": nrm((DEPTH, N_EXPERTS, EXPERT_FF, D_MODEL), EXPERT_FF ** -0.5 * DEEPNORM_BETA),
        "ple_gate_w": nrm((DEPTH, D_MODEL, D_MODEL), D_MODEL ** -0.5),
        "ple_gate_b": nrm((DEPTH, D_MODEL), 0.02),
        "ple_w": nrm((DEPTH, PLE_DIM, D_MODEL), PLE_DIM ** -0.5 * DEEPNORM_BETA),
        "ln2_g": gain((DEPTH, D_MODEL)),
        "ln2_b": nrm((DEPTH, D_MODEL), 0.02),
    }

def first_block(x, p, w_in_even, mla_q_norm, w_uq, mla_kv_norm, w_ukv,
              gla_gate_w_fwd, gla_gate_b_fwd, gla_gate_w_bwd, gla_gate_b_bwd, gla_norm,
              w_in_odd, gqa_q_norm, gqa_k_norm,
              w_o, ln1_g, ln1_b, router_w, w1, w3, w2,
              ple_gate_w, ple_gate_b, ple_w, ln2_g, ln2_b):
    seq = x.shape[1]
    cos_a, sin_a = axial_rope(seq, MLA_ROPE)
    cos_c, sin_c = axial_rope(seq, GQA_HEAD_DIM)
    for i in range(DEPTH):
        if i % 2 == 0:
            j = i // 2
            mix = even_mixer(x, w_in_even[j], mla_q_norm[j], w_uq[j], mla_kv_norm[j], w_ukv[j],
                             gla_gate_w_fwd[j], gla_gate_b_fwd[j], gla_gate_w_bwd[j], gla_gate_b_bwd[j],
                             gla_norm[j], cos_a, sin_a)
        else:
            j = i // 2
            mix = odd_mixer(x, w_in_odd[j], gqa_q_norm[j], gqa_k_norm[j], cos_c, sin_c)
        x = layer_norm(DEEPNORM_ALPHA * x + mix @ w_o[i], ln1_g[i], ln1_b[i])
        ffn = expert_choice_moe(x, router_w[i], w1[i], w3[i], w2[i])
        ple = jax.nn.sigmoid(x @ ple_gate_w[i] + ple_gate_b[i]) * (p[i] @ ple_w[i])
        x = layer_norm(DEEPNORM_ALPHA * x + ffn + ple, ln2_g[i], ln2_b[i])
    return x


HEAD_DIM = 64
RET_HEADS = (3 * D_MODEL // 8) // HEAD_DIM
MOBA_HEADS = (3 * D_MODEL // 8) // HEAD_DIM
CONV_GROUPS = (D_MODEL // 4) // HEAD_DIM
RET_WIDTH = RET_HEADS * HEAD_DIM
MOBA_WIDTH = MOBA_HEADS * HEAD_DIM
CONV_WIDTH = CONV_GROUPS * HEAD_DIM
MIX_WIDTH = RET_WIDTH + MOBA_WIDTH + CONV_WIDTH
IN_WIDTH = 4 * RET_WIDTH + 3 * MOBA_WIDTH + 2 * CONV_WIDTH
D_FF = ((8 * D_MODEL // 3 + 255) // 256) * 256
RET_CHUNK = 256
RET_ROT_BASE = 10000.0
MOBA_BLOCK = 256
MOBA_TOPK = 3
MOBA_QBLOCK = 128
ROPE_THETA_2 = 500000.0
ROPE_DIMS = HEAD_DIM // 4
CONV_KERNEL = 31
FFN_RES_WEIGHT = 0.5
PAD_MULT = 256


def rms_norm_2(x, g):
    xf = x.astype(jnp.float32)
    y = xf * lax.rsqrt(jnp.mean(xf * xf, -1, keepdims=True) + EPS)
    return (y * g.astype(jnp.float32)).astype(x.dtype)

def swiglu(h, wg, wu, wd):
    return (jax.nn.silu(h @ wg) * (h @ wu)) @ wd

def to_heads(t, n_heads):
    b, s, _ = t.shape
    return t.reshape(b, s, n_heads, HEAD_DIM).transpose(0, 2, 1, 3)

def from_heads(t):
    b, h, s, d = t.shape
    return t.transpose(0, 2, 1, 3).reshape(b, s, h * d)

def rotary(x, pos, inv_freq):
    half = inv_freq.shape[0]
    n_rot = 2 * half
    ang = pos.astype(jnp.float32)[:, None, :, None] * inv_freq
    cos, sin = jnp.cos(ang), jnp.sin(ang)
    xr = x[..., :n_rot].astype(jnp.float32)
    x1, x2 = xr[..., :half], xr[..., half:]
    rot = jnp.concatenate([x1 * cos - x2 * sin, x2 * cos + x1 * sin], -1).astype(x.dtype)
    return jnp.concatenate([rot, x[..., n_rot:]], -1)

def retention(q, k, v):
    b, h, s, d = q.shape
    c = RET_CHUNK
    n = s // c
    log_gamma = jnp.log1p(-jnp.exp2(-5.0 - jnp.arange(h, dtype=jnp.float32)))
    lg = log_gamma[:, None]
    qc = q.reshape(b, h, n, c, d)
    kc = (k * (d ** -0.5)).reshape(b, h, n, c, d)
    vc = v.reshape(b, h, n, c, d)
    idx = jnp.arange(c, dtype=jnp.float32)
    rel = idx[:, None] - idx[None, :]
    decay_in = jnp.where(rel >= 0, jnp.exp(lg[:, :, None] * jnp.maximum(rel, 0.0)), 0.0)
    scores = jnp.einsum('bhncd,bhnmd->bhncm', qc, kc) * decay_in[None, :, None]
    inner = jnp.einsum('bhncm,bhnme->bhnce', scores, vc)
    w_state = jnp.exp(lg * (c - 1 - idx))
    kv = jnp.einsum('bhncd,hc,bhnce->bhnde', kc, w_state, vc)
    chunk_decay = jnp.exp(log_gamma * c).astype(kv.dtype)[None, :, None, None]

    def step(state, kv_i):
        return state * chunk_decay + kv_i, state

    _, prev = lax.scan(step, jnp.zeros((b, h, d, d), kv.dtype), jnp.moveaxis(kv, 2, 0))
    prev = jnp.moveaxis(prev, 0, 2)
    w_cross = jnp.exp(lg * (idx + 1.0))
    cross = jnp.einsum('bhncd,bhnde->bhnce', qc, prev) * w_cross[None, :, None, :, None]
    return (inner + cross).reshape(b, h, s, d)

def moba_attention(q, k, v):
    b, h, s, d = q.shape
    bs = MOBA_BLOCK
    nb = s // bs
    qb = MOBA_QBLOCK
    nq = s // qb
    topk = min(MOBA_TOPK, nb)
    scale = d ** -0.5
    kb = k.reshape(b, h, nb, bs, d)
    vb = v.reshape(b, h, nb, bs, d)
    kmean = jnp.mean(kb.astype(jnp.float32), axis=3)
    b_i = jnp.arange(b)[:, None, None]
    h_i = jnp.arange(h)[None, :, None]
    klocal = jnp.arange(bs)

    def one_qblock(args):
        qblk, qi = args
        qpos = qi * qb + jnp.arange(qb)
        own = (qi * qb) // bs
        gate = jnp.einsum('bhqd,bhnd->bhqn', qblk.astype(jnp.float32), kmean)
        gate = jnp.where(jnp.arange(nb) < own, gate, -jnp.inf)
        _, sel = lax.top_k(gate, topk)
        valid = sel < own
        k_own = lax.dynamic_index_in_dim(kb, own, axis=2, keepdims=False)
        v_own = lax.dynamic_index_in_dim(vb, own, axis=2, keepdims=False)
        s_own = jnp.einsum('bhqd,bhkd->bhqk', qblk, k_own).astype(jnp.float32) * scale
        causal = (own * bs + klocal)[None, :] <= qpos[:, None]
        s_list = [jnp.where(causal, s_own, -jnp.inf)]
        for j in range(topk):
            k_j = kb[b_i, h_i, sel[..., j]]
            s_j = jnp.einsum('bhqd,bhqkd->bhqk', qblk, k_j).astype(jnp.float32) * scale
            s_list.append(jnp.where(valid[..., j, None], s_j, -jnp.inf))
        p = jax.nn.softmax(jnp.concatenate(s_list, -1), axis=-1).astype(v.dtype)
        out = jnp.einsum('bhqk,bhkd->bhqd', p[..., :bs], v_own)
        for j in range(topk):
            v_j = vb[b_i, h_i, sel[..., j]]
            out = out + jnp.einsum('bhqk,bhqkd->bhqd', p[..., (j + 1) * bs:(j + 2) * bs], v_j)
        return out

    qs = jnp.moveaxis(q.reshape(b, h, nq, qb, d), 2, 0)
    outs = lax.map(one_qblock, (qs, jnp.arange(nq)))
    return jnp.moveaxis(outs, 0, 2).reshape(b, h, s, d)

def conv_module(a, gate, w, bias, ln_g, ln_b):
    bsz, s, c = a.shape
    u = a * jax.nn.sigmoid(gate)
    y = lax.conv_general_dilated(u, w[:, None, :], window_strides=(1,), padding=[(CONV_KERNEL - 1, 0)],
                                 dimension_numbers=('NWC', 'WIO', 'NWC'), feature_group_count=c) + bias
    yg = y.reshape(bsz, s, CONV_GROUPS, c // CONV_GROUPS).astype(jnp.float32)
    mu = jnp.mean(yg, -1, keepdims=True)
    var = jnp.mean(jnp.square(yg - mu), -1, keepdims=True)
    yn = ((yg - mu) * lax.rsqrt(var + EPS)).reshape(bsz, s, c) * ln_g.astype(jnp.float32) + ln_b.astype(jnp.float32)
    return jax.nn.silu(yn).astype(a.dtype)

def second_inputs(seed: int = 0) -> dict:
    key = jax.random.key(seed)
    ks = jax.random.split(key, 20)
    f32 = jnp.float32

    def w(k, shape, fan_in):
        return jax.random.normal(k, shape, f32) * (fan_in ** -0.5)

    def gain(k, shape):
        return 1.0 + 0.02 * jax.random.normal(k, shape, f32)

    return {
        "x": jax.random.normal(ks[0], (BATCH, SEQ, D_MODEL), f32),
        "positions": jnp.broadcast_to(jnp.arange(SEQ, dtype=jnp.int32), (BATCH, SEQ)),
        "ffn1_norm": gain(ks[1], (DEPTH, D_MODEL)),
        "ffn1_wg": w(ks[2], (DEPTH, D_MODEL, D_FF), D_MODEL),
        "ffn1_wu": w(ks[3], (DEPTH, D_MODEL, D_FF), D_MODEL),
        "ffn1_wd": w(ks[4], (DEPTH, D_FF, D_MODEL), D_FF),
        "mix_norm": gain(ks[5], (DEPTH, D_MODEL)),
        "w_in": w(ks[6], (DEPTH, D_MODEL, IN_WIDTH), D_MODEL),
        "conv_w": w(ks[7], (DEPTH, CONV_KERNEL, CONV_WIDTH), CONV_KERNEL),
        "conv_b": 0.02 * jax.random.normal(ks[8], (DEPTH, CONV_WIDTH), f32),
        "conv_ln_g": gain(ks[9], (DEPTH, CONV_WIDTH)),
        "conv_ln_b": 0.02 * jax.random.normal(ks[10], (DEPTH, CONV_WIDTH), f32),
        "w_out": w(ks[11], (DEPTH, MIX_WIDTH, D_MODEL), MIX_WIDTH),
        "ffn2_norm": gain(ks[12], (DEPTH, D_MODEL)),
        "ffn2_wg": w(ks[13], (DEPTH, D_MODEL, D_FF), D_MODEL),
        "ffn2_wu": w(ks[14], (DEPTH, D_MODEL, D_FF), D_MODEL),
        "ffn2_wd": w(ks[15], (DEPTH, D_FF, D_MODEL), D_FF),
        "final_norm": gain(ks[16], (D_MODEL,)),
    }

def second_block(x, positions, ffn1_norm, ffn1_wg, ffn1_wu, ffn1_wd, mix_norm, w_in, conv_w, conv_b,
              conv_ln_g, conv_ln_b, w_out, ffn2_norm, ffn2_wg, ffn2_wu, ffn2_wd, final_norm):
    s = x.shape[1]
    s_pad = ((s + PAD_MULT - 1) // PAD_MULT) * PAD_MULT
    pad = s_pad - s
    pos = jnp.pad(positions, ((0, 0), (0, pad)))
    half_ret = HEAD_DIM // 2
    ret_inv = RET_ROT_BASE ** (-jnp.linspace(0.0, 1.0, half_ret, dtype=jnp.float32))
    half_rope = ROPE_DIMS // 2
    rope_inv = ROPE_THETA_2 ** (-jnp.arange(half_rope, dtype=jnp.float32) / half_rope)
    sizes = [RET_WIDTH] * 4 + [MOBA_WIDTH] * 3 + [CONV_WIDTH] * 2
    cuts = [int(c) for c in np.cumsum(sizes)[:-1]]

    for l in range(DEPTH):
        h = rms_norm_2(x, ffn1_norm[l])
        x = x + FFN_RES_WEIGHT * swiglu(h, ffn1_wg[l], ffn1_wu[l], ffn1_wd[l])

        h = rms_norm_2(x, mix_norm[l])
        z = jnp.pad(h @ w_in[l], ((0, 0), (0, pad), (0, 0)))
        rq, rk, rv, rg, mq, mk, mv, ca, cg = jnp.split(z, cuts, axis=-1)

        rq = rotary(to_heads(rq, RET_HEADS), pos, ret_inv)
        rk = rotary(to_heads(rk, RET_HEADS), pos, ret_inv)
        y_ret = retention(rq, rk, to_heads(rv, RET_HEADS)).astype(jnp.float32)
        y_ret = y_ret * lax.rsqrt(jnp.mean(y_ret * y_ret, -1, keepdims=True) + EPS)
        y_ret = jax.nn.silu(rg) * from_heads(y_ret).astype(rg.dtype)

        mq = rotary(to_heads(mq, MOBA_HEADS), pos, rope_inv)
        mk = rotary(to_heads(mk, MOBA_HEADS), pos, rope_inv)
        y_moba = from_heads(moba_attention(mq, mk, to_heads(mv, MOBA_HEADS)))

        y_conv = conv_module(ca, cg, conv_w[l], conv_b[l], conv_ln_g[l], conv_ln_b[l])

        mix = jnp.concatenate([y_ret, y_moba, y_conv], axis=-1)[:, :s]
        x = x + mix @ w_out[l]

        h = rms_norm_2(x, ffn2_norm[l])
        x = x + FFN_RES_WEIGHT * swiglu(h, ffn2_wg[l], ffn2_wu[l], ffn2_wd[l])

    return rms_norm_2(x, final_norm)


def setup_inputs(seed=0):
    out = dict(first_inputs(seed))
    for name, value in second_inputs(seed + 1).items():
        if name != "x":
            out[name + "_2"] = value
    return out


def reference(
    x, p, w_in_even, mla_q_norm, w_uq, mla_kv_norm, w_ukv, gla_gate_w_fwd, gla_gate_b_fwd,
    gla_gate_w_bwd, gla_gate_b_bwd, gla_norm, w_in_odd, gqa_q_norm, gqa_k_norm, w_o, ln1_g,
    ln1_b, router_w, w1, w3, w2, ple_gate_w, ple_gate_b, ple_w, ln2_g, ln2_b, positions_2,
    ffn1_norm_2, ffn1_wg_2, ffn1_wu_2, ffn1_wd_2, mix_norm_2, w_in_2, conv_w_2, conv_b_2,
    conv_ln_g_2, conv_ln_b_2, w_out_2, ffn2_norm_2, ffn2_wg_2, ffn2_wu_2, ffn2_wd_2,
    final_norm_2,
):
    x = first_block(
        x, p, w_in_even, mla_q_norm, w_uq, mla_kv_norm, w_ukv, gla_gate_w_fwd, gla_gate_b_fwd,
        gla_gate_w_bwd, gla_gate_b_bwd, gla_norm, w_in_odd, gqa_q_norm, gqa_k_norm, w_o, ln1_g,
        ln1_b, router_w, w1, w3, w2, ple_gate_w, ple_gate_b, ple_w, ln2_g, ln2_b,
    )
    return second_block(
        x, positions_2, ffn1_norm_2, ffn1_wg_2, ffn1_wu_2, ffn1_wd_2, mix_norm_2, w_in_2,
        conv_w_2, conv_b_2, conv_ln_g_2, conv_ln_b_2, w_out_2, ffn2_norm_2, ffn2_wg_2,
        ffn2_wu_2, ffn2_wd_2, final_norm_2,
    )


_drawn_inputs = setup_inputs


def setup_inputs(seed=0):
    import zlib

    import numpy as np

    out = dict(_drawn_inputs(seed))
    spreads = {}
    factors = {'mla_q_norm': 8.0,
     'mla_kv_norm': 8.0,
     'gla_gate_w_fwd': 3.378,
     'gla_gate_b_fwd': 6.922,
     'gla_gate_w_bwd': 3.218,
     'gla_gate_b_bwd': 6.989,
     'gla_norm': 8.0,
     'gqa_q_norm': 8.0,
     'gqa_k_norm': 8.0,
     'ple_gate_b': 8.0,
     'ffn1_norm_2': 3.975,
     'conv_b_2': 2.946,
     'conv_ln_g_2': 28.35,
     'conv_ln_b_2': 26.001,
     'ffn2_norm_2': 5.069,
     'final_norm_2': 7.46,
     'mix_norm_2': 3.729}
    for name, (base, spread) in spreads.items():
        noise = np.random.default_rng([zlib.crc32(name.encode()), seed]).standard_normal(out[name].shape)
        drawn = base * np.exp(spread * noise) if base else spread * noise
        out[name] = __import__('jax').numpy.asarray(drawn.astype(out[name].dtype))
    for name, factor in factors.items():
        out[name] = (out[name] * factor).astype(out[name].dtype)
    return out
```

```python
import concourse.bass as bass
import concourse.mybir as mybir
import numpy as np
from concourse.alu_op_type import AluOpType as ALU

F32 = mybir.dt.float32
BF16 = mybir.dt.bfloat16
I32 = mybir.dt.int32
ACT = mybir.ActivationFunctionType
AX = mybir.AxisListType.X

P = 128
SEQ = 256
TILES = SEQ // P
D = 1024
DC = D // P
DEPTH = 2
EPS = 1e-6
ALPHA = (2.0 * DEPTH) ** 0.25
BANK = 512

Q_LORA, KV_LORA, ROPE_A = 256, 128, 32
MLA_HEADS, NOPE, V_DIM = 8, 64, 64
MLA_QK = NOPE + ROPE_A
GLA_HEADS, DK, DV, RANK, CHUNK = 4, 64, 128, 16, 64
N_CHUNKS = SEQ // CHUNK
GATE_NORM = 16.0
O_CQ = 0
O_CKV = O_CQ + Q_LORA
O_KPE = O_CKV + KV_LORA
O_GQ = O_KPE + ROPE_A
O_GK = O_GQ + GLA_HEADS * DK
O_GV = O_GK + GLA_HEADS * DK
O_LR = O_GV + GLA_HEADS * DV
O_GR = O_LR + 2 * RANK
EVEN_IN = O_GR + GLA_HEADS * DV
GQA_HEADS, KV_HEADS, HD = 16, 4, 64
ODD_IN = (GQA_HEADS + 2 * KV_HEADS) * HD
EXPERTS, FF, PLE_DIM = 16, 1024, 256
CAP = 2 * SEQ // EXPERTS
QUADS = 4
QW = FF // QUADS
RET_HEADS, MOBA_HEADS, CONV_W, KERNEL = 6, 6, 256, 31
RW, MW = RET_HEADS * HD, MOBA_HEADS * HD
IN_2 = 4 * RW + 3 * MW + 2 * CONV_W
D_FF = 2816
FG = 256
F_GROUPS = D_FF // FG
ROT_RET, ROT_MOBA = HD // 2, HD // 8

WEIGHT_SLOTS, SLOT = 6, 4096


def axial_tables(rot_dim):
    row = np.repeat(np.arange(SEQ // 64, dtype=np.float32), 64)
    col = np.tile(np.arange(64, dtype=np.float32), SEQ // 64)
    half = rot_dim // 2
    inv = (np.float32(10000.0) ** (-np.arange(0, half, 2, dtype=np.float32) / half)).astype(np.float32)
    ang = np.concatenate([row[:, None] * inv, col[:, None] * inv], axis=-1)
    return np.stack([np.cos(ang), np.sin(ang)], axis=1).astype(np.float32)


def shape_constants():
    m, l = np.arange(P)[:, None], np.arange(P)[None, :]
    same = (m // CHUNK) == (l // CHUNK)
    tri = np.stack([same & (m <= l), same & (m >= l), same & (m > l), same & (m < l)], axis=1)
    heads = np.arange(RET_HEADS, dtype=np.float32)
    log_gamma = np.log1p(-np.exp2(-5.0 - heads)).astype(np.float32)
    km, qc = np.arange(SEQ)[:, None], np.arange(SEQ)[None, :]
    rel = (qc - km).astype(np.float32)
    decay = np.where(rel >= 0, np.exp(log_gamma[:, None, None] * np.maximum(rel, 0.0)), 0.0) * HD ** -0.5
    ret_inv = np.float32(10000.0) ** (-np.linspace(0.0, 1.0, ROT_RET, dtype=np.float32))
    moba_inv = np.float32(500000.0) ** (-np.arange(ROT_MOBA, dtype=np.float32) / ROT_MOBA)
    f = np.float32
    return {
        "c_ident": np.eye(P, dtype=f),
        "c_chunk_masks": tri.astype(f),
        "c_rope_mla": axial_tables(ROPE_A),
        "c_rope_gqa": axial_tables(HD),
        "c_slots": np.arange(1, CAP + 1, dtype=f)[None, :],
        "c_causal": np.where(l <= m, 0.0, -1e30).astype(f),
        "c_decay": decay.astype(f).reshape(RET_HEADS, TILES, P, SEQ),
        "c_inv_freq": np.concatenate([ret_inv, moba_inv]).astype(f)[None, :],
        "c_group_mean": (((m // HD) == (l // HD)) / HD).astype(f),
    }


class Signal:

    def __init__(self, nc, name):
        self.sem = nc.alloc_semaphore(name)
        self.base = 0

    def at(self, n):
        return self.base + n

    def advance(self, n):
        self.base += n


class Chain:

    def __init__(self, nc, name):
        self.sem = nc.alloc_semaphore(name)
        self.steps = 0

    def link(self, engine, instruction):
        self.steps += 1
        instruction.then_inc(self.sem, 1)
        engine.wait_ge(self.sem, self.steps)


class WeightStream:

    def __init__(self, nc, ring):
        self.ring = ring
        self.arrived = [nc.alloc_semaphore(f"weights_arrived_{s}") for s in range(WEIGHT_SLOTS)]
        self.used = nc.alloc_semaphore("weights_used")
        self.units, self.value = [], []
        self.total = [0] * WEIGHT_SLOTS
        self.issued = self.taken = 0

    def add(self, loads, index, n_loads=1):
        slot = len(self.units) % WEIGHT_SLOTS
        self.total[slot] += 16 * n_loads
        self.units.append((loads, index))
        self.value.append(self.total[slot])

    def take(self, n):
        self.taken += n
        return self.taken - n

    def slot(self, u):
        return self.ring[:, u % WEIGHT_SLOTS, :]

    def load(self, sp, u, index):
        for dst, src in self.units[u][0](self.slot(u), index):
            sp.dma_start(dst, src).then_inc(self.arrived[u % WEIGHT_SLOTS], 16)

    def issue(self, sp):
        for u in range(self.issued, min(self.taken + WEIGHT_SLOTS, len(self.units))):
            if u >= WEIGHT_SLOTS:
                sp.wait_ge(self.used, u - WEIGHT_SLOTS + 1)
            self.load(sp, u, self.units[u][1])
            self.issued = u + 1

    def wait(self, pe, u):
        pe.wait_ge(self.arrived[u % WEIGHT_SLOTS], self.value[u])


def columns_of(w, n0, width):
    return w[:, n0:n0 + width].rearrange("(c p) n -> p c n", p=P)


def plan_weights(nc, stream, t):

    def matrix(w, n):
        for n0 in range(0, n, BANK):
            width = min(BANK, n - n0)

            def loads(slot, n0, width=width, w=w):
                rows = w.shape[0] // P
                dst = slot[:, 0:rows * width].rearrange("p (c n) -> p c n", c=rows)
                return [(dst, columns_of(w, n0, width))]

            stream.add(loads, n0)

    def up_projections(slot, _):
        uq = slot[:, 0:2 * MLA_HEADS * MLA_QK].rearrange("p (c n) -> p c n", c=2)
        ukv = slot[:, 2 * MLA_HEADS * MLA_QK:2 * MLA_HEADS * MLA_QK + D]
        return [(uq, t["w_uq"][0].rearrange("(c p) n -> p c n", p=P)), (ukv, t["w_ukv"][0])]

    def ple_projection(slot, layer):
        return [(slot[:, 0:2 * D].rearrange("p (c n) -> p c n", c=2),
                 t["ple_w"][layer].rearrange("(c p) n -> p c n", p=P))]

    def experts(layer):
        def half(name, which, by_rows):
            def loads(slot, e):
                w = t[name][layer, bass.ds(e, 1)].rearrange("e (c p) f -> p (e c) f", p=P)
                if by_rows:
                    c0 = which * DC // 2
                    return [(slot.rearrange("p (c f) -> p c f", c=DC // 2), w[:, c0:c0 + DC // 2, :])]
                return [(slot.rearrange("p (c f) -> p c f", c=DC), w[:, :, which * BANK:(which + 1) * BANK])]
            return loads

        parts = [half("w1", 0, True), half("w1", 1, True), half("w3", 0, True), half("w3", 1, True),
                 half("w2", 0, False), half("w2", 1, False)]
        for e in range(EXPERTS):
            for part in parts:
                stream.add(part, e)

    def ffn(which, layer):
        wg, wu, wd = (t[f"ffn{which}_{k}_2"] for k in ("wg", "wu", "wd"))

        def up(slot, f0):
            halves = slot.rearrange("p (h c f) -> p h c f", h=2, c=DC)
            return [(halves[:, h], w[layer, :, bass.ds(f0, FG)].rearrange("(c p) f -> p c f", p=P))
                    for h, w in enumerate((wg, wu))]

        def down(slot, f0):
            return [(slot[:, 0:2 * D].rearrange("p (c n) -> p c n", c=2),
                     wd[layer, bass.ds(f0, FG), :].rearrange("(c p) n -> p c n", p=P))]

        stream.add(up, 0, 2)
        for i in range(1, F_GROUPS):
            stream.add(up, i * FG, 2)
            stream.add(down, (i - 1) * FG)
        stream.add(down, (F_GROUPS - 1) * FG)

    for layer in range(DEPTH):
        if layer % 2 == 0:
            matrix(t["w_in_even"][0], EVEN_IN)
            stream.add(up_projections, 0, 2)
        else:
            matrix(t["w_in_odd"][0], ODD_IN)
        matrix(t["w_o"][layer], D)
        matrix(t["ple_gate_w"][layer], D)
        stream.add(ple_projection, layer)
        experts(layer)
    for layer in range(DEPTH):
        ffn(1, layer)
        matrix(t["w_in_2"][layer], IN_2)
        matrix(t["w_out_2"][layer], D)
        ffn(2, layer)


def build_program(nc, t, out):
    def sb(name, *dims, dtype=F32):
        return nc.alloc_sbuf_tensor(name, [P, *dims], dtype)

    ring = sb("weight_ring", WEIGHT_SLOTS, SLOT)
    x = sb("x", TILES, D)
    x_cols = sb("x_cols", DC, SEQ)
    mix_cols = sb("mix_cols", DC, SEQ)
    ln_params = sb("ln_params", 2, D)
    ident = sb("ident", P)
    chunk_masks = sb("chunk_masks", 4, P)
    rope_mla = sb("rope_mla", TILES, 2, ROPE_A // 2)
    rope_gqa = sb("rope_gqa", TILES, 2, HD // 2)
    causal = sb("causal", P)
    group_mean = sb("group_mean", P)
    ones_row = sb("ones_row", P)
    zeros_bf = sb("zeros_bf", BANK, dtype=BF16)
    half_power = sb("half_power", 64)
    norm_cols = sb("norm_cols", DC)
    stat = sb("stat", 256)
    arena_size = 18300
    arena = sb("arena", arena_size)
    ps = nc.alloc_psum_tensor("psum", [P, 8, BANK], F32)

    signals = {}

    def signal(name):
        if name not in signals:
            signals[name] = Signal(nc, name)
        return signals[name]

    dve_chain, act_chain, pool_chain = (Chain(nc, n) for n in ("dve_chain", "act_chain", "pool_chain"))
    stream = WeightStream(nc, ring)
    plan_weights(nc, stream, t)
    params = signal("params_loaded")
    params_count = [0]

    class Arena:

        def __init__(self, at=0):
            self.at = at

        def take(self, *dims):
            n = int(np.prod(dims))
            assert self.at + n <= arena_size, (self.at, n)
            flat = arena[:, self.at:self.at + n]
            self.at += n
            if len(dims) == 1:
                return flat
            names = "abcd"[:len(dims)]
            spec = f"p ({' '.join(names)}) -> p {' '.join(names)}"
            return flat.rearrange(spec, **dict(zip(names[1:], dims[1:])))

    def load_params(sp, *pairs):
        for dst, src in pairs:
            sp.dma_start(dst, src, allow_slow_non_contiguous=True).then_inc(params.sem, 16)
            params_count[0] += 16

    def params_ready(engine):
        engine.wait_ge(params.sem, params_count[0])

    def spread(row):
        return row.partition_broadcast(P) if len(row.shape) == 1 else row.broadcast_to([P, row.shape[-1]])

    with nc.Block() as block:
        @block.sync
        def _(sp):
            load_params(
                sp,
                (x[:, :, :], t["x"][0].rearrange("(a p) d -> p a d", p=P)),
                (ident[:, :], t["c_ident"]),
                (chunk_masks[:, :, :], t["c_chunk_masks"]),
                (rope_mla[:, :, :, :], t["c_rope_mla"].rearrange("(a p) k f -> p a k f", p=P)),
                (rope_gqa[:, :, :, :], t["c_rope_gqa"].rearrange("(a p) k f -> p a k f", p=P)),
                (causal[:, :], t["c_causal"]),
                (group_mean[:, :], t["c_group_mean"]),
            )
            stream.issue(sp)

        @block.gpsimd
        def _(pool):
            pool.memset(ones_row[:, :], 1.0)
            pool.memset(zeros_bf[:, :], 0.0)
            pool.memset(half_power[:, :], -0.5)

    def to_columns(src, dst, n, gain=None, more_params=()):
        turned, taken = signal("columns_turned"), signal("columns_taken")
        with nc.Block() as block:
            @block.sync
            def _(sp):
                stream.issue(sp)
                load_params(sp, *more_params)

            @block.tensor
            def _(pe):
                params_ready(pe)
                for c in range(n):
                    for a in range(TILES):
                        last = pe.transpose(ps[:, c // 2, (c % 2) * SEQ + a * P:(c % 2) * SEQ + (a + 1) * P],
                                            src[:, a, c * P:(c + 1) * P], ident[:, :])
                    if c % 2:
                        last.then_inc(turned.sem, 1)

            @block.scalar
            def _(act):
                params_ready(act)
                for b in range(0, n // 2, 2):
                    act.wait_ge(turned.sem, turned.at(b + 1))
                    if gain is None:
                        act.copy(dst[:, 2 * b:2 * b + 2, :], ps[:, b, :].rearrange("p (c q) -> p c q", c=2))
                    else:
                        for c in (2 * b, 2 * b + 1):
                            act.activation(dst[:, c, :], ps[:, b, c % 2 * SEQ:c % 2 * SEQ + SEQ], ACT.Copy,
                                           scale=gain[:, c:c + 1])

            @block.vector
            def _(dve):
                params_ready(dve)
                for b in range(1, n // 2, 2):
                    dve.wait_ge(turned.sem, turned.at(b + 1))
                    if gain is None:
                        dve.tensor_copy(dst[:, 2 * b:2 * b + 2, :], ps[:, b, :].rearrange("p (c q) -> p c q", c=2))
                    else:
                        for c in (2 * b, 2 * b + 1):
                            dve.tensor_scalar(dst[:, c, :], ps[:, b, c % 2 * SEQ:c % 2 * SEQ + SEQ],
                                              gain[:, c:c + 1], None, ALU.mult)
        turned.advance(n // 2)

    def project_products(pe, first, n, ready, freed):
        k = 0
        for i, n0 in enumerate(range(0, n, BANK)):
            width = min(BANK, n - n0)
            w = stream.slot(first + i)[:, 0:DC * width].rearrange("p (c n) -> p c n", c=DC)
            stream.wait(pe, first + i)
            for a in range(TILES):
                if k >= 8:
                    pe.wait_ge(freed.sem, freed.at(k - 7))
                for c in range(DC):
                    last = pe.matmul(ps[:, k % 8, 0:width], x_cols[:, c, a * P:(a + 1) * P], w[:, c, :],
                                     start=c == 0, stop=c == DC - 1)
                last.then_inc(ready.sem if a == 0 else stream.used, 1)
                k += 1

    def project(n, dst):
        units = -(-n // BANK)
        first = stream.take(units)
        ready, freed = signal("projected"), signal("projection_kept")
        with nc.Block() as block:
            @block.sync
            def _(sp):
                stream.issue(sp)

            @block.tensor
            def _(pe):
                project_products(pe, first, n, ready, freed)

            @block.scalar
            def _(act):
                k = 0
                for i, n0 in enumerate(range(0, n, BANK)):
                    width = min(BANK, n - n0)
                    for a in range(TILES):
                        if a == 0:
                            act.wait_ge(ready.sem, ready.at(i + 1))
                        else:
                            act.wait_ge(stream.used, first + i + 1)
                        act.copy(dst[:, a, n0:n0 + width], ps[:, k % 8, 0:width]).then_inc(freed.sem, 1)
                        k += 1
        ready.advance(units)
        freed.advance(units * TILES)

    def inverse_root(pool, dst, sums, count):
        n = dst.shape[-1]
        pool_chain.link(pool, pool.tensor_scalar(dst, sums, 1.0 / count, EPS, ALU.mult, ALU.add))
        return pool.tensor_tensor(dst, dst, half_power[:, 0:n], ALU.pow)

    def rotate(engine, first, second, cos, sin, scratch, chain=dve_chain):
        fs, sc, fc, ss = scratch
        engine.tensor_tensor(fc, first, cos, ALU.mult)
        engine.tensor_tensor(ss, second, sin, ALU.mult)
        engine.tensor_tensor(fs, first, sin, ALU.mult)
        chain.link(engine, engine.tensor_tensor(sc, second, cos, ALU.mult))
        engine.tensor_tensor(first, fc, ss, ALU.subtract)
        return engine.tensor_tensor(second, fs, sc, ALU.add)

    def layer_norm_steps(dve, y, stats, root_wanted, root_ready):
        for a in range(TILES):
            for h in range(2):
                last = dve.bn_stats(stats[:, a, 6 * h:6 * h + 6], y[:, a, h * BANK:(h + 1) * BANK])
        dve_chain.link(dve, last)
        for a in range(TILES):
            last = dve.bn_aggr(stats[:, a, 12:14], stats[:, a, 0:12])
        last.then_inc(root_wanted.sem, 1)
        dve.wait_ge(root_ready.sem, root_ready.at(1))
        dve.wait_ge(root_wanted.sem, root_wanted.at(1))
        for a in range(TILES):
            dve_chain.link(dve, dve.tensor_scalar(y[:, a, :], y[:, a, :], stats[:, a, 12:13], stats[:, a, 14:15],
                                                  ALU.subtract, ALU.mult))
            dve_chain.link(dve, dve.tensor_tensor(y[:, a, :], y[:, a, :], ln_params[:, 0, :], ALU.mult))
            dve.tensor_tensor(x[:, a, :], y[:, a, :], ln_params[:, 1, :], ALU.add)

    def layer_norm_root(pool, stats, root_wanted, root_ready):
        pool.wait_ge(root_wanted.sem, root_wanted.at(1))
        for a in range(TILES):
            pool_chain.link(pool, pool.tensor_scalar(stats[:, a, 14:15], stats[:, a, 13:14], 1.0, EPS,
                                                     ALU.mult, ALU.add))
            last = pool.tensor_tensor(stats[:, a, 14:15], stats[:, a, 14:15], half_power[:, 0:1], ALU.pow)
        last.then_inc(root_ready.sem, 1)

    def output_products(pe, first, ready):
        for h in range(2):
            w = stream.slot(first + h).rearrange("p (c n) -> p c n", c=DC)
            stream.wait(pe, first + h)
            for a in range(TILES):
                for c in range(DC):
                    last = pe.matmul(ps[:, 2 * h + a, :], mix_cols[:, c, a * P:(a + 1) * P], w[:, c, :],
                                     start=c == 0, stop=c == DC - 1)
                last.then_inc(ready.sem if a == 0 else stream.used, 1)

    def output_ready(engine, first, ready, h, a):
        if a == 0:
            engine.wait_ge(ready.sem, ready.at(h + 1))
        else:
            engine.wait_ge(stream.used, first + h + 1)

    def mix_out_norm():
        first = stream.take(2)
        ready, wanted, got = signal("projected"), signal("root_wanted"), signal("root_ready")
        y = Arena().take(TILES, D)
        stats = stat[:, 0:32].rearrange("p (a k) -> p a k", a=TILES)
        with nc.Block() as block:
            @block.sync
            def _(sp):
                stream.issue(sp)

            @block.tensor
            def _(pe):
                output_products(pe, first, ready)

            @block.vector
            def _(dve):
                params_ready(dve)
                for h in range(2):
                    for a in range(TILES):
                        output_ready(dve, first, ready, h, a)
                        cols = slice(h * BANK, (h + 1) * BANK)
                        last = dve.scalar_tensor_tensor(out=y[:, a, cols], in0=x[:, a, cols], scalar=ALPHA,
                                                        in1=ps[:, 2 * h + a, :], op0=ALU.mult, op1=ALU.add)
                dve_chain.link(dve, last)
                layer_norm_steps(dve, y, stats, wanted, got)

            @block.gpsimd
            def _(pool):
                layer_norm_root(pool, stats, wanted, got)
        ready.advance(2)
        wanted.advance(1)
        got.advance(1)

    def attention(heads, q_of, k_of, v_of, mix_head, scale, masked, mem, stages=None):
        scores, norm, turned, kept, summed, stored = (signal(s) for s in (
            "scores_ready", "probs_ready", "probs_turned", "turned_kept", "values_summed", "values_kept"))
        peak, expd = signal("peaks_ready"), signal("exps_ready")
        e_buf = mem.take(2, TILES, SEQ)
        pt_buf = mem.take(2, TILES, SEQ)
        small = mem.take(2, TILES, 4)
        s_buf = mem.take(2, TILES, SEQ) if masked else None

        def keys(a):
            return (a + 1) * P if masked else SEQ

        with nc.Block() as block:
            @block.sync
            def _(sp):
                stream.issue(sp)

            @block.tensor
            def _(pe):
                def score(h):
                    if h >= 2:
                        pe.wait_ge(expd.sem, expd.at(TILES * (h - 1)))
                    for a in range(TILES):
                        last = pe.matmul(ps[:, h % 2, a * SEQ:a * SEQ + keys(a)], q_of(h)[:, a * P:(a + 1) * P],
                                         k_of(h)[:, 0:keys(a)], start=True, stop=True)
                    last.then_inc(scores.sem, 1)

                def turn(h):
                    pe.wait_ge(norm.sem, norm.at(h + 1))
                    if h >= 2:
                        pe.wait_ge(kept.sem, kept.at(h - 1))
                    for b in range(TILES):
                        for a in range(b if masked else 0, TILES):
                            last = pe.transpose(ps[:, 2 + h % 2, b * SEQ + a * P:b * SEQ + (a + 1) * P],
                                                e_buf[:, h % 2, a, b * P:(b + 1) * P], ident[:, :])
                    last.then_inc(turned.sem, 1)

                def sum_values(h):
                    pe.wait_ge(kept.sem, kept.at(h + 1))
                    if h >= 4:
                        pe.wait_ge(stored.sem, stored.at(h // 2 - 1))
                    half = slice((h % 2) * HD, (h % 2) * HD + HD)
                    for b in range(TILES):
                        lo = b * P if masked else 0
                        last = pe.matmul(ps[half, 4 + (h // 2) % 2 * 2 + h % 2, lo:SEQ], v_of(h, b),
                                         pt_buf[:, h % 2, b, lo:SEQ], start=b == 0, stop=b == TILES - 1)
                    last.then_inc(summed.sem, 1)

                for i in range(heads + 2):
                    if i < heads:
                        score(i)
                    if 1 <= i <= heads:
                        turn(i - 1)
                    if i >= 2:
                        sum_values(i - 2)

            @block.vector
            def _(dve):
                def peaks(h):
                    dve.wait_ge(scores.sem, scores.at(h + 1))
                    src = ps[:, h % 2, :].rearrange("p (a k) -> p a k", a=TILES)
                    if masked:
                        dve.tensor_copy(s_buf[:, h % 2, 1, 0:P], src[:, 1, 0:P])
                        for a in range(TILES):
                            last = dve.tensor_tensor(s_buf[:, h % 2, a, a * P:(a + 1) * P],
                                                     src[:, a, a * P:(a + 1) * P], causal[:, :], ALU.add)
                        dve_chain.link(dve, last)
                        for a in range(TILES):
                            last = dve.tensor_reduce(small[:, h % 2, a, 0:1], s_buf[:, h % 2, a, 0:keys(a)], AX,
                                                     ALU.max)
                    else:
                        last = dve.tensor_reduce(small[:, h % 2, :, 0:1], src, AX, ALU.max)
                    dve_chain.link(dve, last)
                    dve.tensor_scalar(small[:, h % 2, :, 1:2], small[:, h % 2, :, 0:1], -scale, None,
                                      ALU.mult).then_inc(peak.sem, 1)

                def normalise(h):
                    dve.wait_ge(expd.sem, expd.at(TILES * (h + 1)))
                    dve_chain.link(dve, dve.reciprocal(small[:, h % 2, :, 3:4], small[:, h % 2, :, 2:3]))
                    for a in range(TILES):
                        last = dve.tensor_scalar(e_buf[:, h % 2, a, 0:keys(a)], e_buf[:, h % 2, a, 0:keys(a)],
                                                 small[:, h % 2, a, 3:4], None, ALU.mult)
                    last.then_inc(norm.sem, 1)

                for i in range(heads + 1):
                    if i < heads:
                        peaks(i)
                    if i >= 1:
                        normalise(i - 1)

            @block.scalar
            def _(act):
                def exps(h):
                    act.wait_ge(peak.sem, peak.at(h + 1))
                    if h >= 2:
                        act.wait_ge(turned.sem, turned.at(h - 1))
                    for a in range(TILES):
                        src = s_buf[:, h % 2, a, 0:keys(a)] if masked else ps[:, h % 2, a * SEQ:(a + 1) * SEQ]
                        act.activation(e_buf[:, h % 2, a, 0:keys(a)], src, ACT.Exp,
                                       bias=small[:, h % 2, a, 1:2], scale=scale,
                                       accum_out=small[:, h % 2, a, 2:3]).then_inc(expd.sem, 1)

                def keep(h):
                    act.wait_ge(turned.sem, turned.at(h + 1))
                    if h >= 2:
                        act.wait_ge(summed.sem, summed.at(h - 1))
                    if masked:
                        act.copy(pt_buf[:, h % 2, 0, :], ps[:, 2 + h % 2, 0:SEQ])
                        last = act.copy(pt_buf[:, h % 2, 1, P:SEQ], ps[:, 2 + h % 2, SEQ + P:2 * SEQ])
                    else:
                        last = act.copy(pt_buf[:, h % 2, :, :],
                                        ps[:, 2 + h % 2, :].rearrange("p (b q) -> p b q", b=TILES))
                    last.then_inc(kept.sem, 1)

                def store(h):
                    act.wait_ge(summed.sem, summed.at(h + 1))
                    for hh in range(2):
                        half = slice(hh * HD, hh * HD + HD)
                        last = act.copy(mix_cols[half, (mix_head + h) // 2, :],
                                        ps[half, 4 + (h // 2) % 2 * 2 + hh, 0:SEQ])
                    last.then_inc(stored.sem, 1)

                for i in range(heads + 3):
                    if i < heads:
                        exps(i)
                    if 1 <= i <= heads:
                        keep(i - 1)
                    if i >= 3 and (i - 3) % 2 == 1:
                        store(i - 3)
        for s in (scores, norm, turned, kept, summed, peak):
            s.advance(heads)
        expd.advance(TILES * heads)
        stored.advance(heads // 2)

    def even_mixer():
        mem = Arena()
        h = mem.take(TILES, EVEN_IN)
        load = [(norm_cols[:, 0:2], t["mla_q_norm"][0].rearrange("(c p) -> p c", p=P)),
                (norm_cols[:, 2:3], t["mla_kv_norm"][0].rearrange("(c p) -> p c", p=P)),
                (ln_params[:, 0, :], spread(t["ln1_g"][0])), (ln_params[:, 1, :], spread(t["ln1_b"][0]))]
        to_columns(x, x_cols, DC, more_params=load)
        project(EVEN_IN, h)
        base = mem.at

        q = mem.take(TILES, MLA_HEADS, MLA_QK)
        kv = mem.take(TILES, MLA_HEADS, NOPE + V_DIM)
        k = mem.take(TILES, MLA_HEADS, MLA_QK)
        q_cols = mem.take(MLA_HEADS, SEQ)
        k_cols = mem.take(MLA_HEADS, SEQ)
        mem_att = mem.at
        latent = mem.take(TILES, Q_LORA + KV_LORA)
        latent_cols = mem.take(3, SEQ)
        scratch = mem.take(4, TILES * MLA_HEADS * ROPE_A // 2)
        sums = stat[:, 0:4]
        roots = stat[:, 4:8]
        unit = stream.take(1)
        squared, rooted, scaled, turned, taken, ready, kept, k_made, qk_made, freed = (signal(s) for s in (
            "squares_summed", "root_ready", "latents_scaled", "columns_turned", "latents_turned", "up_projected",
            "up_kept", "k_heads_ready", "qk_heads_ready", "head_columns_kept"))
        with nc.Block() as block:
            @block.sync
            def _(sp):
                stream.issue(sp)

            @block.scalar
            def _(act):
                for a in range(TILES):
                    act.activation(latent[:, a, 0:Q_LORA], h[:, a, O_CQ:O_CQ + Q_LORA], ACT.Square,
                                   accum_out=sums[:, a:a + 1])
                    last = act.activation(latent[:, a, Q_LORA:], h[:, a, O_CKV:O_CKV + KV_LORA], ACT.Square,
                                          accum_out=sums[:, 2 + a:3 + a])
                last.then_inc(squared.sem, 1)
                act.wait_ge(rooted.sem, rooted.at(1))
                act.wait_ge(squared.sem, squared.at(1))
                for a in range(TILES):
                    act.activation(latent[:, a, 0:Q_LORA], h[:, a, O_CQ:O_CQ + Q_LORA], ACT.Copy,
                                   scale=roots[:, a:a + 1])
                    last = act.activation(latent[:, a, Q_LORA:], h[:, a, O_CKV:O_CKV + KV_LORA], ACT.Copy,
                                          scale=roots[:, 2 + a:3 + a])
                last.then_inc(scaled.sem, 1)
                params_ready(act)
                for c in range(3):
                    act.wait_ge(turned.sem, turned.at(c + 1))
                    last = act.activation(latent_cols[:, c, :], ps[:, c, 0:SEQ], ACT.Copy,
                                          scale=norm_cols[:, c:c + 1])
                last.then_inc(taken.sem, 1)
                for a in range(TILES):
                    if a == 0:
                        act.wait_ge(ready.sem, ready.at(1))
                    else:
                        act.wait_ge(stream.used, unit + 1)
                    width = MLA_HEADS * MLA_QK // 2
                    for i in range(2):
                        act.copy(q[:, a, 4 * i:4 * i + 4, :],
                                 ps[:, 4 * a + i, 0:width].rearrange("p (h d) -> p h d", d=MLA_QK))
                    for i in range(2):
                        last = act.copy(kv[:, a, 4 * i:4 * i + 4, :],
                                        ps[:, 4 * a + 2 + i, :].rearrange("p (h d) -> p h d", d=NOPE + V_DIM))
                    last.then_inc(kept.sem, 1)
                for g in range(MLA_HEADS):
                    act.wait_ge(turned.sem, turned.at(3 + g + 1))
                    dst = (q_cols if g < 4 else k_cols)[0:MLA_QK, 2 * (g % 4):2 * (g % 4) + 2, :]
                    act.copy(dst, ps[0:MLA_QK, g, :].rearrange("p (h q) -> p h q", h=2))

            @block.gpsimd
            def _(pool):
                pool.wait_ge(squared.sem, squared.at(1))
                inverse_root(pool, roots[:, 0:2], sums[:, 0:2], Q_LORA)
                inverse_root(pool, roots[:, 2:4], sums[:, 2:4], KV_LORA).then_inc(rooted.sem, 1)

            @block.tensor
            def _(pe):
                pe.wait_ge(scaled.sem, scaled.at(1))
                for c in range(3):
                    for a in range(TILES):
                        last = pe.transpose(ps[:, c, a * P:(a + 1) * P], latent[:, a, c * P:(c + 1) * P],
                                            ident[:, :])
                    last.then_inc(turned.sem, 1)
                pe.wait_ge(taken.sem, taken.at(1))
                stream.wait(pe, unit)
                w = stream.slot(unit)
                uq = w[:, 0:2 * MLA_HEADS * MLA_QK].rearrange("p (c n) -> p c n", c=2)
                ukv = w[:, 2 * MLA_HEADS * MLA_QK:2 * MLA_HEADS * MLA_QK + D]
                width = MLA_HEADS * MLA_QK // 2
                for a in range(TILES):
                    for i in range(2):
                        for c in range(2):
                            pe.matmul(ps[:, 4 * a + i, 0:width], latent_cols[:, c, a * P:(a + 1) * P],
                                      uq[:, c, i * width:(i + 1) * width], start=c == 0, stop=c == 1)
                    for i in range(2):
                        last = pe.matmul(ps[:, 4 * a + 2 + i, :], latent_cols[:, 2, a * P:(a + 1) * P],
                                         ukv[:, i * BANK:(i + 1) * BANK], start=True, stop=True)
                    last.then_inc(ready.sem if a == 0 else stream.used, 1)
                pe.wait_ge(qk_made.sem, qk_made.at(1))
                for g in range(MLA_HEADS):
                    src = q if g < 4 else k
                    for i in range(4):
                        hd, a = 2 * (g % 4) + i // 2, i % 2
                        last = pe.transpose(ps[0:MLA_QK, g, i * P:(i + 1) * P], src[:, a, hd, :], ident[:, :])
                    last.then_inc(turned.sem, 1)

            @block.vector
            def _(dve):
                half = ROPE_A // 2
                kpe = h[:, :, O_KPE:O_KPE + ROPE_A]
                small = [scratch[:, i, 0:TILES * half].rearrange("p (a f) -> p a f", a=TILES) for i in range(4)]
                dve_chain.link(dve, rotate(dve, kpe[:, :, 0:half], kpe[:, :, half:], rope_mla[:, :, 0, :],
                                           rope_mla[:, :, 1, :], small))
                for a in range(TILES):
                    dve.tensor_copy(k[:, a, :, NOPE:], kpe[:, a, :].rearrange("p (u r) -> p u r", u=1)
                                    .broadcast_to([P, MLA_HEADS, ROPE_A]))
                dve.wait_ge(kept.sem, kept.at(TILES))
                for a in range(TILES):
                    dve.tensor_copy(k[:, a, :, 0:NOPE], kv[:, a, :, 0:NOPE])
                for a in range(TILES):
                    wide = [scratch[:, i, 0:MLA_HEADS * half].rearrange("p (h f) -> p h f", h=MLA_HEADS)
                            for i in range(4)]
                    cos, sin = (rope_mla[:, a, i:i + 1, :].broadcast_to([P, MLA_HEADS, half]) for i in range(2))
                    last = rotate(dve, q[:, a, :, NOPE:NOPE + half], q[:, a, :, NOPE + half:], cos, sin, wide)
                    if a == 0:
                        dve_chain.link(dve, last)
                last.then_inc(qk_made.sem, 1)
        squared.advance(1), rooted.advance(1), scaled.advance(1), turned.advance(3 + MLA_HEADS)
        taken.advance(1), ready.advance(1), kept.advance(TILES), qk_made.advance(1)

        attention(MLA_HEADS, lambda i: q_cols[0:MLA_QK, i, :], lambda i: k_cols[0:MLA_QK, i, :],
                  lambda i, b: kv[:, b, i, NOPE:], 0, MLA_QK ** -0.5, False, Arena(mem_att))
        return h, base

    def gla(h, base):
        mem = Arena(base)
        width = GLA_HEADS * DK
        pairs = GLA_HEADS // 2
        gate_w = mem.take(2 * width)
        gate_b = mem.take(2 * width)
        gain = mem.take(DV)
        lr_cols = mem.take(SEQ)
        log_a = mem.take(TILES, 2 * width)
        soft = mem.take(TILES, 2 * width)
        up = mem.take(2, pairs, SEQ)
        down = mem.take(2, pairs, SEQ)
        tail = mem.take(TILES, 2, width)
        qk_cols = mem.take(2, pairs, SEQ)
        q_up = mem.take(2, pairs, SEQ)
        state = mem.take(2, pairs, N_CHUNKS, DV)
        o = mem.take(TILES, GLA_HEADS * DV)
        gate = mem.take(TILES, GLA_HEADS * DV)
        att = x_cols[:, :, :].rearrange("p c q -> p (c q)").rearrange("p (g i l) -> p g i l", g=4, i=4)
        sums, roots = stat[:, 0:8], stat[:, 8:16]
        cleared = signal("gate_weights_cleared")
        with nc.Block() as block:
            @block.gpsimd
            def _(pool):
                pool.memset(gate_w, 0.0).then_inc(cleared.sem, 1)

            @block.sync
            def _(sp):
                sp.wait_ge(cleared.sem, cleared.at(1))
                load_params(sp, (gate_w[0:RANK, 0:width], t["gla_gate_w_fwd"][0]),
                            (gate_w[RANK:2 * RANK, width:], t["gla_gate_w_bwd"][0]),
                            (gate_b[0:1, 0:width], t["gla_gate_b_fwd"]),
                            (gate_b[0:1, width:], t["gla_gate_b_bwd"]),
                            (gain, spread(t["gla_norm"][0])))
        cleared.advance(1)
        turned, taken, gates, softs, logs, cums, exps, tails = (signal(s) for s in (
            "columns_turned", "columns_taken", "gate_logits", "soft_parts", "log_decays", "decays_summed",
            "decay_factors", "decayed_keys"))
        silus, gains, ups, states, atts, masked, outs, squares, rooted, normed, mixed = (signal(s) for s in (
            "gates_activated", "gates_scaled", "updates_ready", "states_ready", "chunk_scores", "chunk_scores_masked",
            "chunk_outputs", "squares_summed", "root_ready", "outputs_normed", "outputs_turned"))
        updates = [(d, pr, hh, n) for par in range(2) for d in range(2) for pr in range(pairs) for hh in range(2)
                   for n in range(par, N_CHUNKS, 2) if n != (N_CHUNKS - 1 if d == 0 else 0)]
        with nc.Block() as block:
            @block.sync
            def _(sp):
                stream.issue(sp)

            @block.tensor
            def _(pe):
                for a in range(TILES):
                    pe.transpose(ps[0:2 * RANK, 0, a * P:(a + 1) * P], h[:, a, O_LR:O_LR + 2 * RANK], ident[:, :])
                for i, off in enumerate((O_GQ, O_GK)):
                    for pr in range(pairs):
                        for a in range(TILES):
                            last = pe.transpose(ps[:, 1 + i, pr * SEQ + a * P:pr * SEQ + (a + 1) * P],
                                                h[:, a, off + pr * P:off + (pr + 1) * P], ident[:, :])
                last.then_inc(turned.sem, 1)
                params_ready(pe)
                pe.wait_ge(taken.sem, taken.at(1))
                for a in range(TILES):
                    pe.matmul(ps[:, 3 + a, :], lr_cols[0:2 * RANK, a * P:(a + 1) * P], gate_w[0:2 * RANK, :],
                              start=True, stop=False)
                    last = pe.matmul(ps[:, 3 + a, :], ones_row[0:1, :], gate_b[0:1, :], start=False, stop=True)
                last.then_inc(gates.sem, 1)
                pe.wait_ge(logs.sem, logs.at(1))
                for d in range(2):
                    for pr in range(pairs):
                        for a in range(TILES):
                            pe.matmul(ps[:, 5 + d, pr * SEQ + a * P:pr * SEQ + (a + 1) * P],
                                      log_a[:, a, d * width + pr * P:d * width + (pr + 1) * P],
                                      chunk_masks[:, d, :], start=True, stop=True)
                for a in range(TILES):
                    for d in range(2):
                        last = pe.matmul(ps[:, 7 * a, d * width:(d + 1) * width], chunk_masks[:, 2 + d, :],
                                         log_a[:, a, d * width:(d + 1) * width], start=True, stop=True)
                last.then_inc(cums.sem, 1)
                pe.wait_ge(tails.sem, tails.at(1))
                for d, pr, hh, n in updates:
                    half = slice(n % 2 * CHUNK, n % 2 * CHUNK + CHUNK)
                    hd = 2 * pr + hh
                    last = pe.matmul(ps[hh * DK:(hh + 1) * DK, 2 * d + pr + 4 * (n % 2), n // 2 * DV:n // 2 * DV + DV],
                                     tail[half, n // 2, d, hd * DK:(hd + 1) * DK],
                                     h[half, n // 2, O_GV + hd * DV:O_GV + (hd + 1) * DV], start=True, stop=True)
                last.then_inc(ups.sem, 1)
                pe.wait_ge(states.sem, states.at(1))
                for d in range(2):
                    for hh in range(2):
                        half = slice(hh * DK, (hh + 1) * DK)
                        for pr in range(pairs):
                            for a in range(TILES):
                                last = pe.matmul(ps[:, 2 * d + hh, (2 * pr + a) * P:(2 * pr + a + 1) * P],
                                                 down[half, d, pr, a * P:(a + 1) * P],
                                                 q_up[half, d, pr, a * P:(a + 1) * P], start=True, stop=True)
                        last.then_inc(atts.sem, 1)
                pe.wait_ge(masked.sem, masked.at(4))
                for a in range(TILES):
                    for hd in range(GLA_HEADS):
                        pr, hh = hd // 2, hd % 2
                        bank = 4 + 2 * a + hh
                        cols = slice(pr * DV, (pr + 1) * DV)
                        inter = [(d, n) for d in range(2) for n in (2 * a, 2 * a + 1)
                                 if n != (0 if d == 0 else N_CHUNKS - 1)]
                        for d in range(2):
                            pe.matmul(ps[:, bank, cols], att[:, 2 * d + hh, 2 * pr + a, :],
                                      h[:, a, O_GV + hd * DV:O_GV + (hd + 1) * DV], start=d == 0, stop=False,
                                      skip_group_check=True)
                        for d, n in inter:
                            last = pe.matmul(ps[n % 2 * CHUNK:n % 2 * CHUNK + CHUNK, bank, cols],
                                             q_up[hh * DK:(hh + 1) * DK, d, pr, n * CHUNK:(n + 1) * CHUNK],
                                             state[hh * DK:(hh + 1) * DK, d, pr, n, :], start=False,
                                             stop=(d, n) == inter[-1], skip_group_check=True)
                last.then_inc(outs.sem, 1)
                pe.wait_ge(normed.sem, normed.at(1))
                for c in range(GLA_HEADS):
                    for a in range(TILES):
                        last = pe.transpose(ps[:, c // 2, c % 2 * SEQ + a * P:c % 2 * SEQ + (a + 1) * P],
                                            o[:, a, c * P:(c + 1) * P], ident[:, :])
                last.then_inc(mixed.sem, 1)

            @block.scalar
            def _(act):
                act.activation(gate, h[:, :, O_GR:O_GR + GLA_HEADS * DV], ACT.Silu).then_inc(silus.sem, 1)
                act.wait_ge(turned.sem, turned.at(1))
                act.copy(lr_cols[0:2 * RANK, :], ps[0:2 * RANK, 0, 0:SEQ]).then_inc(taken.sem, 1)
                act.activation(qk_cols[:, 0], ps[:, 1, :].rearrange("p (c q) -> p c q", c=pairs), ACT.Copy,
                               scale=DK ** -0.5)
                act.copy(qk_cols[:, 1], ps[:, 2, :].rearrange("p (c q) -> p c q", c=pairs))
                act.wait_ge(gates.sem, gates.at(1))
                z = ps[:, 3:3 + TILES, :]
                act_chain.link(act, act.activation(soft, z, ACT.Abs))
                act_chain.link(act, act.activation(soft, soft, ACT.Exp, scale=-1.0))
                act.activation(soft, soft, ACT.Ln, bias=1.0).then_inc(softs.sem, 1)
                act.wait_ge(cums.sem, cums.at(1))
                for d in range(2):
                    cum = ps[:, 5 + d, :].rearrange("p (c q) -> p c q", c=pairs)
                    act.activation(up[:, d], cum, ACT.Exp, scale=1.0 / GATE_NORM)
                    act.activation(down[:, d], cum, ACT.Exp, scale=-1.0 / GATE_NORM)
                for a in range(TILES):
                    last = act.activation(tail[:, a], ps[:, 7 * a, :].rearrange("p (d f) -> p d f", d=2), ACT.Exp,
                                          scale=1.0 / GATE_NORM)
                last.then_inc(exps.sem, 1)
                act.wait_ge(outs.sem, outs.at(1))
                for a in range(TILES):
                    for hd in range(GLA_HEADS):
                        last = act.activation(soft[:, 0, 0:DV], ps[:, 4 + 2 * a + hd % 2, hd // 2 * DV:hd // 2 * DV + DV],
                                              ACT.Square, accum_out=sums[:, GLA_HEADS * a + hd:GLA_HEADS * a + hd + 1])
                        act_chain.link(act, last)
                act.copy(sums[:, 0:1], sums[:, 0:1]).then_inc(squares.sem, 1)
                act.wait_ge(mixed.sem, mixed.at(1))
                for c in range(0, GLA_HEADS, 2):
                    act.copy(mix_cols[:, 4 + c:6 + c, :], ps[:, c // 2, :].rearrange("p (c q) -> p c q", c=2))

            @block.gpsimd
            def _(pool):
                pool.wait_ge(squares.sem, squares.at(1))
                inverse_root(pool, roots, sums, DV).then_inc(rooted.sem, 1)

            @block.vector
            def _(dve):
                params_ready(dve)
                dve.wait_ge(silus.sem, silus.at(1))
                for a in range(TILES):
                    view = gate[:, a, :].rearrange("p (h e) -> p h e", e=DV)
                    dve.tensor_tensor(view, view, gain.rearrange("p (u e) -> p u e", u=1)
                                      .broadcast_to([P, GLA_HEADS, DV]), ALU.mult)
                dve.wait_ge(softs.sem, softs.at(1))
                for a in range(TILES):
                    last = dve.scalar_tensor_tensor(out=log_a[:, a, :], in0=ps[:, 3 + a, :], scalar=0.0,
                                                    in1=soft[:, a, :], op0=ALU.min, op1=ALU.subtract)
                last.then_inc(logs.sem, 1)
                dve.wait_ge(exps.sem, exps.at(1))
                for d in range(2):
                    dve.tensor_tensor(q_up[:, d], qk_cols[:, 0], up[:, d], ALU.mult)
                    dve.tensor_tensor(down[:, d], qk_cols[:, 1], down[:, d], ALU.mult)
                for a in range(TILES):
                    for d in range(2):
                        last = dve.tensor_tensor(tail[:, a, d, :], tail[:, a, d, :], h[:, a, O_GK:O_GK + width],
                                                 ALU.mult)
                last.then_inc(tails.sem, 1)
                dve.wait_ge(ups.sem, ups.at(1))
                order = {0: range(0, N_CHUNKS - 1), 1: range(N_CHUNKS - 1, 0, -1)}
                for step in range(N_CHUNKS - 1):
                    for d in range(2):
                        n = order[d][step]
                        nxt, end = (n + 1, (n + 1) * CHUNK - 1) if d == 0 else (n - 1, n * CHUNK)
                        for pr in range(pairs):
                            update = ps[:, 2 * d + pr + 4 * (n % 2), n // 2 * DV:n // 2 * DV + DV]
                            if step == 0:
                                last = dve.tensor_copy(state[:, d, pr, nxt, :], update)
                            else:
                                last = dve.scalar_tensor_tensor(
                                    out=state[:, d, pr, nxt, :], in0=state[:, d, pr, n, :],
                                    scalar=up[:, d, pr, end:end + 1], in1=update, op0=ALU.mult, op1=ALU.add)
                    if step < N_CHUNKS - 2:
                        dve_chain.link(dve, last)
                last.then_inc(states.sem, 1)
                for g in range(4):
                    dve.wait_ge(atts.sem, atts.at(g + 1))
                    mask = chunk_masks[:, g // 2:g // 2 + 1, :].broadcast_to([P, 4, P])
                    dve.tensor_tensor(att[:, g], ps[:, g, :].rearrange("p (i l) -> p i l", i=4), mask,
                                      ALU.mult).then_inc(masked.sem, 1)
                dve.wait_ge(rooted.sem, rooted.at(1))
                for a in range(TILES):
                    for hd in range(GLA_HEADS):
                        cols = slice(hd * DV, (hd + 1) * DV)
                        last = dve.scalar_tensor_tensor(
                            out=o[:, a, cols], in0=ps[:, 4 + 2 * a + hd % 2, hd // 2 * DV:hd // 2 * DV + DV],
                            scalar=roots[:, GLA_HEADS * a + hd:GLA_HEADS * a + hd + 1], in1=gate[:, a, cols],
                            op0=ALU.mult, op1=ALU.mult)
                last.then_inc(normed.sem, 1)
        for s in (turned, taken, gates, softs, logs, cums, exps, tails, silus, ups, states, outs, squares, rooted,
                  normed, mixed):
            s.advance(1)
        atts.advance(4), masked.advance(4)

    def odd_mixer():
        mem = Arena()
        h = mem.take(TILES, ODD_IN)
        n_heads = GQA_HEADS + KV_HEADS
        gains = mem.take(2, HD)
        to_columns(x, x_cols, DC, more_params=[(gains[:, 0, :], spread(t["gqa_q_norm"][0])),
                                               (gains[:, 1, :], spread(t["gqa_k_norm"][0])),
                                               (ln_params[:, 0, :], spread(t["ln1_g"][1])),
                                               (ln_params[:, 1, :], spread(t["ln1_b"][1]))])
        project(ODD_IN, h)
        q_cols = mem.take(GQA_HEADS // 2, SEQ)
        k_cols = mem.take(KV_HEADS, SEQ)
        mem_att = mem.at
        k_twice = mem.take(TILES, KV_HEADS, 2, HD)
        squares = mem.take(TILES, n_heads * HD)
        scratch = mem.take(TILES, 4, n_heads * HD // 2)
        sums = stat[:, 0:TILES * n_heads]
        roots = stat[:, TILES * n_heads:2 * TILES * n_heads]
        squared, summed, rooted, made, turned = (signal(s) for s in (
            "squares_made", "squares_summed", "root_ready", "qk_heads_ready", "columns_turned"))
        qk = [h[:, a, 0:n_heads * HD].rearrange("p (h d) -> p h d", d=HD) for a in range(TILES)]

        def heads_of(engine, chain, a):
            root = roots[:, a * n_heads:(a + 1) * n_heads].rearrange("p (h u) -> p h u", u=1)
            chain.link(engine, engine.tensor_tensor(qk[a], qk[a], root.broadcast_to([P, n_heads, HD]), ALU.mult))
            engine.tensor_tensor(qk[a][:, 0:GQA_HEADS], qk[a][:, 0:GQA_HEADS],
                                 gains[:, 0:1, :].broadcast_to([P, GQA_HEADS, HD]), ALU.mult)
            chain.link(engine, engine.tensor_tensor(qk[a][:, GQA_HEADS:], qk[a][:, GQA_HEADS:],
                                                    gains[:, 1:2, :].broadcast_to([P, KV_HEADS, HD]), ALU.mult))
            wide = [scratch[:, a, i, :].rearrange("p (h f) -> p h f", h=n_heads) for i in range(4)]
            cos, sin = (rope_gqa[:, a, i:i + 1, :].broadcast_to([P, n_heads, HD // 2]) for i in range(2))
            chain.link(engine, rotate(engine, qk[a][:, :, 0:HD // 2], qk[a][:, :, HD // 2:], cos, sin, wide, chain))
            return engine.tensor_copy(k_twice[:, a], qk[a][:, GQA_HEADS:, :].rearrange("p h (u d) -> p h u d", u=1)
                                      .broadcast_to([P, KV_HEADS, 2, HD]))

        with nc.Block() as block:
            @block.sync
            def _(sp):
                stream.issue(sp)

            @block.scalar
            def _(act):
                for a in range(TILES):
                    act.activation(squares[:, a, :], h[:, a, 0:n_heads * HD], ACT.Square).then_inc(squared.sem, 1)
                for b in range((GQA_HEADS // 2 + KV_HEADS) // 2):
                    act.wait_ge(turned.sem, turned.at(b + 1))
                    dst = q_cols[:, 2 * b:2 * b + 2, :] if b < GQA_HEADS // 4 else \
                        k_cols[:, 2 * b - GQA_HEADS // 2:2 * b - GQA_HEADS // 2 + 2, :]
                    act.copy(dst, ps[:, b, :].rearrange("p (c q) -> p c q", c=2))

            @block.vector
            def _(dve):
                for a in range(TILES):
                    dve.wait_ge(squared.sem, squared.at(a + 1))
                    dve.tensor_reduce(sums[:, a * n_heads:(a + 1) * n_heads],
                                      squares[:, a, :].rearrange("p (h d) -> p h d", d=HD), AX,
                                      ALU.add).then_inc(summed.sem, 1)
                params_ready(dve)
                dve.wait_ge(rooted.sem, rooted.at(1))
                heads_of(dve, dve_chain, 0).then_inc(made.sem, 1)

            @block.gpsimd
            def _(pool):
                pool.wait_ge(summed.sem, summed.at(TILES))
                inverse_root(pool, roots, sums, HD).then_inc(rooted.sem, 1)
                params_ready(pool)
                pool.wait_ge(rooted.sem, rooted.at(1))
                heads_of(pool, pool_chain, 1).then_inc(made.sem, 1)

            @block.tensor
            def _(pe):
                pe.wait_ge(made.sem, made.at(2))
                for b in range((GQA_HEADS // 2 + KV_HEADS) // 2):
                    for i in range(2):
                        c = 2 * b + i
                        for a in range(TILES):
                            src = h[:, a, c * P:(c + 1) * P] if c < GQA_HEADS // 2 else \
                                k_twice[:, a, c - GQA_HEADS // 2].rearrange("p u d -> p (u d)")
                            last = pe.transpose(ps[:, b, i * SEQ + a * P:i * SEQ + (a + 1) * P], src, ident[:, :])
                    last.then_inc(turned.sem, 1)
        squared.advance(TILES), summed.advance(TILES), rooted.advance(1), made.advance(2)
        turned.advance((GQA_HEADS // 2 + KV_HEADS) // 2)
        group = GQA_HEADS // KV_HEADS
        half = lambda i: slice(i % 2 * HD, i % 2 * HD + HD)
        attention(GQA_HEADS, lambda i: q_cols[half(i), i // 2, :], lambda i: k_cols[half(i), i // group, :],
                  lambda i, b: h[:, b, (n_heads + i // group) * HD:(n_heads + i // group + 1) * HD], 0, HD ** -0.5,
                  False, Arena(mem_att))

    def experts(layer):
        mem = Arena()
        picked_cols = mem.take(DC, EXPERTS, CAP)
        spread_back = mem.take(EXPERTS, SEQ)
        rest = mem.take(TILES, D)
        tokens_now = mem.take(DC, CAP)
        back_now = mem.take(SEQ)
        silu_g = mem.take(QW)
        hidden = mem.take(QW)
        hidden_cols = mem.take(2, P)
        partial = mem.take(D)
        loop_end = mem.at
        one_hot = mem.take(TILES, EXPERTS, CAP)
        p_tokens = mem.take(TILES, PLE_DIM)
        p_cols = mem.take(2, SEQ)
        router = mem.take(DC, EXPERTS)
        slots = mem.take(CAP)
        aff = mem.take(TILES, EXPERTS)
        slot_tokens = mem.take(TILES, EXPERTS)
        ones = mem.take(SEQ)
        left = mem.take(SEQ)
        chosen = mem.take(SEQ)
        rank = mem.take(SEQ)
        bias = Arena(loop_end - D).take(D)
        tops = stat[:, 32:64]
        stats = stat[:, 64:96]
        four_hot = [x_cols[:, :, :].rearrange("p c q -> p (c q)"), mix_cols[:, :, :].rearrange("p c q -> p (c q)")]
        four_hot = [v.rearrange("p (e j s) -> p e j s", e=EXPERTS, j=QUADS) for v in four_hot]

        to_columns(x, x_cols, DC, more_params=[
            (router, t["router_w"][layer].rearrange("(c p) e -> p c e", p=P)),
            (p_tokens, t["p"][layer, 0].rearrange("(a p) d -> p a d", p=P)),
            (slots, spread(t["c_slots"])),
            (bias[0:1, :], t["ple_gate_b"][layer:layer + 1, :]),
            (ln_params[:, 0, :], spread(t["ln2_g"][layer])), (ln_params[:, 1, :], spread(t["ln2_b"][layer]))])

        gate_units = stream.take(2)
        ple_unit = stream.take(1)
        logits, affs, turned, ranked, turned_back, hot, gathered, kept, four, spread_s = (signal(s) for s in (
            "logits_ready", "affinities_ready", "affinities_turned", "slots_ranked", "slots_turned", "one_hot_ready",
            "tokens_gathered", "gathered_kept", "four_hot_ready", "one_hot_turned"))
        exped, maxed = signal("router_exps"), signal("router_max")
        ple_p, ple_pk, ple_g, ple_s, ple_v = (signal(s) for s in (
            "ple_inputs_turned", "ple_inputs_kept", "ple_gates_ready", "ple_gates_activated", "ple_values_ready"))
        spread_kept, ones_made = signal("one_hot_kept"), signal("ones_made")
        with nc.Block() as block:
            @block.sync
            def _(sp):
                stream.issue(sp)

            @block.tensor
            def _(pe):
                params_ready(pe)
                for a in range(TILES):
                    for c in range(DC):
                        last = pe.matmul(ps[:, 0, a * EXPERTS:(a + 1) * EXPERTS], x_cols[:, c, a * P:(a + 1) * P],
                                         router[:, c, :], start=c == 0, stop=c == DC - 1)
                last.then_inc(logits.sem, 1)
                for c in range(2):
                    for a in range(TILES):
                        last = pe.transpose(ps[:, 1, c * SEQ + a * P:c * SEQ + (a + 1) * P],
                                            p_tokens[:, a, c * P:(c + 1) * P], ident[:, :])
                last.then_inc(ple_p.sem, 1)
                for h in range(2):
                    w = stream.slot(gate_units + h).rearrange("p (c n) -> p c n", c=DC)
                    stream.wait(pe, gate_units + h)
                    for a in range(TILES):
                        pe.matmul(ps[:, 4 + 2 * h + a, :], ones_row[0:1, :], bias[0:1, h * BANK:(h + 1) * BANK],
                                  start=True, stop=False)
                        for c in range(DC):
                            last = pe.matmul(ps[:, 4 + 2 * h + a, :], x_cols[:, c, a * P:(a + 1) * P], w[:, c, :],
                                             start=False, stop=c == DC - 1)
                        last.then_inc(ple_g.sem if a == 0 else stream.used, 1)
                    if h == 0:
                        pe.wait_ge(affs.sem, affs.at(1))
                        for a in range(TILES):
                            last = pe.transpose(ps[0:EXPERTS, 2, a * P:(a + 1) * P], aff[:, a, :], ident[:, :])
                        last.then_inc(turned.sem, 1)
                stream.wait(pe, ple_unit)
                pe.wait_ge(ple_pk.sem, ple_pk.at(1))
                w = stream.slot(ple_unit)[:, 0:2 * D].rearrange("p (c n) -> p c n", c=2)
                pe.wait_ge(ple_s.sem, ple_s.at(4))
                for h in range(2):
                    for a in range(TILES):
                        for c in range(2):
                            last = pe.matmul(ps[:, 4 + 2 * h + a, :], p_cols[:, c, a * P:(a + 1) * P],
                                             w[:, c, h * BANK:(h + 1) * BANK], start=c == 0, stop=c == 1)
                        last.then_inc(stream.used if (h, a) == (1, 1) else ple_v.sem, 1)
                pe.wait_ge(ranked.sem, ranked.at(1))
                for a in range(TILES):
                    last = pe.transpose(ps[:, 3, a * EXPERTS:(a + 1) * EXPERTS], rank[0:EXPERTS, a * P:(a + 1) * P],
                                        ident[0:EXPERTS, 0:EXPERTS])
                last.then_inc(turned_back.sem, 1)
                pe.wait_ge(hot.sem, hot.at(1))
                for c in range(DC):
                    if c >= 4:
                        pe.wait_ge(kept.sem, kept.at(c - 3))
                    for a in range(TILES):
                        last = pe.matmul(ps[:, c % 4, :], x[:, a, c * P:(c + 1) * P],
                                         one_hot[:, a].rearrange("p e s -> p (e s)"), start=a == 0,
                                         stop=a == TILES - 1)
                    last.then_inc(gathered.sem, 1)
                pe.wait_ge(four.sem, four.at(2))
                for g in range(EXPERTS // 2):
                    bank = 4 + g % 4
                    if g >= 4:
                        pe.wait_ge(spread_kept.sem, spread_kept.at(g - 3))
                    for i in range(2):
                        for a in range(TILES):
                            last = pe.transpose(ps[:, bank, i * SEQ + a * P:i * SEQ + (a + 1) * P],
                                                four_hot[a][:, 2 * g + i].rearrange("p j s -> p (j s)"), ident[:, :])
                    last.then_inc(spread_s.sem, 1)

            @block.scalar
            def _(act):
                act.wait_ge(maxed.sem, maxed.at(1))
                act.activation(aff, aff, ACT.Exp).then_inc(exped.sem, 1)
                act.wait_ge(ple_p.sem, ple_p.at(1))
                act.copy(p_cols, ps[:, 1, :].rearrange("p (c q) -> p c q", c=2)).then_inc(ple_pk.sem, 1)
                for h in range(2):
                    for a in range(TILES):
                        if a == 0:
                            act.wait_ge(ple_g.sem, ple_g.at(h + 1))
                        else:
                            act.wait_ge(stream.used, gate_units + h + 1)
                        act.activation(rest[:, a, h * BANK:(h + 1) * BANK], ps[:, 4 + 2 * h + a, :],
                                       ACT.Sigmoid).then_inc(ple_s.sem, 1)
                for c in range(DC):
                    act.wait_ge(gathered.sem, gathered.at(c + 1))
                    act.copy(picked_cols[:, c], ps[:, c % 4, :].rearrange("p (e s) -> p e s", e=EXPERTS)
                             ).then_inc(kept.sem, 1)
                for g in range(EXPERTS // 2):
                    act.wait_ge(spread_s.sem, spread_s.at(g + 1))
                    act.copy(spread_back[:, 2 * g:2 * g + 2, :], ps[:, 4 + g % 4, :].rearrange("p (e q) -> p e q", e=2)
                             ).then_inc(spread_kept.sem, 1)

            @block.vector
            def _(dve):
                params_ready(dve)
                dve.wait_ge(logits.sem, logits.at(1))
                lg = ps[:, 0, 0:TILES * EXPERTS].rearrange("p (a e) -> p a e", a=TILES)
                top, total = tops[:, 0:TILES], tops[:, TILES:2 * TILES]
                wide = lambda v: v.rearrange("p (a u) -> p a u", u=1).broadcast_to([P, TILES, EXPERTS])
                dve_chain.link(dve, dve.tensor_reduce(top, lg, AX, ALU.max))
                dve.tensor_tensor(aff, lg, wide(top), ALU.subtract).then_inc(maxed.sem, 1)
                dve.wait_ge(exped.sem, exped.at(1))
                dve_chain.link(dve, dve.tensor_reduce(total, aff, AX, ALU.add))
                dve_chain.link(dve, dve.reciprocal(total, total))
                dve.tensor_tensor(aff, aff, wide(total), ALU.mult).then_inc(affs.sem, 1)
                dve.wait_ge(turned.sem, turned.at(1))
                dve_chain.link(dve, dve.tensor_copy(left[0:EXPERTS, :], ps[0:EXPERTS, 2, 0:SEQ]))
                for r in range(CAP // 8):
                    dve_chain.link(dve, dve.max(tops[0:EXPERTS, 8:16], left[0:EXPERTS, :]))
                    dve_chain.link(dve, dve.match_replace(out=left[0:EXPERTS, :], in_to_replace=tops[0:EXPERTS, 8:16],
                                                          in_values=left[0:EXPERTS, :], imm_value=-1.0))
                dve_chain.link(dve, dve.tensor_scalar(chosen[0:EXPERTS, :], left[0:EXPERTS, :], 0.0, None, ALU.is_lt))
                dve.wait_ge(ones_made.sem, ones_made.at(1))
                dve_chain.link(dve, dve.tensor_tensor_scan(rank[0:EXPERTS, :], ones[0:EXPERTS, :],
                                                           chosen[0:EXPERTS, :], 0.0, ALU.mult, ALU.add))
                dve.tensor_tensor(rank[0:EXPERTS, :], rank[0:EXPERTS, :], chosen[0:EXPERTS, :],
                                  ALU.mult).then_inc(ranked.sem, 1)
                for h in range(2):
                    for a in range(TILES):
                        if (h, a) == (1, 1):
                            dve.wait_ge(stream.used, ple_unit + 1)
                        else:
                            dve.wait_ge(ple_v.sem, ple_v.at(2 * h + a + 1))
                        last = dve.tensor_tensor(rest[:, a, h * BANK:(h + 1) * BANK],
                                                 rest[:, a, h * BANK:(h + 1) * BANK], ps[:, 4 + 2 * h + a, :], ALU.mult)
                dve.wait_ge(turned_back.sem, turned_back.at(1))
                dve_chain.link(dve, dve.tensor_copy(
                    slot_tokens, ps[:, 3, 0:TILES * EXPERTS].rearrange("p (a e) -> p a e", a=TILES)))
                for a in range(TILES):
                    last = dve.tensor_tensor(one_hot[:, a],
                                             slot_tokens[:, a].rearrange("p (e u) -> p e u", u=1)
                                             .broadcast_to([P, EXPERTS, CAP]),
                                             slots.rearrange("p (u s) -> p u s", u=1).broadcast_to([P, EXPERTS, CAP]),
                                             ALU.is_equal)
                last.then_inc(hot.sem, 1)
                dve.wait_ge(hot.sem, hot.at(1))
                for a in range(TILES):
                    dve.tensor_tensor(four_hot[a],
                                      one_hot[:, a].rearrange("p e (u s) -> p e u s", u=1)
                                      .broadcast_to([P, EXPERTS, QUADS, CAP]),
                                      aff[:, a].rearrange("p (e u v) -> p e u v", u=1, v=1)
                                      .broadcast_to([P, EXPERTS, QUADS, CAP]), ALU.mult).then_inc(four.sem, 1)
                for a in range(TILES):
                    dve.scalar_tensor_tensor(out=rest[:, a, :], in0=x[:, a, :], scalar=ALPHA, in1=rest[:, a, :],
                                             op0=ALU.mult, op1=ALU.add)

            @block.gpsimd
            def _(pool):
                pool.memset(ones, 1.0).then_inc(ones_made.sem, 1)
        for s in (logits, affs, turned, ranked, turned_back, hot, exped, ple_p, ple_pk):
            s.advance(1)
        maxed.advance(1), ones_made.advance(1), four.advance(2), ple_g.advance(2), ple_s.advance(4), ple_v.advance(3)
        gathered.advance(DC), kept.advance(DC), spread_s.advance(EXPERTS // 2), spread_kept.advance(EXPERTS // 2)

        first = stream.take(6 * EXPERTS)
        assert stream.issued == first + WEIGHT_SLOTS
        token_set, back_set, silued, hid, h_turned, h_kept, part_0, part_1 = (signal(s) for s in (
            "expert_tokens_set", "scatter_rows_set", "expert_gates_activated", "expert_hidden_ready",
            "expert_hidden_turned", "expert_hidden_kept", "partial_0_kept", "partial_1_kept"))
        used = stream.used
        hc = hidden_cols
        with nc.Block() as block:
            @block.sync
            def _(sp):
                with sp.Fori(0, EXPERTS - 1) as e:
                    for k in range(6):
                        sp.wait_ge(used, e * 6 + (first + k + 1))
                        stream.load(sp, first + k, e + 1)
                stream.issued = first + 6 * EXPERTS
                stream.issue(sp)

            @block.tensor
            def _(pe):
                for b in range(4):
                    pe.matmul(ps[:, b, :], zeros_bf[:, 0:P], zeros_bf[:, :], start=True, stop=False,
                              skip_group_check=True)
                with pe.Fori(0, EXPERTS) as e:
                    pe.wait_ge(token_set.sem, e + token_set.at(1))
                    for k in range(4):
                        u = first + k
                        w = stream.slot(u).rearrange("p (c f) -> p c f", c=DC // 2)
                        pe.wait_ge(stream.arrived[u % WEIGHT_SLOTS], e * 16 + stream.value[u])
                        for c in range(DC // 2):
                            cc = k % 2 * DC // 2 + c
                            for j in range(QUADS):
                                last = pe.matmul(ps[j * CAP:(j + 1) * CAP, 4 + k // 2, 0:QW], tokens_now[:, cc, :],
                                                 w[:, c, j * QW:(j + 1) * QW], start=cc == 0, stop=cc == DC - 1)
                        last.then_inc(used, 1)
                    pe.wait_ge(hid.sem, e + hid.at(1))
                    for i in range(2):
                        last = pe.transpose(ps[:, 4, i * P:(i + 1) * P], hidden[:, i * P:(i + 1) * P], ident[:, :])
                    last.then_inc(h_turned.sem, 1)
                    pe.wait_ge(h_kept.sem, e + h_kept.at(1))
                    for h in range(2):
                        u = first + 4 + h
                        w = stream.slot(u).rearrange("p (c f) -> p c f", c=DC)
                        pe.wait_ge(stream.arrived[u % WEIGHT_SLOTS], e * 16 + stream.value[u])
                        for i in range(2):
                            for j in range(QUADS):
                                last = pe.matmul(ps[j * CAP:(j + 1) * CAP, 6 + h, :], hc[:, i, j * CAP:(j + 1) * CAP],
                                                 w[:, 2 * j + i, :], start=i == 0, stop=i == 1)
                        last.then_inc(used, 1)
                    pe.wait_ge(back_set.sem, e + back_set.at(1))
                    for h, part in enumerate((part_0, part_1)):
                        pe.wait_ge(part.sem, e + part.at(1))
                        for a in range(TILES):
                            pe.matmul(ps[:, 2 * h + a, :], back_now[:, a * P:(a + 1) * P],
                                             partial[:, h * BANK:(h + 1) * BANK], start=False, stop=False,
                                             skip_group_check=True)

            @block.scalar
            def _(act):
                with act.Fori(0, EXPERTS) as e:
                    act.wait_ge(used, e * 6 + (first + 2))
                    act.activation(silu_g, ps[:, 4, 0:QW], ACT.Silu).then_inc(silued.sem, 1)
                    act.wait_ge(h_turned.sem, e + h_turned.at(1))
                    act.copy(hc, ps[:, 4, 0:2 * P].rearrange("p (i q) -> p i q", i=2)).then_inc(h_kept.sem, 1)
                    act.wait_ge(used, e * 6 + (first + 5))
                    act.copy(partial[:, 0:BANK], ps[:, 6, :]).then_inc(part_0.sem, 1)

            @block.vector
            def _(dve):
                with dve.Fori(0, EXPERTS) as e:
                    dve.wait_ge(silued.sem, e + silued.at(1))
                    dve.wait_ge(used, e * 6 + (first + 4))
                    dve.tensor_tensor(hidden, silu_g, ps[:, 5, 0:QW], ALU.mult).then_inc(hid.sem, 1)
                    dve.wait_ge(used, e * 6 + (first + 6))
                    dve.tensor_copy(partial[:, BANK:], ps[:, 7, :]).then_inc(part_1.sem, 1)

            @block.gpsimd
            def _(pool):
                with pool.Fori(0, EXPERTS) as e:
                    pool.wait_ge(used, e * 6 + (first - 2))
                    pool.tensor_copy(tokens_now.rearrange("p c (u s) -> p c u s", u=1),
                                     picked_cols[:, :, bass.ds(e, 1), :]).then_inc(token_set.sem, 1)
                    pool.wait_ge(used, e * 6 + (first + 1))
                    pool.tensor_copy(back_now.rearrange("p (u q) -> p u q", u=1),
                                     spread_back[:, bass.ds(e, 1), :]).then_inc(back_set.sem, 1)
        for s in (token_set, back_set, silued, hid, h_turned, h_kept, part_0, part_1):
            s.advance(EXPERTS)

        wanted, got = signal("root_wanted"), signal("root_ready")
        stats = stat[:, 0:32].rearrange("p (a k) -> p a k", a=TILES)
        with nc.Block() as block:
            @block.sync
            def _(sp):
                stream.issue(sp)

            @block.vector
            def _(dve):
                params_ready(dve)
                for h in range(2):
                    for a in range(TILES):
                        cols = slice(h * BANK, (h + 1) * BANK)
                        last = dve.tensor_tensor(rest[:, a, cols], rest[:, a, cols], ps[:, 2 * h + a, :], ALU.add)
                dve_chain.link(dve, last)
                layer_norm_steps(dve, rest, stats, wanted, got)

            @block.gpsimd
            def _(pool):
                layer_norm_root(pool, stats, wanted, got)
        wanted.advance(1), got.advance(1)

    def rms_columns(gain_row):
        normed = Arena(arena_size - TILES * D).take(TILES, D)
        sums, roots = stat[:, 0:TILES], stat[:, TILES:2 * TILES]
        squares, rooted, scaled = signal("squares_summed"), signal("root_ready"), signal("tokens_scaled")
        with nc.Block() as block:
            @block.sync
            def _(sp):
                load_params(sp, (norm_cols[:, :], gain_row.rearrange("(c p) -> p c", p=P)))
                stream.issue(sp)

            @block.scalar
            def _(act):
                for a in range(TILES):
                    last = act.activation(normed[:, a, :], x[:, a, :], ACT.Square, accum_out=sums[:, a:a + 1])
                last.then_inc(squares.sem, 1)
                act.wait_ge(rooted.sem, rooted.at(1))
                act.wait_ge(squares.sem, squares.at(1))
                act.activation(normed[:, 0, :], x[:, 0, :], ACT.Copy, scale=roots[:, 0:1])

            @block.vector
            def _(dve):
                dve.wait_ge(rooted.sem, rooted.at(1))
                dve.tensor_scalar(normed[:, 1, :], x[:, 1, :], roots[:, 1:2], None, ALU.mult)

            @block.gpsimd
            def _(pool):
                pool.wait_ge(squares.sem, squares.at(1))
                inverse_root(pool, roots, sums, D).then_inc(rooted.sem, 1)
        squares.advance(1), rooted.advance(1)
        to_columns(normed, x_cols, DC, gain=norm_cols)

    def ffn():
        mem = Arena()
        silu_g = mem.take(2, SEQ)
        hid = mem.take(3, 2, SEQ)
        n_units = 2 * F_GROUPS
        first = stream.take(n_units)
        assert stream.issued == first + WEIGHT_SLOTS
        used = stream.used
        up_ready, silued, made = signal("up_products_ready"), signal("ffn_gates_activated"), signal("hidden_ready")
        body = WEIGHT_SLOTS // 2
        trips = (F_GROUPS - 2) // body
        assert trips * body == F_GROUPS - 2

        def up_unit(i):
            return first if i == 0 else first + 2 * i - 1

        def down_unit(i):
            return first + 2 * i + 2 if i < F_GROUPS - 1 else first + n_units - 1

        def each_group(engine, steps):
            steps(0, 0)
            with engine.Fori(0, trips) as r:
                for i in range(1, body + 1):
                    steps(i, r)
            steps(F_GROUPS - 1, 0)

        def arrived(pe, u, r):
            value = stream.value[u]
            step = stream.value[u + WEIGHT_SLOTS] - value if u + WEIGHT_SLOTS < first + n_units else 0
            pe.wait_ge(stream.arrived[u % WEIGHT_SLOTS], value if isinstance(r, int) else r * step + value)

        with nc.Block() as block:
            @block.sync
            def _(sp):
                def reload(u, r, shift):
                    sp.wait_ge(used, r * WEIGHT_SLOTS + (u - WEIGHT_SLOTS + 1))
                    for dst, src in stream.units[u][0](stream.slot(u), r * (body * FG) + stream.units[u][1]):
                        sp.dma_start(dst, src).then_inc(stream.arrived[u % WEIGHT_SLOTS], 16)

                reload(first + WEIGHT_SLOTS, 0, 0)
                with sp.Fori(0, trips - 1) as r:
                    for k in range(WEIGHT_SLOTS):
                        reload(first + WEIGHT_SLOTS + 1 + k, r, 0)
                stream.issued = first + 1 + WEIGHT_SLOTS * trips
                stream.issue(sp)

            @block.tensor
            def _(pe):
                for b in range(4):
                    pe.matmul(ps[:, b, :], zeros_bf[:, 0:P], zeros_bf[:, :], start=True, stop=False,
                              skip_group_check=True)

                def up(i, r):
                    u = up_unit(i)
                    arrived(pe, u, r)
                    w = stream.slot(u).rearrange("p (h c f) -> p h c f", h=2, c=DC)
                    for f in range(2):
                        if i > 0:
                            pe.wait_ge(made.sem, r * (2 * body) + made.at(2 * i + f - 1))
                        for h in range(2):
                            for c in range(DC):
                                last = pe.matmul(ps[:, 4 + f, h * SEQ:(h + 1) * SEQ], w[:, h, c, f * P:(f + 1) * P],
                                                 x_cols[:, c, :], start=c == 0, stop=c == DC - 1)
                        last.then_inc(up_ready.sem if f == 0 else used, 1)

                def down(i, r):
                    u = down_unit(i)
                    arrived(pe, u, r)
                    w = stream.slot(u)[:, 0:2 * D].rearrange("p (c n) -> p c n", c=2)
                    for f in range(2):
                        pe.wait_ge(made.sem, r * (2 * body) + made.at(2 * i + f + 1))
                        for a in range(TILES):
                            for h in range(2):
                                last = pe.matmul(ps[:, 2 * h + a, :], hid[:, i % 3, f, a * P:(a + 1) * P],
                                                 w[:, f, h * BANK:(h + 1) * BANK], start=False, stop=False,
                                                 skip_group_check=True)
                    last.then_inc(used, 1)

                def steps(i, r):
                    up(i, r)
                    if i > 0:
                        down(i - 1, r)

                each_group(pe, steps)
                down(F_GROUPS - 1, 0)

            def products_ready(engine, i, f, r):
                if f == 0:
                    engine.wait_ge(up_ready.sem, r * body + up_ready.at(i + 1))
                else:
                    engine.wait_ge(used, r * WEIGHT_SLOTS + (up_unit(i) + 1))

            @block.scalar
            def _(act):
                def steps(i, r):
                    for f in range(2):
                        products_ready(act, i, f, r)
                        if i > 0:
                            act.wait_ge(made.sem, r * (2 * body) + made.at(2 * i + f - 1))
                        act.activation(silu_g[:, f, :], ps[:, 4 + f, 0:SEQ], ACT.Silu).then_inc(silued.sem, 1)

                each_group(act, steps)

            @block.vector
            def _(dve):
                def steps(i, r):
                    for f in range(2):
                        products_ready(dve, i, f, r)
                        if i >= 1:
                            dve.wait_ge(used, r * WEIGHT_SLOTS + (first + 2 * i - 3))
                        dve.wait_ge(silued.sem, r * (2 * body) + silued.at(2 * i + f + 1))
                        dve.tensor_tensor(hid[:, i % 3, f, :], silu_g[:, f, :], ps[:, 4 + f, SEQ:2 * SEQ],
                                          ALU.mult).then_inc(made.sem, 1)

                each_group(dve, steps)
                dve.wait_ge(used, first + n_units)
                for h in range(2):
                    for a in range(TILES):
                        cols = slice(h * BANK, (h + 1) * BANK)
                        dve.scalar_tensor_tensor(out=x[:, a, cols], in0=ps[:, 2 * h + a, :], scalar=0.5,
                                                 in1=x[:, a, cols], op0=ALU.mult, op1=ALU.add)
        up_ready.advance(F_GROUPS), silued.advance(2 * F_GROUPS), made.advance(2 * F_GROUPS)

    rope_2 = sb("rope_2", TILES, 2, ROT_RET + ROT_MOBA)

    def position_tables():
        n = ROT_RET + ROT_MOBA
        mem = Arena()
        inv, angle, turns, absolute = mem.take(n), mem.take(TILES, n), mem.take(TILES, n), mem.take(TILES, n)
        pos_f = mem.take(TILES)
        pos_i = sb("positions", TILES, dtype=I32)
        reduced = signal("angles_reduced")
        two_pi = 2 * np.pi
        c1 = 6.28125
        c2 = float(np.float32(np.round((two_pi - c1) * 2 ** 20) / 2 ** 20))
        c3 = float(np.float32(two_pi - c1 - c2))
        magic = 1.5 * 2 ** 23
        with nc.Block() as block:
            @block.sync
            def _(sp):
                load_params(sp, (pos_i[:, :], t["positions_2"][0].rearrange("(a p) -> p a", p=P)),
                            (inv, spread(t["c_inv_freq"])))
                stream.issue(sp)
        with nc.Block() as block:
            @block.vector
            def _(dve):
                params_ready(dve)
                dve_chain.link(dve, dve.tensor_copy(pos_f, pos_i[:, :]))
                for a in range(TILES):
                    last = dve.tensor_scalar(angle[:, a, :], inv, pos_f[:, a:a + 1], None, ALU.mult)
                dve_chain.link(dve, last)
                dve_chain.link(dve, dve.tensor_scalar(turns, angle, 1.0 / two_pi, magic, ALU.mult, ALU.add))
                dve_chain.link(dve, dve.tensor_scalar(turns, turns, -magic, None, ALU.add))
                for c in (c1, c2, c3):
                    dve_chain.link(dve, dve.scalar_tensor_tensor(out=angle, in0=turns, scalar=-c, in1=angle,
                                                                 op0=ALU.mult, op1=ALU.add))
                dve.tensor_scalar(angle, angle, 3.1415925, -3.1415925, ALU.min, ALU.max).then_inc(reduced.sem, 1)

            @block.scalar
            def _(act):
                act.wait_ge(reduced.sem, reduced.at(1))
                act_chain.link(act, act.activation(absolute, angle, ACT.Abs))
                act.activation(rope_2[:, :, 1, :], angle, ACT.Sin)
                act.activation(rope_2[:, :, 0, :], absolute, ACT.Sin, scale=-1.0, bias=float(np.pi / 2))
        reduced.advance(1)

    def second_mixer(layer):
        mem = Arena()
        z = mem.take(TILES, IN_2)
        decay = mem.take(RET_HEADS, TILES, SEQ)
        qk_cols = mem.take(4 * RW // P, SEQ)
        conv_pad = mem.take(2, KERNEL - 1 + SEQ)
        taps = mem.take(CONV_W)
        tap_cols = mem.take(2, KERNEL + 1)
        conv_norm = mem.take(2, 2)
        after = mem.at
        scratch = mem.take(TILES, 4, 2 * RET_HEADS * HD // 2)
        project(IN_2, z)
        o_rq, o_rk, o_rv, o_rg = 0, RW, 2 * RW, 3 * RW
        o_mq = 4 * RW
        o_mv = o_mq + 2 * MW
        o_ca, o_cg = o_mv + MW, o_mv + MW + CONV_W
        n_chunks = 4 * RW // P
        rotated, gated, turned = signal("heads_rotated"), signal("conv_gated"), signal("columns_turned")
        sig = signal("conv_gates_activated")
        starts = [o_rq + i * P for i in range(2 * RW // P)] + [o_mq + i * P for i in range(2 * MW // P)]
        taps_turned, padded = signal("taps_turned"), signal("conv_padding_cleared")
        with nc.Block() as block:
            @block.sync
            def _(sp):
                load_params(sp, (decay, t["c_decay"].rearrange("h a p q -> p h a q")),
                            (taps[0:KERNEL, :], t["conv_w_2"][layer]),
                            (taps[KERNEL:KERNEL + 1, :], t["conv_b_2"][layer:layer + 1, :]),
                            (conv_norm[:, 0, :], t["conv_ln_g_2"][layer].rearrange("(c p) -> p c", p=P)),
                            (conv_norm[:, 1, :], t["conv_ln_b_2"][layer].rearrange("(c p) -> p c", p=P)))
                stream.issue(sp)

            def heads_of(engine, chain, a):
                ret = z[:, a, o_rq:o_rq + 2 * RW].rearrange("p (h d) -> p h d", d=HD)
                moba = z[:, a, o_mq:o_mq + 2 * MW].rearrange("p (h d) -> p h d", d=HD)
                for view, f0, n in ((ret, 0, ROT_RET), (moba, ROT_RET, ROT_MOBA)):
                    nh = 2 * RET_HEADS
                    wide = [scratch[:, a, i, 0:nh * n].rearrange("p (h f) -> p h f", h=nh) for i in range(4)]
                    cos, sin = (rope_2[:, a, i:i + 1, f0:f0 + n].broadcast_to([P, nh, n]) for i in range(2))
                    last = rotate(engine, view[:, :, 0:n], view[:, :, n:2 * n], cos, sin, wide, chain)
                    if f0 == 0:
                        chain.link(engine, last)
                return last

            @block.scalar
            def _(act):
                act.activation(z[:, :, o_cg:o_cg + CONV_W], z[:, :, o_cg:o_cg + CONV_W],
                               ACT.Sigmoid).then_inc(sig.sem, 1)
                act.activation(z[:, :, o_rg:o_rg + RW], z[:, :, o_rg:o_rg + RW], ACT.Silu)
                act.wait_ge(taps_turned.sem, taps_turned.at(1))
                act.copy(tap_cols, ps[:, 7, 0:2 * (KERNEL + 1)].rearrange("p (c k) -> p c k", c=2))
                act.wait_ge(padded.sem, padded.at(1))
                for g in range(n_chunks // 2 + 1):
                    act.wait_ge(turned.sem, turned.at(g + 1))
                    src = ps[:, g, :].rearrange("p (c q) -> p c q", c=2)
                    dst = conv_pad[:, :, KERNEL - 1:] if g == 0 else qk_cols[:, 2 * g - 2:2 * g, :]
                    act.copy(dst, src)

            @block.vector
            def _(dve):
                heads_of(dve, dve_chain, 0).then_inc(rotated.sem, 1)

            @block.gpsimd
            def _(pool):
                pool.memset(conv_pad[:, :, 0:KERNEL - 1], 0.0).then_inc(padded.sem, 1)
                pool.wait_ge(sig.sem, sig.at(1))
                pool.tensor_tensor(z[:, :, o_ca:o_ca + CONV_W], z[:, :, o_ca:o_ca + CONV_W],
                                   z[:, :, o_cg:o_cg + CONV_W], ALU.mult).then_inc(gated.sem, 1)
                heads_of(pool, pool_chain, 1).then_inc(rotated.sem, 1)

            @block.tensor
            def _(pe):
                params_ready(pe)
                for c in range(2):
                    last = pe.transpose(ps[:, 7, c * (KERNEL + 1):(c + 1) * (KERNEL + 1)],
                                        taps[0:KERNEL + 1, c * P:(c + 1) * P], ident[0:KERNEL + 1, 0:KERNEL + 1])
                last.then_inc(taps_turned.sem, 1)
                pe.wait_ge(gated.sem, gated.at(1))
                for g in range(n_chunks // 2 + 1):
                    if g == 1:
                        pe.wait_ge(rotated.sem, rotated.at(2))
                    for i in range(2):
                        off = o_ca + i * P if g == 0 else starts[2 * g - 2 + i]
                        for a in range(TILES):
                            last = pe.transpose(ps[:, g, i * SEQ + a * P:i * SEQ + (a + 1) * P],
                                                z[:, a, off:off + P], ident[:, :])
                    last.then_inc(turned.sem, 1)
        rotated.advance(2), gated.advance(1), sig.advance(1), turned.advance(n_chunks // 2 + 1)
        taps_turned.advance(1), padded.advance(1)

        mem = Arena(after)
        s_buf = mem.take(2, TILES, SEQ)
        y = mem.take(TILES, RW)
        squares = mem.take(TILES, RW)
        sums, roots = stat[:, 0:TILES * RET_HEADS], stat[:, 16:16 + TILES * RET_HEADS]
        scores, decayed, outs, squared, summed, rooted, normed, mixed = (signal(s) for s in (
            "scores_ready", "scores_decayed", "outputs_ready", "squares_made", "squares_summed", "root_ready",
            "outputs_normed", "outputs_turned"))
        rc = RW // P
        with nc.Block() as block:
            @block.sync
            def _(sp):
                stream.issue(sp)

            @block.tensor
            def _(pe):
                def score(h):
                    half = slice(h % 2 * HD, h % 2 * HD + HD)
                    if h >= 2:
                        pe.wait_ge(decayed.sem, decayed.at(h - 1))
                    for b in range(TILES):
                        last = pe.matmul(ps[:, h % 2, b * SEQ + b * P:(b + 1) * SEQ],
                                         qk_cols[half, rc + h // 2, b * P:(b + 1) * P],
                                         qk_cols[half, h // 2, b * P:SEQ], start=True, stop=True)
                    last.then_inc(scores.sem, 1)

                def sum_values(h):
                    pe.wait_ge(decayed.sem, decayed.at(h + 1))
                    for a in range(TILES):
                        for b in range(a + 1):
                            last = pe.matmul(ps[:, 4 + a, h * HD:(h + 1) * HD], s_buf[:, h % 2, b, a * P:(a + 1) * P],
                                             z[:, b, o_rv + h * HD:o_rv + (h + 1) * HD], start=b == 0, stop=b == a)
                    last.then_inc(outs.sem, 1)

                for i in range(RET_HEADS + 1):
                    if i < RET_HEADS:
                        score(i)
                    if i >= 1:
                        sum_values(i - 1)
                pe.wait_ge(normed.sem, normed.at(1))
                for c in range(rc):
                    for a in range(TILES):
                        last = pe.transpose(ps[:, 2 + c // 2, c % 2 * SEQ + a * P:c % 2 * SEQ + (a + 1) * P],
                                            y[:, a, c * P:(c + 1) * P], ident[:, :])
                last.then_inc(mixed.sem, 1)

            @block.vector
            def _(dve):
                params_ready(dve)
                for h in range(RET_HEADS):
                    dve.wait_ge(scores.sem, scores.at(h + 1))
                    if h >= 2:
                        dve.wait_ge(outs.sem, outs.at(h - 1))
                    for b in range(TILES):
                        last = dve.tensor_tensor(s_buf[:, h % 2, b, b * P:], ps[:, h % 2, b * SEQ + b * P:(b + 1) * SEQ],
                                                 decay[:, h, b, b * P:], ALU.mult)
                    last.then_inc(decayed.sem, 1)
                dve.wait_ge(squared.sem, squared.at(1))
                dve.tensor_reduce(sums.rearrange("p (a h) -> p a h", a=TILES),
                                  squares.rearrange("p a (h d) -> p a h d", d=HD), AX, ALU.add).then_inc(summed.sem, 1)
                dve.wait_ge(rooted.sem, rooted.at(1))
                for a in range(TILES):
                    root = roots[:, a * RET_HEADS:(a + 1) * RET_HEADS].rearrange("p (h u) -> p h u", u=1)
                    last = dve.tensor_tensor(y[:, a, :].rearrange("p (h d) -> p h d", d=HD),
                                             ps[:, 4 + a, 0:RW].rearrange("p (h d) -> p h d", d=HD),
                                             root.broadcast_to([P, RET_HEADS, HD]), ALU.mult)
                dve_chain.link(dve, last)
                dve.tensor_tensor(y, y, z[:, :, o_rg:o_rg + RW], ALU.mult).then_inc(normed.sem, 1)

            @block.scalar
            def _(act):
                act.wait_ge(outs.sem, outs.at(RET_HEADS))
                act.activation(squares, ps[:, 4:4 + TILES, 0:RW], ACT.Square).then_inc(squared.sem, 1)
                act.wait_ge(mixed.sem, mixed.at(1))
                act.copy(mix_cols[:, 0:2, :], ps[:, 2, :].rearrange("p (c q) -> p c q", c=2))
                act.copy(mix_cols[:, 2, :], ps[:, 3, 0:SEQ])

            @block.gpsimd
            def _(pool):
                pool.wait_ge(summed.sem, summed.at(1))
                inverse_root(pool, roots, sums, HD).then_inc(rooted.sem, 1)
        scores.advance(RET_HEADS), decayed.advance(RET_HEADS), outs.advance(RET_HEADS)
        squared.advance(1), summed.advance(1), rooted.advance(1), normed.advance(1), mixed.advance(1)

        half = lambda i: slice(i % 2 * HD, i % 2 * HD + HD)
        attention(MOBA_HEADS, lambda i: qk_cols[half(i), 2 * rc + i // 2, :],
                  lambda i: qk_cols[half(i), 3 * rc + i // 2, :],
                  lambda i, b: z[:, b, o_mv + i * HD:o_mv + (i + 1) * HD], RET_HEADS, HD ** -0.5, True, Arena(after))

        mem = Arena(after)
        acc = mem.take(2, SEQ)
        centred = mem.take(2, SEQ)
        square = mem.take(2, SEQ)
        root = mem.take(2, SEQ)
        tapped, means, centre_ready, sq, variances, rooted, scaled = (signal(s) for s in (
            "taps_added", "means_ready", "centred_ready", "squares_made", "variances_ready", "root_ready",
            "tokens_scaled"))
        with nc.Block() as block:
            @block.sync
            def _(sp):
                stream.issue(sp)

            @block.vector
            def _(dve):
                for j in range(KERNEL):
                    for c in range(2):
                        if j > 0:
                            dve.wait_ge(tapped.sem, tapped.at(2 * j + c - 1))
                        window = conv_pad[:, c, j:j + SEQ]
                        if j == 0:
                            last = dve.tensor_scalar(acc[:, c, :], window, tap_cols[:, c, 0:1],
                                                     tap_cols[:, c, KERNEL:KERNEL + 1], ALU.mult, ALU.add)
                        else:
                            last = dve.scalar_tensor_tensor(out=acc[:, c, :], in0=window, scalar=tap_cols[:, c, j:j + 1],
                                                            in1=acc[:, c, :], op0=ALU.mult, op1=ALU.add)
                        last.then_inc(tapped.sem, 1)
                dve.wait_ge(means.sem, means.at(1))
                dve.tensor_tensor(centred, acc, ps[:, 0, :].rearrange("p (c q) -> p c q", c=2),
                                  ALU.subtract).then_inc(centre_ready.sem, 1)
                dve.wait_ge(rooted.sem, rooted.at(1))
                dve.wait_ge(centre_ready.sem, centre_ready.at(1))
                dve_chain.link(dve, dve.reciprocal(root, root))
                dve.tensor_tensor(centred, centred, root, ALU.mult).then_inc(scaled.sem, 1)

            @block.tensor
            def _(pe):
                params_ready(pe)
                pe.wait_ge(tapped.sem, tapped.at(2 * KERNEL))
                pe.matmul(ps[:, 0, :], group_mean[:, :], acc.rearrange("p c q -> p (c q)"), start=True,
                          stop=True).then_inc(means.sem, 1)
                pe.wait_ge(sq.sem, sq.at(1))
                pe.matmul(ps[:, 1, :], group_mean[:, :], square.rearrange("p c q -> p (c q)"), start=True,
                          stop=True).then_inc(variances.sem, 1)

            @block.scalar
            def _(act):
                params_ready(act)
                act.wait_ge(centre_ready.sem, centre_ready.at(1))
                act.activation(square, centred, ACT.Square).then_inc(sq.sem, 1)
                act.wait_ge(variances.sem, variances.at(1))
                act.activation(root, ps[:, 1, :].rearrange("p (c q) -> p c q", c=2), ACT.Sqrt,
                               bias=EPS).then_inc(rooted.sem, 1)
                act.wait_ge(scaled.sem, scaled.at(1))
                for c in range(2):
                    act.activation(mix_cols[:, 2 * rc + c, :], centred[:, c, :], ACT.Silu,
                                   scale=conv_norm[:, 0, c:c + 1], bias=conv_norm[:, 1, c:c + 1])
        tapped.advance(2 * KERNEL)
        for s in (means, centre_ready, sq, variances, rooted, scaled):
            s.advance(1)

        first = stream.take(2)
        ready = signal("projected")
        with nc.Block() as block:
            @block.sync
            def _(sp):
                stream.issue(sp)

            @block.tensor
            def _(pe):
                output_products(pe, first, ready)

            @block.vector
            def _(dve):
                for h in range(2):
                    for a in range(TILES):
                        output_ready(dve, first, ready, h, a)
                        cols = slice(h * BANK, (h + 1) * BANK)
                        dve.tensor_tensor(x[:, a, cols], x[:, a, cols], ps[:, 2 * h + a, :], ALU.add)
        ready.advance(2)

    def final_norm():
        normed = Arena().take(TILES, D)
        sums, roots = stat[:, 0:TILES], stat[:, TILES:2 * TILES]
        squares, rooted, done, stored = (signal(s) for s in ("squares_summed", "root_ready", "tokens_scaled",
                                                            "output_stored"))
        with nc.Block() as block:
            @block.sync
            def _(sp):
                load_params(sp, (ln_params[:, 0, :], spread(t["final_norm_2"])))
                for a in range(TILES):
                    sp.wait_ge(done.sem, done.at(a + 1))
                    sp.dma_start(out[0, a * P:(a + 1) * P, :], normed[:, a, :]).then_inc(stored.sem, 16)
                sp.wait_ge(stored.sem, 16 * TILES)

            @block.scalar
            def _(act):
                for a in range(TILES):
                    last = act.activation(normed[:, a, :], x[:, a, :], ACT.Square, accum_out=sums[:, a:a + 1])
                last.then_inc(squares.sem, 1)

            @block.gpsimd
            def _(pool):
                pool.wait_ge(squares.sem, squares.at(1))
                inverse_root(pool, roots, sums, D).then_inc(rooted.sem, 1)

            @block.vector
            def _(dve):
                params_ready(dve)
                dve.wait_ge(rooted.sem, rooted.at(1))
                for a in range(TILES):
                    dve.scalar_tensor_tensor(out=normed[:, a, :], in0=x[:, a, :], scalar=roots[:, a:a + 1],
                                             in1=ln_params[:, 0, :], op0=ALU.mult, op1=ALU.mult).then_inc(done.sem, 1)

    h, base = even_mixer()
    gla(h, base)
    mix_out_norm()
    experts(0)
    odd_mixer()
    mix_out_norm()
    experts(1)
    position_tables()
    for layer in range(DEPTH):
        rms_columns(t["ffn1_norm_2"][layer])
        ffn()
        rms_columns(t["mix_norm_2"][layer])
        second_mixer(layer)
        rms_columns(t["ffn2_norm_2"][layer])
        ffn()
    final_norm()


INPUTS = ["x", "p", "w_in_even", "mla_q_norm", "w_uq", "mla_kv_norm", "w_ukv", "gla_gate_w_fwd", "gla_gate_b_fwd",
          "gla_gate_w_bwd", "gla_gate_b_bwd", "gla_norm", "w_in_odd", "gqa_q_norm", "gqa_k_norm", "w_o", "ln1_g",
          "ln1_b", "router_w", "w1", "w3", "w2", "ple_gate_w", "ple_gate_b", "ple_w", "ln2_g", "ln2_b",
          "positions_2", "ffn1_norm_2", "ffn1_wg_2", "ffn1_wu_2", "ffn1_wd_2", "mix_norm_2", "w_in_2", "conv_w_2",
          "conv_b_2", "conv_ln_g_2", "conv_ln_b_2", "w_out_2", "ffn2_norm_2", "ffn2_wg_2", "ffn2_wu_2", "ffn2_wd_2",
          "final_norm_2"]


def kernel(**inputs):
    import concourse.bacc as bacc
    from concourse.bass_utils import run_bass_kernel_spmd

    nc = bacc.Bacc("TRN2", target_bir_lowering=False, num_devices=1)
    arrays = {name: np.ascontiguousarray(inputs[name]) for name in INPUTS}
    arrays.update(shape_constants())
    tensors = {name: nc.dram_tensor(f"in_{name}", a.shape, mybir.dt.from_np(a.dtype), kind="ExternalInput").ap()
               for name, a in arrays.items()}
    out = nc.dram_tensor("out", (1, SEQ, D), F32, kind="ExternalOutput").ap()
    build_program(nc, tensors, out)
    result = run_bass_kernel_spmd(nc, [{f"in_{name}": a for name, a in arrays.items()}], core_ids=[0])
    return result.results[0]["out"]
```

```python
import concourse.bass as bass
import concourse.mybir as mybir
import numpy as np
from concourse.alu_op_type import AluOpType as ALU

F32 = mybir.dt.float32
BF16 = mybir.dt.bfloat16
I32 = mybir.dt.int32
F32R = mybir.dt.float32r
ACT = mybir.ActivationFunctionType
AX = mybir.AxisListType.X

P = 128
SEQ = 256
TILES = SEQ // P
D = 1024
DC = D // P
DEPTH = 2
EPS = 1e-6
ALPHA = (2.0 * DEPTH) ** 0.25
BANK = 512

Q_LORA, KV_LORA, ROPE_A = 256, 128, 32
MLA_HEADS, NOPE, V_DIM = 8, 64, 64
MLA_QK = NOPE + ROPE_A
GLA_HEADS, DK, DV, RANK, CHUNK = 4, 64, 128, 16, 64
N_CHUNKS = SEQ // CHUNK
GATE_NORM = 16.0
O_CQ = 0
O_CKV = O_CQ + Q_LORA
O_KPE = O_CKV + KV_LORA
O_GQ = O_KPE + ROPE_A
O_GK = O_GQ + GLA_HEADS * DK
O_GV = O_GK + GLA_HEADS * DK
O_LR = O_GV + GLA_HEADS * DV
O_GR = O_LR + 2 * RANK
EVEN_IN = O_GR + GLA_HEADS * DV
GQA_HEADS, KV_HEADS, HD = 16, 4, 64
ODD_IN = (GQA_HEADS + 2 * KV_HEADS) * HD
EXPERTS, FF, PLE_DIM = 16, 1024, 256
CAP = 2 * SEQ // EXPERTS
QUADS = 4
QW = FF // QUADS
RET_HEADS, MOBA_HEADS, CONV_W, KERNEL = 6, 6, 256, 31
RW, MW = RET_HEADS * HD, MOBA_HEADS * HD
IN_2 = 4 * RW + 3 * MW + 2 * CONV_W
D_FF = 2816
FG = 256
F_GROUPS = D_FF // FG
ROT_RET, ROT_MOBA = HD // 2, HD // 8

WEIGHT_SLOTS, SLOT = 6, 4096


def axial_tables(rot_dim):
    row = np.repeat(np.arange(SEQ // 64, dtype=np.float32), 64)
    col = np.tile(np.arange(64, dtype=np.float32), SEQ // 64)
    half = rot_dim // 2
    inv = (np.float32(10000.0) ** (-np.arange(0, half, 2, dtype=np.float32) / half)).astype(np.float32)
    ang = np.concatenate([row[:, None] * inv, col[:, None] * inv], axis=-1)
    return np.stack([np.cos(ang), np.sin(ang)], axis=1).astype(np.float32)


def shape_constants():
    m, l = np.arange(P)[:, None], np.arange(P)[None, :]
    same = (m // CHUNK) == (l // CHUNK)
    tri = np.stack([same & (m <= l), same & (m >= l), same & (m > l), same & (m < l)], axis=1)
    heads = np.arange(RET_HEADS, dtype=np.float32)
    log_gamma = np.log1p(-np.exp2(-5.0 - heads)).astype(np.float32)
    km, qc = np.arange(SEQ)[:, None], np.arange(SEQ)[None, :]
    rel = (qc - km).astype(np.float32)
    decay = np.where(rel >= 0, np.exp(log_gamma[:, None, None] * np.maximum(rel, 0.0)), 0.0) * HD ** -0.5
    ret_inv = np.float32(10000.0) ** (-np.linspace(0.0, 1.0, ROT_RET, dtype=np.float32))
    moba_inv = np.float32(500000.0) ** (-np.arange(ROT_MOBA, dtype=np.float32) / ROT_MOBA)
    f = np.float32
    return {
        "c_ident": np.eye(P, dtype=f),
        "c_chunk_masks": tri.astype(f),
        "c_rope_mla": axial_tables(ROPE_A),
        "c_rope_gqa": axial_tables(HD),
        "c_slots": np.arange(1, CAP + 1, dtype=f)[None, :],
        "c_causal": np.where(l <= m, 0.0, -1e30).astype(f),
        "c_decay": decay.astype(f).reshape(RET_HEADS, TILES, P, SEQ),
        "c_inv_freq": np.concatenate([ret_inv, moba_inv]).astype(f)[None, :],
        "c_group_mean": (((m // HD) == (l // HD)) / HD).astype(f),
    }


class Signal:

    def __init__(self, nc, name):
        self.sem = nc.alloc_semaphore(name)
        self.base = 0

    def at(self, n):
        return self.base + n

    def advance(self, n):
        self.base += n


class Chain:

    def __init__(self, nc, name):
        self.sem = nc.alloc_semaphore(name)
        self.steps = 0

    def link(self, engine, instruction):
        self.steps += 1
        instruction.then_inc(self.sem, 1)
        engine.wait_ge(self.sem, self.steps)


class WeightStream:

    def __init__(self, nc, ring):
        self.ring = ring
        self.arrived = [nc.alloc_semaphore(f"weights_arrived_{s}") for s in range(WEIGHT_SLOTS)]
        self.used = nc.alloc_semaphore("weights_used")
        self.units, self.value = [], []
        self.total = [0] * WEIGHT_SLOTS
        self.issued = self.taken = 0

    def add(self, loads, index, n_loads=1):
        slot = len(self.units) % WEIGHT_SLOTS
        self.total[slot] += 16 * n_loads
        self.units.append((loads, index))
        self.value.append(self.total[slot])

    def take(self, n):
        self.taken += n
        return self.taken - n

    def slot(self, u):
        return self.ring[:, u % WEIGHT_SLOTS, :]

    def load(self, sp, u, index):
        for dst, src in self.units[u][0](self.slot(u), index):
            sp.dma_start(dst, src).then_inc(self.arrived[u % WEIGHT_SLOTS], 16)

    def issue(self, sp):
        for u in range(self.issued, min(self.taken + WEIGHT_SLOTS, len(self.units))):
            if u >= WEIGHT_SLOTS:
                sp.wait_ge(self.used, u - WEIGHT_SLOTS + 1)
            self.load(sp, u, self.units[u][1])
            self.issued = u + 1

    def wait(self, pe, u):
        pe.wait_ge(self.arrived[u % WEIGHT_SLOTS], self.value[u])


def columns_of(w, n0, width):
    return w[:, n0:n0 + width].rearrange("(c p) n -> p c n", p=P)


def plan_weights(nc, stream, t):

    def matrix(w, n, leading=0):
        widths = [min(BANK, n - n0) for n0 in range(0, n, BANK)]
        for i, width in enumerate(widths):
            n0 = i * BANK - leading if i * BANK >= leading else n - leading + i * BANK

            def loads(slot, n0, width=width, w=w):
                rows = w.shape[0] // P
                dst = slot[:, 0:rows * width].rearrange("p (c n) -> p c n", c=rows)
                return [(dst, columns_of(w, n0, width))]

            stream.add(loads, n0)

    def up_projections(slot, _):
        uq = slot[:, 0:2 * MLA_HEADS * MLA_QK].rearrange("p (c n) -> p c n", c=2)
        ukv = slot[:, 2 * MLA_HEADS * MLA_QK:2 * MLA_HEADS * MLA_QK + D]
        return [(uq, t["w_uq"][0].rearrange("(c p) n -> p c n", p=P)), (ukv, t["w_ukv"][0])]

    def ple_projection(slot, layer):
        return [(slot[:, 0:2 * D].rearrange("p (c n) -> p c n", c=2),
                 t["ple_w"][layer].rearrange("(c p) n -> p c n", p=P))]

    def experts(layer):
        def half(name, which, by_rows):
            def loads(slot, e):
                w = t[name][layer, bass.ds(e, 1)].rearrange("e (c p) f -> p (e c) f", p=P)
                if by_rows:
                    c0 = which * DC // 2
                    return [(slot.rearrange("p (c f) -> p c f", c=DC // 2), w[:, c0:c0 + DC // 2, :])]
                return [(slot.rearrange("p (c f) -> p c f", c=DC), w[:, :, which * BANK:(which + 1) * BANK])]
            return loads

        parts = [half("w1", 0, True), half("w1", 1, True), half("w3", 0, True), half("w3", 1, True),
                 half("w2", 0, False), half("w2", 1, False)]
        for e in range(EXPERTS):
            for part in parts:
                stream.add(part, e)

    def ffn(which, layer):
        wg, wu, wd = (t[f"ffn{which}_{k}_2"] for k in ("wg", "wu", "wd"))

        def up(slot, f0):
            halves = slot.rearrange("p (h c f) -> p h c f", h=2, c=DC)
            return [(halves[:, h], w[layer, :, bass.ds(f0, FG)].rearrange("(c p) f -> p c f", p=P))
                    for h, w in enumerate((wg, wu))]

        def down(slot, f0):
            return [(slot[:, 0:2 * D].rearrange("p (c n) -> p c n", c=2),
                     wd[layer, bass.ds(f0, FG), :].rearrange("(c p) n -> p c n", p=P))]

        for i in range(F_GROUPS):
            stream.add(up, i * FG, 2)
            stream.add(down, i * FG)

    for layer in range(DEPTH):
        if layer % 2 == 0:
            matrix(t["w_in_even"][0], EVEN_IN)
            stream.add(up_projections, 0, 2)
        else:
            matrix(t["w_in_odd"][0], ODD_IN)
        matrix(t["w_o"][layer], D)
        matrix(t["ple_gate_w"][layer], D)
        stream.add(ple_projection, layer)
        experts(layer)
    for layer in range(DEPTH):
        ffn(1, layer)
        matrix(t["w_in_2"][layer], IN_2, 2 * CONV_W)
        matrix(t["w_out_2"][layer], D)
        ffn(2, layer)


def build_program(nc, t, out):
    address = {}

    def sb(name, *dims, dtype=F32):
        made = nc.alloc_sbuf_tensor(name, [P, *dims], dtype)
        address[name] = nc.sbuf_base - int(np.prod(dims)) * (2 if dtype == BF16 else 4)
        return made

    ring = sb("weight_ring", WEIGHT_SLOTS, SLOT)
    x = sb("x", TILES, D)
    x_cols = sb("x_cols", DC, SEQ)
    mix_cols = sb("mix_cols", DC, SEQ)
    ln_params = sb("ln_params", 2, D)
    ident = sb("ident", P)
    chunk_masks = sb("chunk_masks", 4, P)
    rope_mla = sb("rope_mla", TILES, 2, ROPE_A // 2)
    rope_gqa = sb("rope_gqa", TILES, 2, HD // 2)
    causal = sb("causal", P)
    group_mean = sb("group_mean", P)
    ones_row = sb("ones_row", P)
    zeros_bf = sb("zeros_bf", BANK, dtype=BF16)
    half_power = sb("half_power", 64)
    norm_cols = sb("norm_cols", DC)
    stat = sb("stat", 256)
    arena_size = 18300
    arena = sb("arena", arena_size)

    def over(name, below, word, *dims):
        return nc.alloc_sbuf_tensor_at(name, [P, *dims], F32R, offset=address[below] + 4 * word)

    HALF = DC // 2 * BANK
    PARTS_AT, GATE_LOW_AT = (arena_size - 4 * HALF) // 8 * 8, (arena_size - DC * SEQ) // 8 * 8

    x_hi, x_lo = over("x_hi", "x_cols", 0, DC, SEQ), over("x_lo", "mix_cols", 0, DC, SEQ)
    gate_parts = over("gate_hi", "mix_cols", 0, DC, SEQ), over("gate_lo", "arena", GATE_LOW_AT, DC, SEQ)
    mix_lo = over("mix_lo", "arena", 4096, DC, SEQ)
    w_parts, gate_w_parts = (tuple(over(f"{name}_{part}", "arena", at + i * 2 * HALF, 2, HALF)
                                   for i, part in enumerate(("hi", "lo")))
                             for name, at in (("w", PARTS_AT), ("gate_w", 0)))
    up_hi, up_lo = over("up_hi", "arena", 0, 2, 2, DC, P), over("up_lo", "arena", 4096, 2, 2, DC, P)
    down_hi, down_lo = over("down_hi", "arena", 8192, 2, D), over("down_lo", "arena", 10240, 2, D)
    hid_hi, hid_lo = over("hid_hi", "arena", 12288, 2, SEQ), over("hid_lo", "arena", 12800, 2, SEQ)
    ps = nc.alloc_psum_tensor("psum", [P, 8, BANK], F32)

    signals = {}

    def signal(name):
        if name not in signals:
            signals[name] = Signal(nc, name)
        return signals[name]

    dve_chain, act_chain, pool_chain = (Chain(nc, n) for n in ("dve_chain", "act_chain", "pool_chain"))
    stream = WeightStream(nc, ring)
    plan_weights(nc, stream, t)
    params = signal("params_loaded")
    setup_loaded = signal("setup_loaded")
    params_count = [0]

    class Arena:

        def __init__(self, at=0):
            self.at = at

        def take(self, *dims):
            n = int(np.prod(dims))
            assert self.at + n <= arena_size, (self.at, n)
            flat = arena[:, self.at:self.at + n]
            self.at += n
            if len(dims) == 1:
                return flat
            names = "abcd"[:len(dims)]
            spec = f"p ({' '.join(names)}) -> p {' '.join(names)}"
            return flat.rearrange(spec, **dict(zip(names[1:], dims[1:])))

    def load_params(sp, *pairs):
        for dst, src in pairs:
            sp.dma_start(dst, src, allow_slow_non_contiguous=True).then_inc(params.sem, 16)
            params_count[0] += 16

    def setup_ready(engine):
        engine.wait_ge(setup_loaded.sem, 32)

    def params_ready(engine):
        engine.wait_ge(params.sem, params_count[0])

    def spread(row):
        return row.partition_broadcast(P) if len(row.shape) == 1 else row.broadcast_to([P, row.shape[-1]])

    with nc.Block() as block:
        @block.sync
        def _(sp):
            sp.dma_start(x[:, :, :], t["x"][0].rearrange("(a p) d -> p a d", p=P)).then_inc(setup_loaded.sem, 16)
            sp.dma_start(ident[:, :], t["c_ident"]).then_inc(setup_loaded.sem, 16)
            load_params(
                sp,
                (chunk_masks[:, :, :], t["c_chunk_masks"]),
                (rope_mla[:, :, :, :], t["c_rope_mla"].rearrange("(a p) k f -> p a k f", p=P)),
                (rope_gqa[:, :, :, :], t["c_rope_gqa"].rearrange("(a p) k f -> p a k f", p=P)),
                (causal[:, :], t["c_causal"]),
                (group_mean[:, :], t["c_group_mean"]),
            )
            stream.issue(sp)

        @block.gpsimd
        def _(pool):
            pool.memset(ones_row[:, :], 1.0)
            pool.memset(zeros_bf[:, :], 0.0)
            pool.memset(half_power[:, :], -0.5)

    def to_columns(src, high, low, full=None, gain=None, more_params=()):
        turned, kept = signal("columns_turned"), signal("columns_high_kept")
        with nc.Block() as block:
            @block.sync
            def _(sp):
                stream.issue(sp)
                load_params(sp, *more_params)

            @block.tensor
            def _(pe):
                setup_ready(pe)
                for c in range(DC):
                    for a in range(TILES):
                        last = pe.transpose(ps[:, c // 2, (c % 2) * SEQ + a * P:(c % 2) * SEQ + (a + 1) * P],
                                            src[:, a, c * P:(c + 1) * P], ident[:, :])
                    if c % 2:
                        last.then_inc(turned.sem, 1)

            @block.scalar
            def _(act):
                if gain is not None:
                    params_ready(act)
                for b in range(DC // 2):
                    act.wait_ge(turned.sem, turned.at(b + 1))
                    if gain is None:
                        last = act.copy(high[:, 2 * b:2 * b + 2, :], ps[:, b, :].rearrange("p (c q) -> p c q", c=2))
                    else:
                        for c in (2 * b, 2 * b + 1):
                            last = act.activation(high[:, c, :], ps[:, b, c % 2 * SEQ:c % 2 * SEQ + SEQ], ACT.Copy,
                                                  scale=gain[:, c:c + 1])
                    last.then_inc(kept.sem, 1)

            @block.vector
            def _(dve):
                for b in range(DC // 2):
                    dve.wait_ge(kept.sem, kept.at(b + 1))
                    both = slice(2 * b, 2 * b + 2)
                    bank = ps[:, b, :].rearrange("p (c q) -> p c q", c=2)
                    if gain is None:
                        dve.tensor_tensor(low[:, both, :], bank, high[:, both, :].bitcast(F32), ALU.subtract)
                    else:
                        for c in (2 * b, 2 * b + 1):
                            dve.scalar_tensor_tensor(out=low[:, c, :], in0=ps[:, b, c % 2 * SEQ:c % 2 * SEQ + SEQ],
                                                     scalar=gain[:, c:c + 1], in1=high[:, c, :].bitcast(F32),
                                                     op0=ALU.mult, op1=ALU.subtract)
                    if full is not None:
                        dve.tensor_copy(full[:, both, :], bank)
        turned.advance(DC // 2), kept.advance(DC // 2)

    class PartedProducts:

        def __init__(self, first, n, x_high, x_low, banks, parts=w_parts, freed=None,
                     bias=None):
            self.first, self.n, self.x_high, self.x_low, self.banks, self.freed = first, n, x_high, x_low, banks, freed
            self.w_hi, self.w_lo = parts
            self.bias = bias
            self.units = -(-n // BANK)
            self.high, self.low, self.done = (signal(s) for s in ("weights_high_kept", "weights_low_kept",
                                                                  "half_products_done"))

        def width(self, i):
            return min(BANK, self.n - i * BANK)

        def raw(self, i, half):
            n = DC // 2 * self.width(i)
            return stream.slot(self.first + i)[:, half * n:(half + 1) * n]

        def part_high(self, act, i, half):
            k = 2 * i + half
            if half == 0:
                stream.wait(act, self.first + i)
            if k >= 2:
                act.wait_ge(self.done.sem, self.done.at(k - 1))
            src = self.raw(i, half)
            act.copy(self.w_hi[:, half, 0:src.shape[-1]], src).then_inc(self.high.sem, 1)

        def part_low(self, dve, i, half):
            src = self.raw(i, half)
            dve.wait_ge(self.high.sem, self.high.at(2 * i + half + 1))
            dve.tensor_tensor(self.w_lo[:, half, 0:src.shape[-1]], src, self.w_hi[:, half, 0:src.shape[-1]].bitcast(F32),
                              ALU.subtract).then_inc(self.low.sem if half == 0 else stream.used, 1)

        def products(self, pe, i, only=None):
            width = self.width(i)
            for half in (range(2) if only is None else (only,)):
                if half == 0:
                    pe.wait_ge(self.low.sem, self.low.at(i + 1))
                else:
                    pe.wait_ge(stream.used, self.first + i + 1)
                parts = [w[:, half, 0:DC // 2 * width].rearrange("p (c n) -> p c n", c=DC // 2) for w in
                         (self.w_hi, self.w_lo)]
                for a in range(TILES):
                    k = TILES * i + a
                    if self.freed is not None and half == 0 and k >= len(self.banks):
                        pe.wait_ge(self.freed.sem, self.freed.at(k - len(self.banks) + 1))
                    if self.bias is not None and half == 0:
                        pe.matmul(ps[:, self.banks[k % len(self.banks)], 0:width], ones_row[0:1, :],
                                  self.bias[0:1, i * BANK:i * BANK + width], start=True, stop=False)
                    for c in range(DC // 2):
                        cc = half * DC // 2 + c
                        for x_part, w_part in ((self.x_high, 0), (self.x_high, 1), (self.x_low, 0)):
                            last = pe.matmul(ps[:, self.banks[k % len(self.banks)], 0:width],
                                             x_part[:, cc, a * P:(a + 1) * P], parts[w_part][:, c, :],
                                             start=self.bias is None and cc == 0 and (x_part, w_part) == (self.x_high, 0),
                                             stop=cc == DC - 1 and x_part is self.x_low)
                last.then_inc(self.done.sem, 1)

        def wait(self, engine, i):
            engine.wait_ge(self.done.sem, self.done.at(2 * i + 2))

        def close(self):
            self.high.advance(2 * self.units), self.low.advance(self.units), self.done.advance(2 * self.units)

    def project(n, dst, leading=0, banks=range(8), extra=None, activated=None,
                more_params=()):
        freed = signal("projection_kept")
        units = -(-n // BANK)
        job = PartedProducts(stream.take(units), n, x_hi, x_lo, banks, freed=freed)
        extra, activated = extra or {}, activated or {}
        nothing = lambda engine, k: None
        with nc.Block() as block:
            @block.sync
            def _(sp):
                load_params(sp, *more_params)
                stream.issue(sp)

            @block.tensor
            def _(pe):
                for k in range(2 * units):
                    job.products(pe, k // 2, k % 2)
                    extra.get("tensor", nothing)(pe, k)

            @block.scalar
            def _(act):
                def keep(i):
                    job.wait(act, i)
                    n0 = i * BANK - leading if i * BANK >= leading else n - leading + i * BANK
                    for a in range(TILES):
                        bank = ps[:, banks[(TILES * i + a) % len(banks)], 0:job.width(i)]
                        split, function = activated.get(n0, (0, None))
                        if function is None:
                            last = act.copy(dst[:, a, n0:n0 + job.width(i)], bank)
                        else:
                            act.copy(dst[:, a, n0:n0 + split], bank[:, 0:split])
                            last = act.activation(dst[:, a, n0 + split:n0 + job.width(i)], bank[:, split:], function)
                        last.then_inc(freed.sem, 1)

                for k in range(2 * units):
                    if k % 2 and k > 1:
                        keep(k // 2 - 1)
                    job.part_high(act, k // 2, k % 2)
                    extra.get("scalar", nothing)(act, k)
                keep(units - 1)

            @block.vector
            def _(dve):
                for k in range(2 * units):
                    job.part_low(dve, k // 2, k % 2)
                    extra.get("vector", nothing)(dve, k)

            if "gpsimd" in extra:
                @block.gpsimd
                def _(pool):
                    extra["gpsimd"](pool)
        job.close()
        freed.advance(units * TILES)

    def inverse_root(pool, dst, sums, count):
        n = dst.shape[-1]
        pool_chain.link(pool, pool.tensor_scalar(dst, sums, 1.0 / count, EPS, ALU.mult, ALU.add))
        return pool.tensor_tensor(dst, dst, half_power[:, 0:n], ALU.pow)

    def rotate(engine, first, second, cos, sin, scratch, chain=dve_chain):
        fs, sc, fc, ss = scratch
        engine.tensor_tensor(fc, first, cos, ALU.mult)
        engine.tensor_tensor(ss, second, sin, ALU.mult)
        engine.tensor_tensor(fs, first, sin, ALU.mult)
        chain.link(engine, engine.tensor_tensor(sc, second, cos, ALU.mult))
        engine.tensor_tensor(first, fc, ss, ALU.subtract)
        return engine.tensor_tensor(second, fs, sc, ALU.add)

    def norm_stats(dve, y, stats, h, a):
        return dve.bn_stats(stats[:, a, 6 * h:6 * h + 6], y[:, a, h * BANK:(h + 1) * BANK])

    def layer_norm_steps(dve, y, stats, wanted, got, centred):
        for a in range(TILES):
            last = dve.bn_aggr(stats[:, a, 12:14], stats[:, a, 0:12])
        last.then_inc(wanted.sem, 1)
        dve.wait_ge(wanted.sem, wanted.at(1))
        dve.wait_ge(got.sem, got.at(1))
        dve_chain.link(dve, dve.tensor_scalar(y[:, 0, :], y[:, 0, :], stats[:, 0, 12:13], stats[:, 0, 14:15],
                                              ALU.subtract, ALU.mult))
        for a in range(TILES):
            if a == 1:
                dve.wait_ge(centred.sem, centred.at(1))
            dve_chain.link(dve, dve.tensor_tensor(y[:, a, :], y[:, a, :], ln_params[:, 0, :], ALU.mult))
            dve.tensor_tensor(x[:, a, :], y[:, a, :], ln_params[:, 1, :], ALU.add)

    def layer_norm_root(pool, stats, wanted, got):
        pool.wait_ge(wanted.sem, wanted.at(1))
        root = stats[:, :, 14:15]
        pool_chain.link(pool, pool.tensor_scalar(root, stats[:, :, 13:14], 1.0, EPS, ALU.mult, ALU.add))
        pool_chain.link(pool, pool.tensor_tensor(root, root, half_power[:, 0:TILES].rearrange(
            "p (a u) -> p a u", u=1), ALU.pow))
        pool_chain.link(pool, pool.tensor_tensor(stats[:, :, 15:16], root, stats[:, :, 12:13], ALU.mult))
        pool.tensor_scalar(stats[:, :, 15:16], stats[:, :, 15:16], -1.0, None, ALU.mult).then_inc(got.sem, 1)

    def layer_norm_centre(act, y, stats, got, centred):
        act.wait_ge(got.sem, got.at(1))
        act.activation(y[:, 1, :], y[:, 1, :], ACT.Identity, scale=stats[:, 1, 14:15],
                       bias=stats[:, 1, 15:16]).then_inc(centred.sem, 1)

    def mix_products(high, job):
        def act_side(act):
            for g in range(2):
                act.copy(x_hi[:, 4 * g:4 * g + 4, :], mix_cols[:, 4 * g:4 * g + 4, :]).then_inc(high.sem, 1)
                job.part_high(act, 0, g)
            for g in range(2):
                job.part_high(act, 1, g)

        def dve_side(dve):
            for g in range(2):
                dve.wait_ge(high.sem, high.at(g + 1))
                dve.tensor_tensor(mix_lo[:, 4 * g:4 * g + 4, :], mix_cols[:, 4 * g:4 * g + 4, :],
                                  x_hi[:, 4 * g:4 * g + 4, :].bitcast(F32), ALU.subtract)
                job.part_low(dve, 0, g)
            for g in range(2):
                job.part_low(dve, 1, g)

        return act_side, dve_side

    def mix_out_norm():
        high, wanted, got, centred = (signal(s) for s in ("mix_high_kept", "root_wanted", "root_ready",
                                                          "tile_centred"))
        job = PartedProducts(stream.take(2), D, x_hi, mix_lo, range(4))
        act_side, dve_side = mix_products(high, job)
        y = Arena().take(TILES, D)
        stats = stat[:, 0:32].rearrange("p (a k) -> p a k", a=TILES)
        with nc.Block() as block:
            @block.sync
            def _(sp):
                stream.issue(sp)

            @block.tensor
            def _(pe):
                job.products(pe, 0), job.products(pe, 1)

            @block.scalar
            def _(act):
                act_side(act)
                layer_norm_centre(act, y, stats, got, centred)

            @block.vector
            def _(dve):
                dve_side(dve)
                params_ready(dve)
                for h in range(2):
                    job.wait(dve, h)
                    cols = slice(h * BANK, (h + 1) * BANK)
                    for a in range(TILES):
                        last = dve.scalar_tensor_tensor(out=y[:, a, cols], in0=x[:, a, cols], scalar=ALPHA,
                                                        in1=ps[:, 2 * h + a, :], op0=ALU.mult, op1=ALU.add)
                    dve_chain.link(dve, last)
                    for a in range(TILES):
                        last = norm_stats(dve, y, stats, h, a)
                dve_chain.link(dve, last)
                layer_norm_steps(dve, y, stats, wanted, got, centred)

            @block.gpsimd
            def _(pool):
                layer_norm_root(pool, stats, wanted, got)
        job.close()
        high.advance(2), wanted.advance(1), got.advance(1), centred.advance(1)

    def attention(heads, q_of, k_of, v_of, mix_head, scale, masked, mem):
        deep = 4
        scores, norm, turned, kept, summed, stored = (signal(s) for s in (
            "scores_ready", "probs_ready", "probs_turned", "turned_kept", "values_summed", "values_kept"))
        peak, expd = signal("peaks_ready"), signal("exps_ready")
        e_buf = mem.take(deep, TILES, SEQ)
        pt_buf = mem.take(2, TILES, SEQ)
        small = mem.take(deep, TILES, 4)

        def keys(a):
            return (a + 1) * P if masked else SEQ

        with nc.Block() as block:
            @block.sync
            def _(sp):
                stream.issue(sp)

            @block.tensor
            def _(pe):
                def score(h):
                    if h >= deep:
                        pe.wait_ge(expd.sem, expd.at(TILES * (h - deep + 1)))
                    for a in range(TILES):
                        last = pe.matmul(ps[:, h % deep, a * SEQ:a * SEQ + keys(a)], q_of(h)[:, a * P:(a + 1) * P],
                                         k_of(h)[:, 0:keys(a)], start=True, stop=True)
                    last.then_inc(scores.sem, 1)

                def turn(h):
                    pe.wait_ge(norm.sem, norm.at(h + 1))
                    if h >= 2:
                        pe.wait_ge(kept.sem, kept.at(h - 1))
                    for b in range(TILES):
                        for a in range(b if masked else 0, TILES):
                            last = pe.transpose(ps[:, deep + h % 2, b * SEQ + a * P:b * SEQ + (a + 1) * P],
                                                e_buf[:, h % deep, a, b * P:(b + 1) * P], ident[:, :])
                    last.then_inc(turned.sem, 1)

                def sum_values(h):
                    pe.wait_ge(kept.sem, kept.at(h + 1))
                    if h >= 4:
                        pe.wait_ge(stored.sem, stored.at(h // 2 - 1))
                    half = slice((h % 2) * HD, (h % 2) * HD + HD)
                    for b in range(TILES):
                        lo = b * P if masked else 0
                        last = pe.matmul(ps[half, 6 + h // 2 % 2, lo:SEQ], v_of(h, b),
                                         pt_buf[:, h % 2, b, lo:SEQ], start=b == 0, stop=b == TILES - 1)
                    last.then_inc(summed.sem, 1)

                for i in range(heads + 3):
                    if i < heads:
                        score(i)
                    if 2 <= i < heads + 2:
                        turn(i - 2)
                    if i >= 3:
                        sum_values(i - 3)

            @block.vector
            def _(dve):
                def peaks(h):
                    dve.wait_ge(scores.sem, scores.at(h + 1))
                    src = ps[:, h % deep, :].rearrange("p (a k) -> p a k", a=TILES)
                    if masked:
                        if h >= deep:
                            dve.wait_ge(turned.sem, turned.at(h - deep + 1))
                        dve.tensor_copy(e_buf[:, h % deep, 1, 0:P], src[:, 1, 0:P])
                        for a in range(TILES):
                            last = dve.tensor_tensor(e_buf[:, h % deep, a, a * P:(a + 1) * P],
                                                     src[:, a, a * P:(a + 1) * P], causal[:, :], ALU.add)
                        dve_chain.link(dve, last)
                        for a in range(TILES):
                            last = dve.tensor_reduce(small[:, h % deep, a, 0:1], e_buf[:, h % deep, a, 0:keys(a)], AX,
                                                     ALU.max)
                    else:
                        last = dve.tensor_reduce(small[:, h % deep, :, 0:1], src, AX, ALU.max)
                    dve_chain.link(dve, last)
                    dve.tensor_scalar(small[:, h % deep, :, 1:2], small[:, h % deep, :, 0:1], -scale, None,
                                      ALU.mult).then_inc(peak.sem, 1)

                def normalise(h):
                    dve.wait_ge(expd.sem, expd.at(TILES * (h + 1)))
                    dve_chain.link(dve, dve.reciprocal(small[:, h % deep, :, 3:4], small[:, h % deep, :, 2:3]))
                    for a in range(TILES):
                        last = dve.tensor_scalar(e_buf[:, h % deep, a, 0:keys(a)], e_buf[:, h % deep, a, 0:keys(a)],
                                                 small[:, h % deep, a, 3:4], None, ALU.mult)
                    last.then_inc(norm.sem, 1)

                for i in range(heads + 1):
                    if i < heads:
                        peaks(i)
                    if i >= 1:
                        normalise(i - 1)

            @block.scalar
            def _(act):
                def exps(h):
                    act.wait_ge(peak.sem, peak.at(h + 1))
                    if h >= deep:
                        act.wait_ge(turned.sem, turned.at(h - deep + 1))
                    for a in range(TILES):
                        src = e_buf[:, h % deep, a, 0:keys(a)] if masked else ps[:, h % deep, a * SEQ:(a + 1) * SEQ]
                        act.activation(e_buf[:, h % deep, a, 0:keys(a)], src, ACT.Exp,
                                       bias=small[:, h % deep, a, 1:2], scale=scale,
                                       accum_out=small[:, h % deep, a, 2:3]).then_inc(expd.sem, 1)

                def keep(h):
                    act.wait_ge(turned.sem, turned.at(h + 1))
                    if h >= 2:
                        act.wait_ge(summed.sem, summed.at(h - 1))
                    if masked:
                        act.copy(pt_buf[:, h % 2, 0, :], ps[:, deep + h % 2, 0:SEQ])
                        last = act.copy(pt_buf[:, h % 2, 1, P:SEQ], ps[:, deep + h % 2, SEQ + P:2 * SEQ])
                    else:
                        last = act.copy(pt_buf[:, h % 2, :, :],
                                        ps[:, deep + h % 2, :].rearrange("p (b q) -> p b q", b=TILES))
                    last.then_inc(kept.sem, 1)

                def store(h):
                    act.wait_ge(summed.sem, summed.at(h + 1))
                    act.copy(mix_cols[:, (mix_head + h) // 2, :], ps[:, 6 + h // 2 % 2, 0:SEQ]).then_inc(stored.sem, 1)

                for i in range(heads + 4):
                    if i < heads:
                        exps(i)
                    if 2 <= i < heads + 2:
                        keep(i - 2)
                    if i >= 4 and (i - 4) % 2 == 1:
                        store(i - 4)
        for s in (scores, norm, turned, kept, summed, peak):
            s.advance(heads)
        expd.advance(TILES * heads)
        stored.advance(heads // 2)

    def even_mixer():
        mem = Arena()
        h = mem.take(TILES, EVEN_IN)
        load = [(norm_cols[:, 0:2], t["mla_q_norm"][0].rearrange("(c p) -> p c", p=P)),
                (norm_cols[:, 2:3], t["mla_kv_norm"][0].rearrange("(c p) -> p c", p=P)),
                (ln_params[:, 0, :], spread(t["ln1_g"][0])), (ln_params[:, 1, :], spread(t["ln1_b"][0]))]
        to_columns(x, x_hi, x_lo, more_params=load)
        project(EVEN_IN, h)
        base = mem.at

        q = mem.take(TILES, MLA_HEADS, MLA_QK)
        kv = mem.take(TILES, MLA_HEADS, NOPE + V_DIM)
        k = mem.take(TILES, MLA_HEADS, MLA_QK)
        q_cols = mem.take(MLA_HEADS, SEQ)
        k_cols = mem.take(MLA_HEADS, SEQ)
        mem_att = mem.at
        latent = mem.take(TILES, Q_LORA + KV_LORA)
        latent_cols = mem.take(3, SEQ)
        scratch = mem.take(4, TILES * MLA_HEADS * ROPE_A // 2)
        sums = stat[:, 0:4]
        roots = stat[:, 4:8]
        unit = stream.take(1)
        squared, rooted, scaled, turned, taken, ready, kept, k_made, qk_made, freed = (signal(s) for s in (
            "squares_summed", "root_ready", "latents_scaled", "columns_turned", "latents_turned", "up_projected",
            "up_kept", "k_heads_ready", "qk_heads_ready", "head_columns_kept"))
        with nc.Block() as block:
            @block.sync
            def _(sp):
                stream.issue(sp)

            @block.scalar
            def _(act):
                for a in range(TILES):
                    act.activation(latent[:, a, 0:Q_LORA], h[:, a, O_CQ:O_CQ + Q_LORA], ACT.Square,
                                   accum_out=sums[:, a:a + 1])
                    last = act.activation(latent[:, a, Q_LORA:], h[:, a, O_CKV:O_CKV + KV_LORA], ACT.Square,
                                          accum_out=sums[:, 2 + a:3 + a])
                last.then_inc(squared.sem, 1)
                act.wait_ge(rooted.sem, rooted.at(1))
                act.wait_ge(squared.sem, squared.at(1))
                for a in range(TILES):
                    act.activation(latent[:, a, 0:Q_LORA], h[:, a, O_CQ:O_CQ + Q_LORA], ACT.Copy,
                                   scale=roots[:, a:a + 1])
                    last = act.activation(latent[:, a, Q_LORA:], h[:, a, O_CKV:O_CKV + KV_LORA], ACT.Copy,
                                          scale=roots[:, 2 + a:3 + a])
                last.then_inc(scaled.sem, 1)
                params_ready(act)
                for c in range(3):
                    act.wait_ge(turned.sem, turned.at(c + 1))
                    last = act.activation(latent_cols[:, c, :], ps[:, c, 0:SEQ], ACT.Copy,
                                          scale=norm_cols[:, c:c + 1])
                last.then_inc(taken.sem, 1)
                for a in range(TILES):
                    if a == 0:
                        act.wait_ge(ready.sem, ready.at(1))
                    else:
                        act.wait_ge(stream.used, unit + 1)
                    width = MLA_HEADS * MLA_QK // 2
                    for i in range(2):
                        act.copy(q[:, a, 4 * i:4 * i + 4, :],
                                 ps[:, 4 * a + i, 0:width].rearrange("p (h d) -> p h d", d=MLA_QK))
                    for i in range(2):
                        last = act.copy(kv[:, a, 4 * i:4 * i + 4, :],
                                        ps[:, 4 * a + 2 + i, :].rearrange("p (h d) -> p h d", d=NOPE + V_DIM))
                    last.then_inc(kept.sem, 1)
                for g in range(MLA_HEADS):
                    act.wait_ge(turned.sem, turned.at(3 + g + 1))
                    dst = (q_cols if g < 4 else k_cols)[0:MLA_QK, 2 * (g % 4):2 * (g % 4) + 2, :]
                    act.copy(dst, ps[0:MLA_QK, g, :].rearrange("p (h q) -> p h q", h=2))

            @block.gpsimd
            def _(pool):
                pool.wait_ge(squared.sem, squared.at(1))
                inverse_root(pool, roots[:, 0:2], sums[:, 0:2], Q_LORA)
                inverse_root(pool, roots[:, 2:4], sums[:, 2:4], KV_LORA).then_inc(rooted.sem, 1)

            @block.tensor
            def _(pe):
                pe.wait_ge(scaled.sem, scaled.at(1))
                for c in range(3):
                    for a in range(TILES):
                        last = pe.transpose(ps[:, c, a * P:(a + 1) * P], latent[:, a, c * P:(c + 1) * P],
                                            ident[:, :])
                    last.then_inc(turned.sem, 1)
                pe.wait_ge(taken.sem, taken.at(1))
                stream.wait(pe, unit)
                w = stream.slot(unit)
                uq = w[:, 0:2 * MLA_HEADS * MLA_QK].rearrange("p (c n) -> p c n", c=2)
                ukv = w[:, 2 * MLA_HEADS * MLA_QK:2 * MLA_HEADS * MLA_QK + D]
                width = MLA_HEADS * MLA_QK // 2
                for a in range(TILES):
                    for i in range(2):
                        for c in range(2):
                            pe.matmul(ps[:, 4 * a + i, 0:width], latent_cols[:, c, a * P:(a + 1) * P],
                                      uq[:, c, i * width:(i + 1) * width], start=c == 0, stop=c == 1)
                    for i in range(2):
                        last = pe.matmul(ps[:, 4 * a + 2 + i, :], latent_cols[:, 2, a * P:(a + 1) * P],
                                         ukv[:, i * BANK:(i + 1) * BANK], start=True, stop=True)
                    last.then_inc(ready.sem if a == 0 else stream.used, 1)
                pe.wait_ge(qk_made.sem, qk_made.at(1))
                for g in range(MLA_HEADS):
                    src = q if g < 4 else k
                    for i in range(4):
                        hd, a = 2 * (g % 4) + i // 2, i % 2
                        last = pe.transpose(ps[0:MLA_QK, g, i * P:(i + 1) * P], src[:, a, hd, :], ident[:, :])
                    last.then_inc(turned.sem, 1)

            @block.vector
            def _(dve):
                half = ROPE_A // 2
                kpe = h[:, :, O_KPE:O_KPE + ROPE_A]
                small = [scratch[:, i, 0:TILES * half].rearrange("p (a f) -> p a f", a=TILES) for i in range(4)]
                dve_chain.link(dve, rotate(dve, kpe[:, :, 0:half], kpe[:, :, half:], rope_mla[:, :, 0, :],
                                           rope_mla[:, :, 1, :], small))
                for a in range(TILES):
                    dve.tensor_copy(k[:, a, :, NOPE:], kpe[:, a, :].rearrange("p (u r) -> p u r", u=1)
                                    .broadcast_to([P, MLA_HEADS, ROPE_A]))
                dve.wait_ge(kept.sem, kept.at(TILES))
                for a in range(TILES):
                    dve.tensor_copy(k[:, a, :, 0:NOPE], kv[:, a, :, 0:NOPE])
                for a in range(TILES):
                    wide = [scratch[:, i, 0:MLA_HEADS * half].rearrange("p (h f) -> p h f", h=MLA_HEADS)
                            for i in range(4)]
                    cos, sin = (rope_mla[:, a, i:i + 1, :].broadcast_to([P, MLA_HEADS, half]) for i in range(2))
                    last = rotate(dve, q[:, a, :, NOPE:NOPE + half], q[:, a, :, NOPE + half:], cos, sin, wide)
                    if a == 0:
                        dve_chain.link(dve, last)
                last.then_inc(qk_made.sem, 1)
        squared.advance(1), rooted.advance(1), scaled.advance(1), turned.advance(3 + MLA_HEADS)
        taken.advance(1), ready.advance(1), kept.advance(TILES), qk_made.advance(1)

        attention(MLA_HEADS, lambda i: q_cols[0:MLA_QK, i, :], lambda i: k_cols[0:MLA_QK, i, :],
                  lambda i, b: kv[:, b, i, NOPE:], 0, MLA_QK ** -0.5, False, Arena(mem_att))
        return h, base

    def gla(h, base):
        mem = Arena(base)
        width = GLA_HEADS * DK
        pairs = GLA_HEADS // 2
        gate_w = mem.take(2 * width)
        gate_b = mem.take(2 * width)
        gain = mem.take(DV)
        lr_cols = mem.take(SEQ)
        log_a = mem.take(TILES, 2 * width)
        soft = mem.take(TILES, 2 * width)
        up = mem.take(2, pairs, SEQ)
        down = mem.take(2, pairs, SEQ)
        tail = mem.take(TILES, 2, width)
        qk_cols = mem.take(2, pairs, SEQ)
        q_up = mem.take(2, pairs, SEQ)
        state = mem.take(2, pairs, N_CHUNKS, DV)
        o = mem.take(TILES, GLA_HEADS * DV)
        gate = mem.take(TILES, GLA_HEADS * DV)
        att = x_cols[:, :, :].rearrange("p c q -> p (c q)").rearrange("p (g i l) -> p g i l", g=4, i=4)
        sums, roots = stat[:, 0:8], stat[:, 8:16]
        cleared = signal("gate_weights_cleared")
        with nc.Block() as block:
            @block.gpsimd
            def _(pool):
                pool.memset(gate_w, 0.0).then_inc(cleared.sem, 1)

            @block.sync
            def _(sp):
                sp.wait_ge(cleared.sem, cleared.at(1))
                load_params(sp, (gate_w[0:RANK, 0:width], t["gla_gate_w_fwd"][0]),
                            (gate_w[RANK:2 * RANK, width:], t["gla_gate_w_bwd"][0]),
                            (gate_b[0:1, 0:width], t["gla_gate_b_fwd"]),
                            (gate_b[0:1, width:], t["gla_gate_b_bwd"]),
                            (gain, spread(t["gla_norm"][0])))
        cleared.advance(1)
        turned, taken, gates, softs, logs, cums, exps, tails = (signal(s) for s in (
            "columns_turned", "columns_taken", "gate_logits", "soft_parts", "log_decays", "decays_summed",
            "decay_factors", "decayed_keys"))
        silus, gains, ups, states, atts, masked, outs, squares, rooted, normed, mixed = (signal(s) for s in (
            "gates_activated", "gates_scaled", "updates_ready", "states_ready", "chunk_scores", "chunk_scores_masked",
            "chunk_outputs", "squares_summed", "root_ready", "outputs_normed", "outputs_turned"))
        updates = [(d, pr, hh, n) for par in range(2) for d in range(2) for pr in range(pairs) for hh in range(2)
                   for n in range(par, N_CHUNKS, 2) if n != (N_CHUNKS - 1 if d == 0 else 0)]
        with nc.Block() as block:
            @block.sync
            def _(sp):
                stream.issue(sp)

            @block.tensor
            def _(pe):
                for a in range(TILES):
                    pe.transpose(ps[0:2 * RANK, 0, a * P:(a + 1) * P], h[:, a, O_LR:O_LR + 2 * RANK], ident[:, :])
                for i, off in enumerate((O_GQ, O_GK)):
                    for pr in range(pairs):
                        for a in range(TILES):
                            last = pe.transpose(ps[:, 1 + i, pr * SEQ + a * P:pr * SEQ + (a + 1) * P],
                                                h[:, a, off + pr * P:off + (pr + 1) * P], ident[:, :])
                last.then_inc(turned.sem, 1)
                params_ready(pe)
                pe.wait_ge(taken.sem, taken.at(1))
                for a in range(TILES):
                    pe.matmul(ps[:, 3 + a, :], lr_cols[0:2 * RANK, a * P:(a + 1) * P], gate_w[0:2 * RANK, :],
                              start=True, stop=False)
                    last = pe.matmul(ps[:, 3 + a, :], ones_row[0:1, :], gate_b[0:1, :], start=False, stop=True)
                last.then_inc(gates.sem, 1)
                pe.wait_ge(logs.sem, logs.at(1))
                for d in range(2):
                    for pr in range(pairs):
                        for a in range(TILES):
                            pe.matmul(ps[:, 5 + d, pr * SEQ + a * P:pr * SEQ + (a + 1) * P],
                                      log_a[:, a, d * width + pr * P:d * width + (pr + 1) * P],
                                      chunk_masks[:, d, :], start=True, stop=True)
                for a in range(TILES):
                    for d in range(2):
                        last = pe.matmul(ps[:, 7 * a, d * width:(d + 1) * width], chunk_masks[:, 2 + d, :],
                                         log_a[:, a, d * width:(d + 1) * width], start=True, stop=True)
                last.then_inc(cums.sem, 1)
                pe.wait_ge(tails.sem, tails.at(1))
                for d, pr, hh, n in updates:
                    half = slice(n % 2 * CHUNK, n % 2 * CHUNK + CHUNK)
                    hd = 2 * pr + hh
                    last = pe.matmul(ps[hh * DK:(hh + 1) * DK, 2 * d + pr + 4 * (n % 2), n // 2 * DV:n // 2 * DV + DV],
                                     tail[half, n // 2, d, hd * DK:(hd + 1) * DK],
                                     h[half, n // 2, O_GV + hd * DV:O_GV + (hd + 1) * DV], start=True, stop=True)
                last.then_inc(ups.sem, 1)
                pe.wait_ge(states.sem, states.at(1))
                for d in range(2):
                    for hh in range(2):
                        half = slice(hh * DK, (hh + 1) * DK)
                        for pr in range(pairs):
                            for a in range(TILES):
                                last = pe.matmul(ps[:, 2 * d + hh, (2 * pr + a) * P:(2 * pr + a + 1) * P],
                                                 down[half, d, pr, a * P:(a + 1) * P],
                                                 q_up[half, d, pr, a * P:(a + 1) * P], start=True, stop=True)
                        last.then_inc(atts.sem, 1)
                pe.wait_ge(masked.sem, masked.at(4))
                for a in range(TILES):
                    for hd in range(GLA_HEADS):
                        pr, hh = hd // 2, hd % 2
                        bank = 4 + 2 * a + hh
                        cols = slice(pr * DV, (pr + 1) * DV)
                        inter = [(d, n) for d in range(2) for n in (2 * a, 2 * a + 1)
                                 if n != (0 if d == 0 else N_CHUNKS - 1)]
                        for d in range(2):
                            pe.matmul(ps[:, bank, cols], att[:, 2 * d + hh, 2 * pr + a, :],
                                      h[:, a, O_GV + hd * DV:O_GV + (hd + 1) * DV], start=d == 0, stop=False,
                                      skip_group_check=True)
                        for d, n in inter:
                            last = pe.matmul(ps[n % 2 * CHUNK:n % 2 * CHUNK + CHUNK, bank, cols],
                                             q_up[hh * DK:(hh + 1) * DK, d, pr, n * CHUNK:(n + 1) * CHUNK],
                                             state[hh * DK:(hh + 1) * DK, d, pr, n, :], start=False,
                                             stop=(d, n) == inter[-1], skip_group_check=True)
                last.then_inc(outs.sem, 1)
                pe.wait_ge(normed.sem, normed.at(1))
                for c in range(GLA_HEADS):
                    for a in range(TILES):
                        last = pe.transpose(ps[:, c // 2, c % 2 * SEQ + a * P:c % 2 * SEQ + (a + 1) * P],
                                            o[:, a, c * P:(c + 1) * P], ident[:, :])
                last.then_inc(mixed.sem, 1)

            @block.scalar
            def _(act):
                act.activation(gate, h[:, :, O_GR:O_GR + GLA_HEADS * DV], ACT.Silu).then_inc(silus.sem, 1)
                act.wait_ge(turned.sem, turned.at(1))
                act.copy(lr_cols[0:2 * RANK, :], ps[0:2 * RANK, 0, 0:SEQ]).then_inc(taken.sem, 1)
                act.activation(qk_cols[:, 0], ps[:, 1, :].rearrange("p (c q) -> p c q", c=pairs), ACT.Copy,
                               scale=DK ** -0.5)
                act.copy(qk_cols[:, 1], ps[:, 2, :].rearrange("p (c q) -> p c q", c=pairs))
                act.wait_ge(gates.sem, gates.at(1))
                z = ps[:, 3:3 + TILES, :]
                act_chain.link(act, act.activation(soft, z, ACT.Abs))
                act_chain.link(act, act.activation(soft, soft, ACT.Exp, scale=-1.0))
                act.activation(soft, soft, ACT.Ln, bias=1.0).then_inc(softs.sem, 1)
                act.wait_ge(cums.sem, cums.at(1))
                for d in range(2):
                    cum = ps[:, 5 + d, :].rearrange("p (c q) -> p c q", c=pairs)
                    act.activation(up[:, d], cum, ACT.Exp, scale=1.0 / GATE_NORM)
                    act.activation(down[:, d], cum, ACT.Exp, scale=-1.0 / GATE_NORM)
                for a in range(TILES):
                    last = act.activation(tail[:, a], ps[:, 7 * a, :].rearrange("p (d f) -> p d f", d=2), ACT.Exp,
                                          scale=1.0 / GATE_NORM)
                last.then_inc(exps.sem, 1)
                act.wait_ge(outs.sem, outs.at(1))
                for a in range(TILES):
                    for hd in range(GLA_HEADS):
                        last = act.activation(soft[:, 0, 0:DV], ps[:, 4 + 2 * a + hd % 2, hd // 2 * DV:hd // 2 * DV + DV],
                                              ACT.Square, accum_out=sums[:, GLA_HEADS * a + hd:GLA_HEADS * a + hd + 1])
                        act_chain.link(act, last)
                act.copy(sums[:, 0:1], sums[:, 0:1]).then_inc(squares.sem, 1)
                act.wait_ge(mixed.sem, mixed.at(1))
                for c in range(0, GLA_HEADS, 2):
                    act.copy(mix_cols[:, 4 + c:6 + c, :], ps[:, c // 2, :].rearrange("p (c q) -> p c q", c=2))

            @block.gpsimd
            def _(pool):
                pool.wait_ge(squares.sem, squares.at(1))
                inverse_root(pool, roots, sums, DV).then_inc(rooted.sem, 1)

            @block.vector
            def _(dve):
                params_ready(dve)
                dve.wait_ge(silus.sem, silus.at(1))
                for a in range(TILES):
                    view = gate[:, a, :].rearrange("p (h e) -> p h e", e=DV)
                    dve.tensor_tensor(view, view, gain.rearrange("p (u e) -> p u e", u=1)
                                      .broadcast_to([P, GLA_HEADS, DV]), ALU.mult)
                dve.wait_ge(softs.sem, softs.at(1))
                for a in range(TILES):
                    last = dve.scalar_tensor_tensor(out=log_a[:, a, :], in0=ps[:, 3 + a, :], scalar=0.0,
                                                    in1=soft[:, a, :], op0=ALU.min, op1=ALU.subtract)
                last.then_inc(logs.sem, 1)
                dve.wait_ge(exps.sem, exps.at(1))
                for d in range(2):
                    dve.tensor_tensor(q_up[:, d], qk_cols[:, 0], up[:, d], ALU.mult)
                    dve.tensor_tensor(down[:, d], qk_cols[:, 1], down[:, d], ALU.mult)
                for a in range(TILES):
                    for d in range(2):
                        last = dve.tensor_tensor(tail[:, a, d, :], tail[:, a, d, :], h[:, a, O_GK:O_GK + width],
                                                 ALU.mult)
                last.then_inc(tails.sem, 1)
                dve.wait_ge(ups.sem, ups.at(1))
                order = {0: range(0, N_CHUNKS - 1), 1: range(N_CHUNKS - 1, 0, -1)}
                for step in range(N_CHUNKS - 1):
                    for d in range(2):
                        n = order[d][step]
                        nxt, end = (n + 1, (n + 1) * CHUNK - 1) if d == 0 else (n - 1, n * CHUNK)
                        for pr in range(pairs):
                            update = ps[:, 2 * d + pr + 4 * (n % 2), n // 2 * DV:n // 2 * DV + DV]
                            if step == 0:
                                last = dve.tensor_copy(state[:, d, pr, nxt, :], update)
                            else:
                                last = dve.scalar_tensor_tensor(
                                    out=state[:, d, pr, nxt, :], in0=state[:, d, pr, n, :],
                                    scalar=up[:, d, pr, end:end + 1], in1=update, op0=ALU.mult, op1=ALU.add)
                    if step < N_CHUNKS - 2:
                        dve_chain.link(dve, last)
                last.then_inc(states.sem, 1)
                for g in range(4):
                    dve.wait_ge(atts.sem, atts.at(g + 1))
                    mask = chunk_masks[:, g // 2:g // 2 + 1, :].broadcast_to([P, 4, P])
                    dve.tensor_tensor(att[:, g], ps[:, g, :].rearrange("p (i l) -> p i l", i=4), mask,
                                      ALU.mult).then_inc(masked.sem, 1)
                dve.wait_ge(rooted.sem, rooted.at(1))
                for a in range(TILES):
                    for hd in range(GLA_HEADS):
                        cols = slice(hd * DV, (hd + 1) * DV)
                        last = dve.scalar_tensor_tensor(
                            out=o[:, a, cols], in0=ps[:, 4 + 2 * a + hd % 2, hd // 2 * DV:hd // 2 * DV + DV],
                            scalar=roots[:, GLA_HEADS * a + hd:GLA_HEADS * a + hd + 1], in1=gate[:, a, cols],
                            op0=ALU.mult, op1=ALU.mult)
                last.then_inc(normed.sem, 1)
        for s in (turned, taken, gates, softs, logs, cums, exps, tails, silus, ups, states, outs, squares, rooted,
                  normed, mixed):
            s.advance(1)
        atts.advance(4), masked.advance(4)

    def odd_mixer():
        mem = Arena()
        h = mem.take(TILES, ODD_IN)
        n_heads = GQA_HEADS + KV_HEADS
        gains = mem.take(2, HD)
        to_columns(x, x_hi, x_lo, more_params=[(gains[:, 0, :], spread(t["gqa_q_norm"][0])),
                                               (gains[:, 1, :], spread(t["gqa_k_norm"][0])),
                                               (ln_params[:, 0, :], spread(t["ln1_g"][1])),
                                               (ln_params[:, 1, :], spread(t["ln1_b"][1]))])
        project(ODD_IN, h)
        q_cols = mem.take(GQA_HEADS // 2, SEQ)
        k_cols = mem.take(KV_HEADS, SEQ)
        mem_att = mem.at
        k_twice = mem.take(TILES, KV_HEADS, 2, HD)
        squares = mem.take(TILES, n_heads * HD)
        scratch = mem.take(TILES, 4, n_heads * HD // 2)
        sums = stat[:, 0:TILES * n_heads]
        roots = stat[:, TILES * n_heads:2 * TILES * n_heads]
        squared, summed, rooted, made, turned = (signal(s) for s in (
            "squares_made", "squares_summed", "root_ready", "qk_heads_ready", "columns_turned"))
        qk = [h[:, a, 0:n_heads * HD].rearrange("p (h d) -> p h d", d=HD) for a in range(TILES)]

        def heads_of(engine, chain, a):
            root = roots[:, a * n_heads:(a + 1) * n_heads].rearrange("p (h u) -> p h u", u=1)
            chain.link(engine, engine.tensor_tensor(qk[a], qk[a], root.broadcast_to([P, n_heads, HD]), ALU.mult))
            engine.tensor_tensor(qk[a][:, 0:GQA_HEADS], qk[a][:, 0:GQA_HEADS],
                                 gains[:, 0:1, :].broadcast_to([P, GQA_HEADS, HD]), ALU.mult)
            chain.link(engine, engine.tensor_tensor(qk[a][:, GQA_HEADS:], qk[a][:, GQA_HEADS:],
                                                    gains[:, 1:2, :].broadcast_to([P, KV_HEADS, HD]), ALU.mult))
            wide = [scratch[:, a, i, :].rearrange("p (h f) -> p h f", h=n_heads) for i in range(4)]
            cos, sin = (rope_gqa[:, a, i:i + 1, :].broadcast_to([P, n_heads, HD // 2]) for i in range(2))
            chain.link(engine, rotate(engine, qk[a][:, :, 0:HD // 2], qk[a][:, :, HD // 2:], cos, sin, wide, chain))
            return engine.tensor_copy(k_twice[:, a], qk[a][:, GQA_HEADS:, :].rearrange("p h (u d) -> p h u d", u=1)
                                      .broadcast_to([P, KV_HEADS, 2, HD]))

        with nc.Block() as block:
            @block.sync
            def _(sp):
                stream.issue(sp)

            @block.scalar
            def _(act):
                for a in range(TILES):
                    act.activation(squares[:, a, :], h[:, a, 0:n_heads * HD], ACT.Square).then_inc(squared.sem, 1)
                for b in range((GQA_HEADS // 2 + KV_HEADS) // 2):
                    act.wait_ge(turned.sem, turned.at(b + 1))
                    dst = q_cols[:, 2 * b:2 * b + 2, :] if b < GQA_HEADS // 4 else \
                        k_cols[:, 2 * b - GQA_HEADS // 2:2 * b - GQA_HEADS // 2 + 2, :]
                    act.copy(dst, ps[:, b, :].rearrange("p (c q) -> p c q", c=2))

            @block.vector
            def _(dve):
                for a in range(TILES):
                    dve.wait_ge(squared.sem, squared.at(a + 1))
                    dve.tensor_reduce(sums[:, a * n_heads:(a + 1) * n_heads],
                                      squares[:, a, :].rearrange("p (h d) -> p h d", d=HD), AX,
                                      ALU.add).then_inc(summed.sem, 1)
                params_ready(dve)
                dve.wait_ge(rooted.sem, rooted.at(1))
                heads_of(dve, dve_chain, 0).then_inc(made.sem, 1)

            @block.gpsimd
            def _(pool):
                pool.wait_ge(summed.sem, summed.at(TILES))
                inverse_root(pool, roots, sums, HD).then_inc(rooted.sem, 1)
                params_ready(pool)
                pool.wait_ge(rooted.sem, rooted.at(1))
                heads_of(pool, pool_chain, 1).then_inc(made.sem, 1)

            @block.tensor
            def _(pe):
                pe.wait_ge(made.sem, made.at(2))
                for b in range((GQA_HEADS // 2 + KV_HEADS) // 2):
                    for i in range(2):
                        c = 2 * b + i
                        for a in range(TILES):
                            src = h[:, a, c * P:(c + 1) * P] if c < GQA_HEADS // 2 else \
                                k_twice[:, a, c - GQA_HEADS // 2].rearrange("p u d -> p (u d)")
                            last = pe.transpose(ps[:, b, i * SEQ + a * P:i * SEQ + (a + 1) * P], src, ident[:, :])
                    last.then_inc(turned.sem, 1)
        squared.advance(TILES), summed.advance(TILES), rooted.advance(1), made.advance(2)
        turned.advance((GQA_HEADS // 2 + KV_HEADS) // 2)
        group = GQA_HEADS // KV_HEADS
        half = lambda i: slice(i % 2 * HD, i % 2 * HD + HD)
        attention(GQA_HEADS, lambda i: q_cols[half(i), i // 2, :], lambda i: k_cols[half(i), i // group, :],
                  lambda i, b: h[:, b, (n_heads + i // group) * HD:(n_heads + i // group + 1) * HD], 0, HD ** -0.5,
                  False, Arena(mem_att))

    def experts(layer):
        mem = Arena()
        picked_cols = mem.take(DC, EXPERTS, CAP)
        spread_back = mem.take(EXPERTS, SEQ)
        rest = mem.take(TILES, D)
        tokens_now = mem.take(DC, CAP)
        back_now = mem.take(SEQ)
        silu_g = mem.take(QW)
        hidden = mem.take(QW)
        hidden_cols = mem.take(2, P)
        partial = mem.take(D)
        loop_end = mem.at
        one_hot = mem.take(TILES, EXPERTS, CAP)
        p_tokens = mem.take(TILES, PLE_DIM)
        p_cols = mem.take(2, SEQ)
        router = mem.take(DC, EXPERTS)
        slots = mem.take(CAP)
        aff = mem.take(TILES, EXPERTS)
        slot_tokens = mem.take(TILES, EXPERTS)
        ones = mem.take(SEQ)
        left = mem.take(SEQ)
        chosen = mem.take(SEQ)
        rank = mem.take(SEQ)
        bias = Arena(loop_end - D).take(D)
        tops = stat[:, 32:64]
        stats = stat[:, 64:96]
        four_hot = [x_cols[:, :, :].rearrange("p c q -> p (c q)"), mix_cols[:, :, :].rearrange("p c q -> p (c q)")]
        gate_hi, gate_lo = gate_parts
        four_hot = [v.rearrange("p (e j s) -> p e j s", e=EXPERTS, j=QUADS) for v in four_hot]

        to_columns(x, gate_hi, gate_lo, full=x_cols, more_params=[
            (router, t["router_w"][layer].rearrange("(c p) e -> p c e", p=P)),
            (p_tokens, t["p"][layer, 0].rearrange("(a p) d -> p a d", p=P)),
            (slots, spread(t["c_slots"])),
            (bias[0:1, :], t["ple_gate_b"][layer:layer + 1, :]),
            (ln_params[:, 0, :], spread(t["ln2_g"][layer])), (ln_params[:, 1, :], spread(t["ln2_b"][layer]))])

        job = PartedProducts(stream.take(2), D, gate_hi, gate_lo, range(4, 8), gate_w_parts,
                             bias=bias)
        ple_unit = stream.take(1)
        logits, affs, turned, ranked, turned_back, hot, gathered, kept, four, spread_s = (signal(s) for s in (
            "logits_ready", "affinities_ready", "affinities_turned", "slots_ranked", "slots_turned", "one_hot_ready",
            "tokens_gathered", "gathered_kept", "four_hot_ready", "one_hot_turned"))
        exped, maxed = signal("router_exps"), signal("router_max")
        ple_p, ple_pk, ple_s, ple_v = (signal(s) for s in (
            "ple_inputs_turned", "ple_inputs_kept", "ple_gates_activated", "ple_values_ready"))
        spread_kept, ones_made = signal("one_hot_kept"), signal("ones_made")
        with nc.Block() as block:
            @block.sync
            def _(sp):
                stream.issue(sp)

            @block.tensor
            def _(pe):
                params_ready(pe)
                for a in range(TILES):
                    for c in range(DC):
                        last = pe.matmul(ps[:, 0, a * EXPERTS:(a + 1) * EXPERTS], x_cols[:, c, a * P:(a + 1) * P],
                                         router[:, c, :], start=c == 0, stop=c == DC - 1)
                last.then_inc(logits.sem, 1)
                for c in range(2):
                    for a in range(TILES):
                        last = pe.transpose(ps[:, 1, c * SEQ + a * P:c * SEQ + (a + 1) * P],
                                            p_tokens[:, a, c * P:(c + 1) * P], ident[:, :])
                last.then_inc(ple_p.sem, 1)
                for h in range(2):
                    job.products(pe, h)
                    if h == 0:
                        pe.wait_ge(affs.sem, affs.at(1))
                        for a in range(TILES):
                            last = pe.transpose(ps[0:EXPERTS, 2, a * P:(a + 1) * P], aff[:, a, :], ident[:, :])
                        last.then_inc(turned.sem, 1)
                stream.wait(pe, ple_unit)
                pe.wait_ge(ple_pk.sem, ple_pk.at(1))
                w = stream.slot(ple_unit)[:, 0:2 * D].rearrange("p (c n) -> p c n", c=2)
                pe.wait_ge(ple_s.sem, ple_s.at(4))
                for h in range(2):
                    for a in range(TILES):
                        for c in range(2):
                            last = pe.matmul(ps[:, 4 + 2 * h + a, :], p_cols[:, c, a * P:(a + 1) * P],
                                             w[:, c, h * BANK:(h + 1) * BANK], start=c == 0, stop=c == 1)
                        last.then_inc(stream.used if (h, a) == (1, 1) else ple_v.sem, 1)
                pe.wait_ge(ranked.sem, ranked.at(1))
                for a in range(TILES):
                    last = pe.transpose(ps[:, 3, a * EXPERTS:(a + 1) * EXPERTS], rank[0:EXPERTS, a * P:(a + 1) * P],
                                        ident[0:EXPERTS, 0:EXPERTS])
                last.then_inc(turned_back.sem, 1)
                pe.wait_ge(hot.sem, hot.at(1))
                for c in range(DC):
                    if c >= 4:
                        pe.wait_ge(kept.sem, kept.at(c - 3))
                    for a in range(TILES):
                        last = pe.matmul(ps[:, c % 4, :], x[:, a, c * P:(c + 1) * P],
                                         one_hot[:, a].rearrange("p e s -> p (e s)"), start=a == 0,
                                         stop=a == TILES - 1)
                    last.then_inc(gathered.sem, 1)
                pe.wait_ge(four.sem, four.at(2))
                for g in range(EXPERTS // 2):
                    bank = 4 + g % 4
                    if g >= 4:
                        pe.wait_ge(spread_kept.sem, spread_kept.at(g - 3))
                    for i in range(2):
                        for a in range(TILES):
                            last = pe.transpose(ps[:, bank, i * SEQ + a * P:i * SEQ + (a + 1) * P],
                                                four_hot[a][:, 2 * g + i].rearrange("p j s -> p (j s)"), ident[:, :])
                    last.then_inc(spread_s.sem, 1)

            @block.scalar
            def _(act):
                job.part_high(act, 0, 0), job.part_high(act, 0, 1)
                act.wait_ge(maxed.sem, maxed.at(1))
                act.activation(aff, aff, ACT.Exp).then_inc(exped.sem, 1)
                act.wait_ge(ple_p.sem, ple_p.at(1))
                act.copy(p_cols, ps[:, 1, :].rearrange("p (c q) -> p c q", c=2)).then_inc(ple_pk.sem, 1)
                for h in range(2):
                    job.part_high(act, 1, h)
                params_ready(act)
                for h in range(2):
                    job.wait(act, h)
                    for a in range(TILES):
                        act.activation(rest[:, a, h * BANK:(h + 1) * BANK], ps[:, 4 + 2 * h + a, :],
                                       ACT.Sigmoid).then_inc(ple_s.sem, 1)
                for c in range(DC):
                    act.wait_ge(gathered.sem, gathered.at(c + 1))
                    act.copy(picked_cols[:, c], ps[:, c % 4, :].rearrange("p (e s) -> p e s", e=EXPERTS)
                             ).then_inc(kept.sem, 1)
                for g in range(EXPERTS // 2):
                    act.wait_ge(spread_s.sem, spread_s.at(g + 1))
                    act.copy(spread_back[:, 2 * g:2 * g + 2, :], ps[:, 4 + g % 4, :].rearrange("p (e q) -> p e q", e=2)
                             ).then_inc(spread_kept.sem, 1)

            @block.vector
            def _(dve):
                job.part_low(dve, 0, 0), job.part_low(dve, 0, 1)
                params_ready(dve)
                dve.wait_ge(logits.sem, logits.at(1))
                lg = ps[:, 0, 0:TILES * EXPERTS].rearrange("p (a e) -> p a e", a=TILES)
                top, total = tops[:, 0:TILES], tops[:, TILES:2 * TILES]
                wide = lambda v: v.rearrange("p (a u) -> p a u", u=1).broadcast_to([P, TILES, EXPERTS])
                dve_chain.link(dve, dve.tensor_reduce(top, lg, AX, ALU.max))
                dve.tensor_tensor(aff, lg, wide(top), ALU.subtract).then_inc(maxed.sem, 1)
                dve.wait_ge(exped.sem, exped.at(1))
                dve_chain.link(dve, dve.tensor_reduce(total, aff, AX, ALU.add))
                dve_chain.link(dve, dve.reciprocal(total, total))
                dve.tensor_tensor(aff, aff, wide(total), ALU.mult).then_inc(affs.sem, 1)
                job.part_low(dve, 1, 0), job.part_low(dve, 1, 1)
                dve.wait_ge(turned.sem, turned.at(1))
                dve_chain.link(dve, dve.tensor_copy(left[0:EXPERTS, :], ps[0:EXPERTS, 2, 0:SEQ]))
                for r in range(CAP // 8):
                    dve_chain.link(dve, dve.max(tops[0:EXPERTS, 8:16], left[0:EXPERTS, :]))
                    dve_chain.link(dve, dve.match_replace(out=left[0:EXPERTS, :], in_to_replace=tops[0:EXPERTS, 8:16],
                                                          in_values=left[0:EXPERTS, :], imm_value=-1.0))
                dve_chain.link(dve, dve.tensor_scalar(chosen[0:EXPERTS, :], left[0:EXPERTS, :], 0.0, None, ALU.is_lt))
                dve.wait_ge(ones_made.sem, ones_made.at(1))
                dve_chain.link(dve, dve.tensor_tensor_scan(rank[0:EXPERTS, :], ones[0:EXPERTS, :],
                                                           chosen[0:EXPERTS, :], 0.0, ALU.mult, ALU.add))
                dve.tensor_tensor(rank[0:EXPERTS, :], rank[0:EXPERTS, :], chosen[0:EXPERTS, :],
                                  ALU.mult).then_inc(ranked.sem, 1)
                for h in range(2):
                    for a in range(TILES):
                        if (h, a) == (1, 1):
                            dve.wait_ge(stream.used, ple_unit + 1)
                        else:
                            dve.wait_ge(ple_v.sem, ple_v.at(2 * h + a + 1))
                        last = dve.tensor_tensor(rest[:, a, h * BANK:(h + 1) * BANK],
                                                 rest[:, a, h * BANK:(h + 1) * BANK], ps[:, 4 + 2 * h + a, :], ALU.mult)
                dve.wait_ge(turned_back.sem, turned_back.at(1))
                dve_chain.link(dve, dve.tensor_copy(
                    slot_tokens, ps[:, 3, 0:TILES * EXPERTS].rearrange("p (a e) -> p a e", a=TILES)))
                for a in range(TILES):
                    last = dve.tensor_tensor(one_hot[:, a],
                                             slot_tokens[:, a].rearrange("p (e u) -> p e u", u=1)
                                             .broadcast_to([P, EXPERTS, CAP]),
                                             slots.rearrange("p (u s) -> p u s", u=1).broadcast_to([P, EXPERTS, CAP]),
                                             ALU.is_equal)
                last.then_inc(hot.sem, 1)
                dve.wait_ge(hot.sem, hot.at(1))
                for a in range(TILES):
                    dve.tensor_tensor(four_hot[a],
                                      one_hot[:, a].rearrange("p e (u s) -> p e u s", u=1)
                                      .broadcast_to([P, EXPERTS, QUADS, CAP]),
                                      aff[:, a].rearrange("p (e u v) -> p e u v", u=1, v=1)
                                      .broadcast_to([P, EXPERTS, QUADS, CAP]), ALU.mult).then_inc(four.sem, 1)
                for a in range(TILES):
                    dve.scalar_tensor_tensor(out=rest[:, a, :], in0=x[:, a, :], scalar=ALPHA, in1=rest[:, a, :],
                                             op0=ALU.mult, op1=ALU.add)

            @block.gpsimd
            def _(pool):
                pool.memset(ones, 1.0).then_inc(ones_made.sem, 1)
        for s in (logits, affs, turned, ranked, turned_back, hot, exped, ple_p, ple_pk):
            s.advance(1)
        job.close()
        maxed.advance(1), ones_made.advance(1), four.advance(2), ple_s.advance(4), ple_v.advance(3)
        gathered.advance(DC), kept.advance(DC), spread_s.advance(EXPERTS // 2), spread_kept.advance(EXPERTS // 2)

        first = stream.take(6 * EXPERTS)
        assert stream.issued == first + WEIGHT_SLOTS
        token_set, back_set, silued, hid, h_turned, h_kept, part_0, part_1 = (signal(s) for s in (
            "expert_tokens_set", "scatter_rows_set", "expert_gates_activated", "expert_hidden_ready",
            "expert_hidden_turned", "expert_hidden_kept", "partial_0_kept", "partial_1_kept"))
        used = stream.used
        hc = hidden_cols
        with nc.Block() as block:
            @block.sync
            def _(sp):
                with sp.Fori(0, EXPERTS - 1) as e:
                    for k in range(6):
                        sp.wait_ge(used, e * 6 + (first + k + 1))
                        stream.load(sp, first + k, e + 1)
                stream.issued = first + 6 * EXPERTS
                stream.issue(sp)

            @block.tensor
            def _(pe):
                for b in range(4):
                    pe.matmul(ps[:, b, :], zeros_bf[:, 0:P], zeros_bf[:, :], start=True, stop=False,
                              skip_group_check=True)
                with pe.Fori(0, EXPERTS) as e:
                    pe.wait_ge(token_set.sem, e + token_set.at(1))
                    for k in range(4):
                        u = first + k
                        w = stream.slot(u).rearrange("p (c f) -> p c f", c=DC // 2)
                        pe.wait_ge(stream.arrived[u % WEIGHT_SLOTS], e * 16 + stream.value[u])
                        for c in range(DC // 2):
                            cc = k % 2 * DC // 2 + c
                            for j in range(QUADS):
                                last = pe.matmul(ps[j * CAP:(j + 1) * CAP, 4 + k // 2, 0:QW], tokens_now[:, cc, :],
                                                 w[:, c, j * QW:(j + 1) * QW], start=cc == 0, stop=cc == DC - 1)
                        last.then_inc(used, 1)
                    pe.wait_ge(hid.sem, e + hid.at(1))
                    for i in range(2):
                        last = pe.transpose(ps[:, 4, i * P:(i + 1) * P], hidden[:, i * P:(i + 1) * P], ident[:, :])
                    last.then_inc(h_turned.sem, 1)
                    pe.wait_ge(h_kept.sem, e + h_kept.at(1))
                    for h in range(2):
                        u = first + 4 + h
                        w = stream.slot(u).rearrange("p (c f) -> p c f", c=DC)
                        pe.wait_ge(stream.arrived[u % WEIGHT_SLOTS], e * 16 + stream.value[u])
                        for i in range(2):
                            for j in range(QUADS):
                                last = pe.matmul(ps[j * CAP:(j + 1) * CAP, 6 + h, :], hc[:, i, j * CAP:(j + 1) * CAP],
                                                 w[:, 2 * j + i, :], start=i == 0, stop=i == 1)
                        last.then_inc(used, 1)
                    pe.wait_ge(back_set.sem, e + back_set.at(1))
                    for h, part in enumerate((part_0, part_1)):
                        pe.wait_ge(part.sem, e + part.at(1))
                        for a in range(TILES):
                            pe.matmul(ps[:, 2 * h + a, :], back_now[:, a * P:(a + 1) * P],
                                             partial[:, h * BANK:(h + 1) * BANK], start=False, stop=False,
                                             skip_group_check=True)

            @block.scalar
            def _(act):
                with act.Fori(0, EXPERTS) as e:
                    act.wait_ge(used, e * 6 + (first + 2))
                    act.activation(silu_g, ps[:, 4, 0:QW], ACT.Silu).then_inc(silued.sem, 1)
                    act.wait_ge(h_turned.sem, e + h_turned.at(1))
                    act.copy(hc, ps[:, 4, 0:2 * P].rearrange("p (i q) -> p i q", i=2)).then_inc(h_kept.sem, 1)
                    act.wait_ge(used, e * 6 + (first + 5))
                    act.copy(partial[:, 0:BANK], ps[:, 6, :]).then_inc(part_0.sem, 1)

            @block.vector
            def _(dve):
                with dve.Fori(0, EXPERTS) as e:
                    dve.wait_ge(silued.sem, e + silued.at(1))
                    dve.wait_ge(used, e * 6 + (first + 4))
                    dve.tensor_tensor(hidden, silu_g, ps[:, 5, 0:QW], ALU.mult).then_inc(hid.sem, 1)
                    dve.wait_ge(used, e * 6 + (first + 6))
                    dve.tensor_copy(partial[:, BANK:], ps[:, 7, :]).then_inc(part_1.sem, 1)

            @block.gpsimd
            def _(pool):
                with pool.Fori(0, EXPERTS) as e:
                    pool.wait_ge(used, e * 6 + (first - 2))
                    pool.tensor_copy(tokens_now.rearrange("p c (u s) -> p c u s", u=1),
                                     picked_cols[:, :, bass.ds(e, 1), :]).then_inc(token_set.sem, 1)
                    pool.wait_ge(used, e * 6 + (first + 1))
                    pool.tensor_copy(back_now.rearrange("p (u q) -> p u q", u=1),
                                     spread_back[:, bass.ds(e, 1), :]).then_inc(back_set.sem, 1)
        for s in (token_set, back_set, silued, hid, h_turned, h_kept, part_0, part_1):
            s.advance(EXPERTS)

        wanted, got, centred = signal("root_wanted"), signal("root_ready"), signal("tile_centred")
        stats = stat[:, 0:32].rearrange("p (a k) -> p a k", a=TILES)
        with nc.Block() as block:
            @block.sync
            def _(sp):
                stream.issue(sp)

            @block.vector
            def _(dve):
                params_ready(dve)
                for h in range(2):
                    for a in range(TILES):
                        cols = slice(h * BANK, (h + 1) * BANK)
                        last = dve.tensor_tensor(rest[:, a, cols], rest[:, a, cols], ps[:, 2 * h + a, :], ALU.add)
                dve_chain.link(dve, last)
                for h in range(2):
                    for a in range(TILES):
                        last = norm_stats(dve, rest, stats, h, a)
                dve_chain.link(dve, last)
                layer_norm_steps(dve, rest, stats, wanted, got, centred)

            @block.scalar
            def _(act):
                layer_norm_centre(act, rest, stats, got, centred)

            @block.gpsimd
            def _(pool):
                layer_norm_root(pool, stats, wanted, got)
        wanted.advance(1), got.advance(1), centred.advance(1)

    def rms_columns(gain_row):
        normed = Arena(arena_size - TILES * D).take(TILES, D)
        sums, roots = stat[:, 0:TILES], stat[:, TILES:2 * TILES]
        squares, rooted, scaled = signal("squares_summed"), signal("root_ready"), signal("tokens_scaled")
        with nc.Block() as block:
            @block.sync
            def _(sp):
                load_params(sp, (norm_cols[:, :], gain_row.rearrange("(c p) -> p c", p=P)))
                stream.issue(sp)

            @block.scalar
            def _(act):
                for a in range(TILES):
                    last = act.activation(normed[:, a, :], x[:, a, :], ACT.Square, accum_out=sums[:, a:a + 1])
                last.then_inc(squares.sem, 1)
                act.wait_ge(rooted.sem, rooted.at(1))
                act.wait_ge(squares.sem, squares.at(1))
                act.activation(normed[:, 0, :], x[:, 0, :], ACT.Copy, scale=roots[:, 0:1])

            @block.vector
            def _(dve):
                dve.wait_ge(rooted.sem, rooted.at(1))
                dve.tensor_scalar(normed[:, 1, :], x[:, 1, :], roots[:, 1:2], None, ALU.mult)

            @block.gpsimd
            def _(pool):
                pool.wait_ge(squares.sem, squares.at(1))
                inverse_root(pool, roots, sums, D).then_inc(rooted.sem, 1)
        squares.advance(1), rooted.advance(1)
        to_columns(normed, x_hi, x_lo, gain=norm_cols)

    def ffn():
        mem = Arena(13312)
        silu_g = mem.take(2, SEQ)
        hidden = mem.take(2, SEQ)
        steps_total = 2 * F_GROUPS
        first = stream.take(2 * F_GROUPS)
        assert stream.issued == first + WEIGHT_SLOTS
        used = stream.used
        names = ("up_high_kept", "up_low_kept", "down_high_kept", "down_low_kept", "up_products_ready",
                 "down_products_done", "ffn_gates_activated", "hidden_parts_made")
        hi_up, lo_up, hi_down, lo_down, up_done, down_done, silued, made = (signal(n) for n in names)
        body = WEIGHT_SLOTS
        trips = (steps_total - 4) // body
        assert trips * body == steps_total - 4

        def shifted(r, per_trip, value):
            return value if isinstance(r, int) else r * per_trip + value

        def up_weights(k):
            slot = stream.slot(first + k // 2 * 2).rearrange("p (h c f) -> p h c f", h=2, c=DC)
            return slot[:, :, :, k % 2 * P:k % 2 * P + P]

        def down_weights(k):
            return stream.slot(first + k // 2 * 2 + 1)[:, k % 2 * D:(k % 2 + 1) * D]

        def arrived(engine, u, r):
            value = stream.value[u]
            step = stream.value[u + WEIGHT_SLOTS] - value if u + WEIGHT_SLOTS < first + 2 * F_GROUPS else 0
            engine.wait_ge(stream.arrived[u % WEIGHT_SLOTS], shifted(r, step, value))

        def all_steps(engine, step, last):
            step(0, 0), step(1, 0)
            with engine.Fori(0, trips) as r:
                for k in range(2, 2 + body):
                    step(k, r)
            for k in range(2 + trips * body, last):
                step(k, 0)

        with nc.Block() as block:
            @block.sync
            def _(sp):
                def reload(u, r):
                    sp.wait_ge(used, r * WEIGHT_SLOTS + (u - WEIGHT_SLOTS + 1))
                    for dst, src in stream.units[u][0](stream.slot(u), r * (WEIGHT_SLOTS // 2 * FG) + stream.units[u][1]):
                        sp.dma_start(dst, src).then_inc(stream.arrived[u % WEIGHT_SLOTS], 16)

                loads = (2 * F_GROUPS - WEIGHT_SLOTS) // WEIGHT_SLOTS
                with sp.Fori(0, loads) as r:
                    for k in range(WEIGHT_SLOTS):
                        reload(first + WEIGHT_SLOTS + k, r)
                stream.issued = first + WEIGHT_SLOTS * (loads + 1)
                stream.issue(sp)

            @block.tensor
            def _(pe):
                for b in range(4):
                    pe.matmul(ps[:, b, :], zeros_bf[:, 0:P], zeros_bf[:, :], start=True, stop=False,
                              skip_group_check=True)

                def down(k, r):
                    f = k % 2
                    if f == 0:
                        pe.wait_ge(lo_down.sem, shifted(r, body // 2, lo_down.at(k // 2 + 1)))
                    else:
                        pe.wait_ge(used, shifted(r, body, first + k // 2 * 2 + 2))
                    pe.wait_ge(made.sem, shifted(r, 3 * body, made.at(3 * k + 3)))
                    for a in range(TILES):
                        rows = slice(a * P, (a + 1) * P)
                        for x_part, w_part in ((hid_hi, down_hi), (hid_hi, down_lo), (hid_lo, down_hi)):
                            for h in range(2):
                                last = pe.matmul(ps[:, 2 * h + a, :], x_part[:, f, rows],
                                                 w_part[:, f, h * BANK:(h + 1) * BANK], start=False, stop=False,
                                                 skip_group_check=True)
                    last.then_inc(down_done.sem, 1)

                def up(k, r):
                    f = k % 2
                    if f == 0:
                        pe.wait_ge(lo_up.sem, shifted(r, body // 2, lo_up.at(k // 2 + 1)))
                    else:
                        pe.wait_ge(used, shifted(r, body, first + k // 2 * 2 + 1))
                    if k >= 2:
                        pe.wait_ge(made.sem, shifted(r, 3 * body, made.at(3 * k - 5)))
                    for h in range(2):
                        for c in range(DC):
                            for w_part, x_part in ((up_hi, x_hi), (up_hi, x_lo), (up_lo, x_hi)):
                                last = pe.matmul(ps[:, 4 + f, h * SEQ:(h + 1) * SEQ], w_part[:, f, h, c, :],
                                                 x_part[:, c, :], start=c == 0 and w_part is up_hi and x_part is x_hi,
                                                 stop=c == DC - 1 and w_part is up_lo)
                    last.then_inc(up_done.sem, 1)

                def step(k, r):
                    if k >= 2:
                        down(k - 2, r)
                    if k < steps_total:
                        up(k, r)

                all_steps(pe, step, steps_total + 2)

            @block.scalar
            def _(act):
                def high_up(k, r):
                    if k % 2 == 0:
                        arrived(act, first + k // 2 * 2, r)
                    if k >= 2:
                        act.wait_ge(up_done.sem, shifted(r, body, up_done.at(k - 1)))
                    act.copy(up_hi[:, k % 2], up_weights(k)).then_inc(hi_up.sem, 1)

                def high_down(k, r):
                    if k % 2 == 0:
                        arrived(act, first + k // 2 * 2 + 1, r)
                    if k >= 2:
                        act.wait_ge(down_done.sem, shifted(r, body, down_done.at(k - 1)))
                    act.copy(down_hi[:, k % 2], down_weights(k)).then_inc(hi_down.sem, 1)

                def step(k, r):
                    if k >= 1:
                        high_down(k - 1, r)
                    if k + 1 < steps_total:
                        high_up(k + 1, r)
                    if k < steps_total:
                        act.wait_ge(up_done.sem, shifted(r, body, up_done.at(k + 1)))
                        if k >= 2:
                            act.wait_ge(made.sem, shifted(r, 3 * body, made.at(3 * k - 5)))
                        act.activation(silu_g[:, k % 2, :], ps[:, 4 + k % 2, 0:SEQ], ACT.Silu).then_inc(silued.sem, 1)

                high_up(0, 0)
                all_steps(act, step, steps_total + 1)

            @block.vector
            def _(dve):
                def low_up(k, r):
                    dve.wait_ge(hi_up.sem, shifted(r, body, hi_up.at(k + 1)))
                    dve.tensor_tensor(up_lo[:, k % 2], up_weights(k), up_hi[:, k % 2].bitcast(F32), ALU.subtract
                                      ).then_inc(lo_up.sem if k % 2 == 0 else used, 1)

                def low_down(k, r):
                    dve.wait_ge(hi_down.sem, shifted(r, body, hi_down.at(k + 1)))
                    dve.tensor_tensor(down_lo[:, k % 2], down_weights(k), down_hi[:, k % 2].bitcast(F32), ALU.subtract
                                      ).then_inc(lo_down.sem if k % 2 == 0 else used, 1)

                def hidden_parts(k, r):
                    f = k % 2
                    dve.wait_ge(silued.sem, shifted(r, body, silued.at(k + 1)))
                    dve.tensor_tensor(hidden[:, f, :], silu_g[:, f, :], ps[:, 4 + f, SEQ:2 * SEQ],
                                      ALU.mult).then_inc(made.sem, 1)
                    if k >= 2:
                        dve.wait_ge(down_done.sem, shifted(r, body, down_done.at(k - 1)))
                    dve.wait_ge(made.sem, shifted(r, 3 * body, made.at(3 * k + 1)))
                    dve.tensor_copy(hid_hi[:, f, :], hidden[:, f, :]).then_inc(made.sem, 1)
                    dve.wait_ge(made.sem, shifted(r, 3 * body, made.at(3 * k + 2)))
                    dve.tensor_tensor(hid_lo[:, f, :], hidden[:, f, :], hid_hi[:, f, :].bitcast(F32),
                                      ALU.subtract).then_inc(made.sem, 1)

                def step(k, r):
                    if k >= 1:
                        low_down(k - 1, r)
                    if k + 1 < steps_total:
                        low_up(k + 1, r)
                    if k < steps_total:
                        hidden_parts(k, r)

                low_up(0, 0)
                all_steps(dve, step, steps_total + 1)
                dve.wait_ge(down_done.sem, down_done.at(steps_total))
                for h in range(2):
                    for a in range(TILES):
                        cols = slice(h * BANK, (h + 1) * BANK)
                        dve.scalar_tensor_tensor(out=x[:, a, cols], in0=ps[:, 2 * h + a, :], scalar=0.5,
                                                 in1=x[:, a, cols], op0=ALU.mult, op1=ALU.add)
        for s in (hi_up, hi_down, up_done, down_done, silued):
            s.advance(steps_total)
        lo_up.advance(F_GROUPS), lo_down.advance(F_GROUPS), made.advance(3 * steps_total)

    rope_2 = sb("rope_2", TILES, 2, ROT_RET + ROT_MOBA)

    def position_tables():
        n = ROT_RET + ROT_MOBA
        mem = Arena()
        inv, angle, turns, absolute = mem.take(n), mem.take(TILES, n), mem.take(TILES, n), mem.take(TILES, n)
        pos_f = mem.take(TILES)
        pos_i = sb("positions", TILES, dtype=I32)
        reduced = signal("angles_reduced")
        two_pi = 2 * np.pi
        c1 = 6.28125
        c2 = float(np.float32(np.round((two_pi - c1) * 2 ** 20) / 2 ** 20))
        c3 = float(np.float32(two_pi - c1 - c2))
        magic = 1.5 * 2 ** 23
        with nc.Block() as block:
            @block.sync
            def _(sp):
                load_params(sp, (pos_i[:, :], t["positions_2"][0].rearrange("(a p) -> p a", p=P)),
                            (inv, spread(t["c_inv_freq"])))
                stream.issue(sp)
        with nc.Block() as block:
            @block.vector
            def _(dve):
                params_ready(dve)
                dve_chain.link(dve, dve.tensor_copy(pos_f, pos_i[:, :]))
                for a in range(TILES):
                    last = dve.tensor_scalar(angle[:, a, :], inv, pos_f[:, a:a + 1], None, ALU.mult)
                dve_chain.link(dve, last)
                dve_chain.link(dve, dve.tensor_scalar(turns, angle, 1.0 / two_pi, magic, ALU.mult, ALU.add))
                dve_chain.link(dve, dve.tensor_scalar(turns, turns, -magic, None, ALU.add))
                for c in (c1, c2, c3):
                    dve_chain.link(dve, dve.scalar_tensor_tensor(out=angle, in0=turns, scalar=-c, in1=angle,
                                                                 op0=ALU.mult, op1=ALU.add))
                dve.tensor_scalar(angle, angle, 3.1415925, -3.1415925, ALU.min, ALU.max).then_inc(reduced.sem, 1)

            @block.scalar
            def _(act):
                act.wait_ge(reduced.sem, reduced.at(1))
                act_chain.link(act, act.activation(absolute, angle, ACT.Abs))
                act.activation(rope_2[:, :, 1, :], angle, ACT.Sin)
                act.activation(rope_2[:, :, 0, :], absolute, ACT.Sin, scale=-1.0, bias=float(np.pi / 2))
        reduced.advance(1)

    def second_mixer(layer):
        mem = Arena()
        z = mem.take(TILES, IN_2)
        conv_mem = Arena(mem.at)
        decay = mem.take(RET_HEADS, TILES, SEQ)
        acc = mem.take(2, SEQ)
        conv_norm = mem.take(2, 2)
        assert mem.at <= PARTS_AT
        conv_pad = conv_mem.take(2, KERNEL - 1 + SEQ)
        taps = conv_mem.take(CONV_W)
        tap_cols = conv_mem.take(2, KERNEL + 1)
        qk_cols = mem.take(4 * RW // P, SEQ)
        after = mem.at
        scratch = mem.take(4, 2 * RET_HEADS * ROT_RET)
        moba_scratch = mem.take(TILES, 4, 2 * MOBA_HEADS * ROT_MOBA)
        centred, square, root = mem.take(2, SEQ), mem.take(2, SEQ), mem.take(2, SEQ)
        o_rq, o_rk, o_rv, o_rg = 0, RW, 2 * RW, 3 * RW
        o_mq = 4 * RW
        o_mv = o_mq + 2 * MW
        o_ca, o_cg = o_mv + MW, o_mv + MW + CONV_W
        n_chunks = 4 * RW // P
        starts = [o_rq + i * P for i in range(2 * RW // P)] + [o_mq + i * P for i in range(2 * MW // P)]
        gated, conv_turned, conv_kept, padded, tapped = (signal(s) for s in (
            "conv_gated", "conv_inputs_turned", "conv_inputs_kept", "conv_padding_cleared", "taps_added"))
        freed = signal("projection_kept")

        def conv_on_tensor(pe, k):
            if k != 2:
                return
            params_ready(pe)
            for c in range(2):
                pe.transpose(ps[:, 7, c * (KERNEL + 1):(c + 1) * (KERNEL + 1)],
                             taps[0:KERNEL + 1, c * P:(c + 1) * P], ident[0:KERNEL + 1, 0:KERNEL + 1])
            pe.wait_ge(gated.sem, gated.at(1))
            for c in range(2):
                for a in range(TILES):
                    last = pe.transpose(ps[:, 6, c * SEQ + a * P:c * SEQ + (a + 1) * P],
                                        z[:, a, o_ca + c * P:o_ca + (c + 1) * P], ident[:, :])
            last.then_inc(conv_turned.sem, 1)

        def conv_on_scalar(act, k):
            if k == 3:
                act.wait_ge(padded.sem, padded.at(1))
                act.wait_ge(conv_turned.sem, conv_turned.at(1))
                act.copy(tap_cols, ps[:, 7, 0:2 * (KERNEL + 1)].rearrange("p (c k) -> p c k", c=2))
                act.copy(conv_pad[:, :, KERNEL - 1:],
                         ps[:, 6, :].rearrange("p (c q) -> p c q", c=2)).then_inc(conv_kept.sem, 1)

        def conv_on_gpsimd(pool):
            pool.memset(conv_pad[:, :, 0:KERNEL - 1], 0.0).then_inc(padded.sem, 1)
            pool.wait_ge(freed.sem, freed.at(TILES))
            pool.tensor_tensor(z[:, :, o_ca:o_ca + CONV_W], z[:, :, o_ca:o_ca + CONV_W],
                               z[:, :, o_cg:o_cg + CONV_W], ALU.mult).then_inc(gated.sem, 1)

        def add_tap(dve, j):
            for c in range(2):
                if j > 0:
                    dve.wait_ge(tapped.sem, tapped.at(2 * j + c - 1))
                window = conv_pad[:, c, j:j + SEQ]
                if j == 0:
                    last = dve.tensor_scalar(acc[:, c, :], window, tap_cols[:, c, 0:1],
                                             tap_cols[:, c, KERNEL:KERNEL + 1], ALU.mult, ALU.add)
                else:
                    last = dve.scalar_tensor_tensor(out=acc[:, c, :], in0=window, scalar=tap_cols[:, c, j:j + 1],
                                                    in1=acc[:, c, :], op0=ALU.mult, op1=ALU.add)
                last.then_inc(tapped.sem, 1)

        def conv_on_vector(dve, k):
            per_half = 4
            if k == 4:
                dve.wait_ge(conv_kept.sem, conv_kept.at(1))
            for j in range(max(k - 4, 0) * per_half, min((k - 3) * per_half, KERNEL)):
                add_tap(dve, j)

        project(IN_2, z, leading=2 * CONV_W, banks=range(6), more_params=[
            (taps[0:KERNEL, :], t["conv_w_2"][layer]),
            (taps[KERNEL:KERNEL + 1, :], t["conv_b_2"][layer:layer + 1, :]),
            (conv_norm[:, 0, :], t["conv_ln_g_2"][layer].rearrange("(c p) -> p c", p=P)),
            (conv_norm[:, 1, :], t["conv_ln_b_2"][layer].rearrange("(c p) -> p c", p=P))],
            extra={"tensor": conv_on_tensor, "scalar": conv_on_scalar, "vector": conv_on_vector,
                   "gpsimd": conv_on_gpsimd},
            activated={o_ca: (CONV_W, ACT.Sigmoid), o_rg // BANK * BANK: (o_rg % BANK, ACT.Silu)})
        tapped.advance(2 * KERNEL)
        for s in (gated, conv_turned, conv_kept, padded):
            s.advance(1)

        turned, rotated_ret, rotated_moba = (signal(s) for s in (
            "columns_turned", "retention_heads_rotated", "block_heads_rotated"))
        means, centre_ready, sq, variances, rooted, scaled = (signal(s) for s in (
            "means_ready", "centred_ready", "squares_made", "variances_ready", "root_ready", "tokens_scaled"))
        with nc.Block() as block:
            @block.sync
            def _(sp):
                load_params(sp, (decay, t["c_decay"].rearrange("h a p q -> p h a q")))
                stream.issue(sp)

            def rotate_heads(engine, chain, a, offset, scratch, f0, n):
                nh = 2 * RET_HEADS
                view = z[:, a, offset:offset + nh * HD].rearrange("p (h d) -> p h d", d=HD)
                wide = [scratch[:, i, :].rearrange("p (h f) -> p h f", h=nh) for i in range(4)]
                cos, sin = (rope_2[:, a, i:i + 1, f0:f0 + n].broadcast_to([P, nh, n]) for i in range(2))
                return rotate(engine, view[:, :, 0:n], view[:, :, n:2 * n], cos, sin, wide, chain)

            @block.scalar
            def _(act):
                act.wait_ge(centre_ready.sem, centre_ready.at(1))
                act.activation(square, centred, ACT.Square).then_inc(sq.sem, 1)
                act.wait_ge(variances.sem, variances.at(1))
                act.activation(root, ps[:, 7, :].rearrange("p (c q) -> p c q", c=2), ACT.Sqrt,
                               bias=EPS).then_inc(rooted.sem, 1)
                for g in range(n_chunks // 2):
                    act.wait_ge(turned.sem, turned.at(g + 1))
                    act.copy(qk_cols[:, 2 * g:2 * g + 2, :], ps[:, g, :].rearrange("p (c q) -> p c q", c=2))
                params_ready(act)
                act.wait_ge(scaled.sem, scaled.at(1))
                for c in range(2):
                    act.activation(mix_cols[:, 2 * RW // P + c, :], centred[:, c, :], ACT.Silu,
                                   scale=conv_norm[:, 0, c:c + 1], bias=conv_norm[:, 1, c:c + 1])

            @block.vector
            def _(dve):
                dve.wait_ge(means.sem, means.at(1))
                dve.tensor_tensor(centred, acc, ps[:, 6, :].rearrange("p (c q) -> p c q", c=2),
                                  ALU.subtract).then_inc(centre_ready.sem, 1)
                for a in range(TILES):
                    last = rotate_heads(dve, dve_chain, a, o_rq, scratch, 0, ROT_RET)
                    if a + 1 < TILES:
                        dve_chain.link(dve, last)
                last.then_inc(rotated_ret.sem, 1)
                dve.wait_ge(rooted.sem, rooted.at(1))
                dve.wait_ge(centre_ready.sem, centre_ready.at(1))
                dve_chain.link(dve, dve.reciprocal(root, root))
                dve.tensor_tensor(centred, centred, root, ALU.mult).then_inc(scaled.sem, 1)

            @block.gpsimd
            def _(pool):
                for a in range(TILES):
                    last = rotate_heads(pool, pool_chain, a, o_mq, moba_scratch[:, a], ROT_RET, ROT_MOBA)
                last.then_inc(rotated_moba.sem, 1)

            @block.tensor
            def _(pe):
                pe.matmul(ps[:, 6, :], group_mean[:, :], acc.rearrange("p c q -> p (c q)"), start=True,
                          stop=True).then_inc(means.sem, 1)
                pe.wait_ge(sq.sem, sq.at(1))
                pe.matmul(ps[:, 7, :], group_mean[:, :], square.rearrange("p c q -> p (c q)"), start=True,
                          stop=True).then_inc(variances.sem, 1)
                for g in range(n_chunks // 2):
                    if g == 0:
                        pe.wait_ge(rotated_ret.sem, rotated_ret.at(1))
                    if g == 2 * RW // P // 2:
                        pe.wait_ge(rotated_moba.sem, rotated_moba.at(1))
                    for i in range(2):
                        off = starts[2 * g + i]
                        for a in range(TILES):
                            last = pe.transpose(ps[:, g, i * SEQ + a * P:i * SEQ + (a + 1) * P],
                                                z[:, a, off:off + P], ident[:, :])
                    last.then_inc(turned.sem, 1)
        turned.advance(n_chunks // 2)
        for s in (rotated_ret, rotated_moba, means, centre_ready, sq, variances, rooted, scaled):
            s.advance(1)

        mem = Arena(after)
        s_buf = mem.take(2, TILES, SEQ)
        y = mem.take(TILES, RW)
        squares = mem.take(TILES, RW)
        sums, roots = stat[:, 0:TILES * RET_HEADS], stat[:, 16:16 + TILES * RET_HEADS]
        scores, decayed, outs, squared, summed, rooted, normed, mixed = (signal(s) for s in (
            "scores_ready", "scores_decayed", "outputs_ready", "squares_made", "squares_summed", "root_ready",
            "outputs_normed", "outputs_turned"))
        rc = RW // P
        with nc.Block() as block:
            @block.sync
            def _(sp):
                stream.issue(sp)

            @block.tensor
            def _(pe):
                def score(h):
                    half = slice(h % 2 * HD, h % 2 * HD + HD)
                    if h >= 2:
                        pe.wait_ge(decayed.sem, decayed.at(h - 1))
                    for b in range(TILES):
                        last = pe.matmul(ps[:, h % 2, b * SEQ + b * P:(b + 1) * SEQ],
                                         qk_cols[half, rc + h // 2, b * P:(b + 1) * P],
                                         qk_cols[half, h // 2, b * P:SEQ], start=True, stop=True)
                    last.then_inc(scores.sem, 1)

                def sum_values(h):
                    pe.wait_ge(decayed.sem, decayed.at(h + 1))
                    for a in range(TILES):
                        for b in range(a + 1):
                            last = pe.matmul(ps[:, 4 + a, h * HD:(h + 1) * HD], s_buf[:, h % 2, b, a * P:(a + 1) * P],
                                             z[:, b, o_rv + h * HD:o_rv + (h + 1) * HD], start=b == 0, stop=b == a)
                    last.then_inc(outs.sem, 1)

                for i in range(RET_HEADS + 1):
                    if i < RET_HEADS:
                        score(i)
                    if i >= 1:
                        sum_values(i - 1)
                pe.wait_ge(normed.sem, normed.at(1))
                for c in range(rc):
                    for a in range(TILES):
                        last = pe.transpose(ps[:, 2 + c // 2, c % 2 * SEQ + a * P:c % 2 * SEQ + (a + 1) * P],
                                            y[:, a, c * P:(c + 1) * P], ident[:, :])
                last.then_inc(mixed.sem, 1)

            @block.vector
            def _(dve):
                params_ready(dve)
                for h in range(RET_HEADS):
                    dve.wait_ge(scores.sem, scores.at(h + 1))
                    if h >= 2:
                        dve.wait_ge(outs.sem, outs.at(h - 1))
                    for b in range(TILES):
                        last = dve.tensor_tensor(s_buf[:, h % 2, b, b * P:], ps[:, h % 2, b * SEQ + b * P:(b + 1) * SEQ],
                                                 decay[:, h, b, b * P:], ALU.mult)
                    last.then_inc(decayed.sem, 1)
                dve.wait_ge(squared.sem, squared.at(1))
                dve.tensor_reduce(sums.rearrange("p (a h) -> p a h", a=TILES),
                                  squares.rearrange("p a (h d) -> p a h d", d=HD), AX, ALU.add).then_inc(summed.sem, 1)
                dve.wait_ge(rooted.sem, rooted.at(1))
                for a in range(TILES):
                    root = roots[:, a * RET_HEADS:(a + 1) * RET_HEADS].rearrange("p (h u) -> p h u", u=1)
                    last = dve.tensor_tensor(y[:, a, :].rearrange("p (h d) -> p h d", d=HD),
                                             ps[:, 4 + a, 0:RW].rearrange("p (h d) -> p h d", d=HD),
                                             root.broadcast_to([P, RET_HEADS, HD]), ALU.mult)
                dve_chain.link(dve, last)
                dve.tensor_tensor(y, y, z[:, :, o_rg:o_rg + RW], ALU.mult).then_inc(normed.sem, 1)

            @block.scalar
            def _(act):
                act.wait_ge(outs.sem, outs.at(RET_HEADS))
                act.activation(squares, ps[:, 4:4 + TILES, 0:RW], ACT.Square).then_inc(squared.sem, 1)
                act.wait_ge(mixed.sem, mixed.at(1))
                act.copy(mix_cols[:, 0:2, :], ps[:, 2, :].rearrange("p (c q) -> p c q", c=2))
                act.copy(mix_cols[:, 2, :], ps[:, 3, 0:SEQ])

            @block.gpsimd
            def _(pool):
                pool.wait_ge(summed.sem, summed.at(1))
                inverse_root(pool, roots, sums, HD).then_inc(rooted.sem, 1)
        scores.advance(RET_HEADS), decayed.advance(RET_HEADS), outs.advance(RET_HEADS)
        squared.advance(1), summed.advance(1), rooted.advance(1), normed.advance(1), mixed.advance(1)

        half = lambda i: slice(i % 2 * HD, i % 2 * HD + HD)
        attention(MOBA_HEADS, lambda i: qk_cols[half(i), 2 * rc + i // 2, :],
                  lambda i: qk_cols[half(i), 3 * rc + i // 2, :],
                  lambda i, b: z[:, b, o_mv + i * HD:o_mv + (i + 1) * HD], RET_HEADS, HD ** -0.5, True, Arena(after))

        high = signal("mix_high_kept")
        job = PartedProducts(stream.take(2), D, x_hi, mix_lo, range(4))
        act_side, dve_side = mix_products(high, job)
        with nc.Block() as block:
            @block.sync
            def _(sp):
                stream.issue(sp)

            @block.tensor
            def _(pe):
                job.products(pe, 0), job.products(pe, 1)

            @block.scalar
            def _(act):
                act_side(act)

            @block.vector
            def _(dve):
                dve_side(dve)
                for h in range(2):
                    job.wait(dve, h)
                    for a in range(TILES):
                        cols = slice(h * BANK, (h + 1) * BANK)
                        dve.tensor_tensor(x[:, a, cols], x[:, a, cols], ps[:, 2 * h + a, :], ALU.add)
        job.close()
        high.advance(2)

    def final_norm():
        normed = Arena().take(TILES, D)
        sums, roots = stat[:, 0:TILES], stat[:, TILES:2 * TILES]
        squares, rooted, done, stored = (signal(s) for s in ("squares_summed", "root_ready", "tokens_scaled",
                                                            "output_stored"))
        with nc.Block() as block:
            @block.sync
            def _(sp):
                load_params(sp, (ln_params[:, 0, :], spread(t["final_norm_2"])))
                for a in range(TILES):
                    sp.wait_ge(done.sem, done.at(a + 1))
                    sp.dma_start(out[0, a * P:(a + 1) * P, :], normed[:, a, :]).then_inc(stored.sem, 16)
                sp.wait_ge(stored.sem, 16 * TILES)

            @block.scalar
            def _(act):
                for a in range(TILES):
                    last = act.activation(normed[:, a, :], x[:, a, :], ACT.Square, accum_out=sums[:, a:a + 1])
                last.then_inc(squares.sem, 1)

            @block.gpsimd
            def _(pool):
                pool.wait_ge(squares.sem, squares.at(1))
                inverse_root(pool, roots, sums, D).then_inc(rooted.sem, 1)

            @block.vector
            def _(dve):
                params_ready(dve)
                dve.wait_ge(rooted.sem, rooted.at(1))
                for a in range(TILES):
                    dve.scalar_tensor_tensor(out=normed[:, a, :], in0=x[:, a, :], scalar=roots[:, a:a + 1],
                                             in1=ln_params[:, 0, :], op0=ALU.mult, op1=ALU.mult).then_inc(done.sem, 1)

    h, base = even_mixer()
    gla(h, base)
    mix_out_norm()
    experts(0)
    odd_mixer()
    mix_out_norm()
    experts(1)
    position_tables()
    for layer in range(DEPTH):
        rms_columns(t["ffn1_norm_2"][layer])
        ffn()
        rms_columns(t["mix_norm_2"][layer])
        second_mixer(layer)
        rms_columns(t["ffn2_norm_2"][layer])
        ffn()
    final_norm()


INPUTS = ["x", "p", "w_in_even", "mla_q_norm", "w_uq", "mla_kv_norm", "w_ukv", "gla_gate_w_fwd", "gla_gate_b_fwd",
          "gla_gate_w_bwd", "gla_gate_b_bwd", "gla_norm", "w_in_odd", "gqa_q_norm", "gqa_k_norm", "w_o", "ln1_g",
          "ln1_b", "router_w", "w1", "w3", "w2", "ple_gate_w", "ple_gate_b", "ple_w", "ln2_g", "ln2_b",
          "positions_2", "ffn1_norm_2", "ffn1_wg_2", "ffn1_wu_2", "ffn1_wd_2", "mix_norm_2", "w_in_2", "conv_w_2",
          "conv_b_2", "conv_ln_g_2", "conv_ln_b_2", "w_out_2", "ffn2_norm_2", "ffn2_wg_2", "ffn2_wu_2", "ffn2_wd_2",
          "final_norm_2"]


def kernel(**inputs):
    import concourse.bacc as bacc
    from concourse.bass_utils import run_bass_kernel_spmd

    nc = bacc.Bacc("TRN2", target_bir_lowering=False, num_devices=1)
    arrays = {name: np.ascontiguousarray(inputs[name]) for name in INPUTS}
    arrays.update(shape_constants())
    tensors = {name: nc.dram_tensor(f"in_{name}", a.shape, mybir.dt.from_np(a.dtype), kind="ExternalInput").ap()
               for name, a in arrays.items()}
    out = nc.dram_tensor("out", (1, SEQ, D), F32, kind="ExternalOutput").ap()
    build_program(nc, tensors, out)
    result = run_bass_kernel_spmd(nc, [{f"in_{name}": a for name, a in arrays.items()}], core_ids=[0])
    return result.results[0]["out"]
```

```python
import concourse.bass as bass
import concourse.mybir as mybir
import numpy as np
from concourse.alu_op_type import AluOpType as ALU

F32 = mybir.dt.float32
BF16 = mybir.dt.bfloat16
I32 = mybir.dt.int32
F32R = mybir.dt.float32r
ACT = mybir.ActivationFunctionType
AX = mybir.AxisListType.X

P = 128
SEQ = 256
TILES = SEQ // P
D = 1024
DC = D // P
DEPTH = 2
EPS = 1e-6
ALPHA = (2.0 * DEPTH) ** 0.25
BANK = 512

Q_LORA, KV_LORA, ROPE_A = 256, 128, 32
MLA_HEADS, NOPE, V_DIM = 8, 64, 64
MLA_QK = NOPE + ROPE_A
GLA_HEADS, DK, DV, RANK, CHUNK = 4, 64, 128, 16, 64
N_CHUNKS = SEQ // CHUNK
GLA_WIDTH = GLA_HEADS * DK
GATE_NORM = 16.0
O_CQ = 0
O_CKV = O_CQ + Q_LORA
O_KPE = O_CKV + KV_LORA
O_GQ = O_KPE + ROPE_A
O_GK = O_GQ + GLA_HEADS * DK
O_GV = O_GK + GLA_HEADS * DK
O_LR = O_GV + GLA_HEADS * DV
O_GR = O_LR + 2 * RANK
EVEN_IN = O_GR + GLA_HEADS * DV
GQA_HEADS, KV_HEADS, HD = 16, 4, 64
ODD_IN = (GQA_HEADS + 2 * KV_HEADS) * HD
EXPERTS, FF, PLE_DIM = 16, 1024, 256
CAP = 2 * SEQ // EXPERTS
QUADS = 4
QW = FF // QUADS
RET_HEADS, MOBA_HEADS, CONV_W, KERNEL = 6, 6, 256, 31
RW, MW = RET_HEADS * HD, MOBA_HEADS * HD
IN_2 = 4 * RW + 3 * MW + 2 * CONV_W
D_FF = 2816
FG = 256
F_GROUPS = D_FF // FG
ROT_RET, ROT_MOBA = HD // 2, HD // 8

WEIGHT_SLOTS, SLOT = 6, 4096


def axial_tables(rot_dim):
    row = np.repeat(np.arange(SEQ // 64, dtype=np.float32), 64)
    col = np.tile(np.arange(64, dtype=np.float32), SEQ // 64)
    half = rot_dim // 2
    inv = (np.float32(10000.0) ** (-np.arange(0, half, 2, dtype=np.float32) / half)).astype(np.float32)
    ang = np.concatenate([row[:, None] * inv, col[:, None] * inv], axis=-1)
    return np.stack([np.cos(ang), np.sin(ang)], axis=1).astype(np.float32)


def shape_constants():
    m, l = np.arange(P)[:, None], np.arange(P)[None, :]
    same = (m // CHUNK) == (l // CHUNK)
    tri = np.stack([same & (m <= l), same & (m >= l), same & (m > l), same & (m < l)], axis=1)
    heads = np.arange(RET_HEADS, dtype=np.float32)
    log_gamma = np.log1p(-np.exp2(-5.0 - heads)).astype(np.float32)
    km, qc = np.arange(SEQ)[:, None], np.arange(SEQ)[None, :]
    rel = (qc - km).astype(np.float32)
    decay = np.where(rel >= 0, np.exp(log_gamma[:, None, None] * np.maximum(rel, 0.0)), 0.0) * HD ** -0.5
    ret_inv = np.float32(10000.0) ** (-np.linspace(0.0, 1.0, ROT_RET, dtype=np.float32))
    moba_inv = np.float32(500000.0) ** (-np.arange(ROT_MOBA, dtype=np.float32) / ROT_MOBA)
    f = np.float32
    return {
        "c_ident": np.eye(P, dtype=f),
        "c_chunk_masks": tri.astype(f),
        "c_rope_mla": axial_tables(ROPE_A),
        "c_rope_gqa": axial_tables(HD),
        "c_slots": np.arange(1, CAP + 1, dtype=f)[None, :],
        "c_causal": np.where(l <= m, 0.0, -1e30).astype(f),
        "c_decay": decay.astype(f).reshape(RET_HEADS, TILES, P, SEQ),
        "c_inv_freq": np.concatenate([ret_inv, moba_inv]).astype(f)[None, :],
        "c_group_mean": (((m // HD) == (l // HD)) / HD).astype(f),
    }


class Signal:

    def __init__(self, nc, name):
        self.sem = nc.alloc_semaphore(name)
        self.base = 0

    def at(self, n):
        return self.base + n

    def advance(self, n):
        self.base += n


class Chain:

    def __init__(self, nc, name):
        self.sem = nc.alloc_semaphore(name)
        self.steps = 0

    def link(self, engine, instruction):
        self.steps += 1
        instruction.then_inc(self.sem, 1)
        engine.wait_ge(self.sem, self.steps)


class WeightStream:

    def __init__(self, nc, ring):
        self.ring = ring
        self.arrived = [nc.alloc_semaphore(f"weights_arrived_{s}") for s in range(WEIGHT_SLOTS)]
        self.used = nc.alloc_semaphore("weights_used")
        self.units, self.value = [], []
        self.total = [0] * WEIGHT_SLOTS
        self.issued = self.taken = 0

    def add(self, loads, index, n_loads=1):
        slot = len(self.units) % WEIGHT_SLOTS
        self.total[slot] += 16 * n_loads
        self.units.append((loads, index))
        self.value.append(self.total[slot])

    def take(self, n):
        self.taken += n
        return self.taken - n

    def slot(self, u):
        return self.ring[:, u % WEIGHT_SLOTS, :]

    def load(self, sp, u, index):
        for dst, src in self.units[u][0](self.slot(u), index):
            sp.dma_start(dst, src).then_inc(self.arrived[u % WEIGHT_SLOTS], 16)

    def issue(self, sp):
        for u in range(self.issued, min(self.taken + WEIGHT_SLOTS, len(self.units))):
            if u >= WEIGHT_SLOTS:
                sp.wait_ge(self.used, u - WEIGHT_SLOTS + 1)
            self.load(sp, u, self.units[u][1])
            self.issued = u + 1

    def wait(self, pe, u):
        pe.wait_ge(self.arrived[u % WEIGHT_SLOTS], self.value[u])


def columns_of(w, n0, width):
    return w[:, n0:n0 + width].rearrange("(c p) n -> p c n", p=P)


def plan_weights(nc, stream, t):

    def matrix(w, n, leading=0):
        widths = [min(BANK, n - n0) for n0 in range(0, n, BANK)]
        for i, width in enumerate(widths):
            n0 = i * BANK - leading if i * BANK >= leading else n - leading + i * BANK

            def loads(slot, n0, width=width, w=w):
                rows = w.shape[0] // P
                dst = slot[:, 0:rows * width].rearrange("p (c n) -> p c n", c=rows)
                return [(dst, columns_of(w, n0, width))]

            stream.add(loads, n0)

    def up_projections(slot, _):
        uq = slot[:, 0:2 * MLA_HEADS * MLA_QK].rearrange("p (c n) -> p c n", c=2)
        ukv = slot[:, 2 * MLA_HEADS * MLA_QK:2 * MLA_HEADS * MLA_QK + D]
        return [(uq, t["w_uq"][0].rearrange("(c p) n -> p c n", p=P)), (ukv, t["w_ukv"][0])]

    def ple_projection(slot, layer):
        return [(slot[:, 0:2 * D].rearrange("p (c n) -> p c n", c=2),
                 t["ple_w"][layer].rearrange("(c p) n -> p c n", p=P))]

    def experts(layer):
        def half(name, which, by_rows):
            def loads(slot, e):
                w = t[name][layer, bass.ds(e, 1)].rearrange("e (c p) f -> p (e c) f", p=P)
                if by_rows:
                    c0 = which * DC // 2
                    return [(slot.rearrange("p (c f) -> p c f", c=DC // 2), w[:, c0:c0 + DC // 2, :])]
                return [(slot.rearrange("p (c f) -> p c f", c=DC), w[:, :, which * BANK:(which + 1) * BANK])]
            return loads

        parts = [half("w1", 0, True), half("w1", 1, True), half("w3", 0, True), half("w3", 1, True),
                 half("w2", 0, False), half("w2", 1, False)]
        for e in range(EXPERTS):
            for part in parts:
                stream.add(part, e)

    def ffn(which, layer):
        wg, wu, wd = (t[f"ffn{which}_{k}_2"] for k in ("wg", "wu", "wd"))

        def up(slot, f0):
            halves = slot.rearrange("p (h c f) -> p h c f", h=2, c=DC)
            return [(halves[:, h], w[layer, :, bass.ds(f0, FG)].rearrange("(c p) f -> p c f", p=P))
                    for h, w in enumerate((wg, wu))]

        def down(slot, f0):
            return [(slot[:, 0:2 * D].rearrange("p (c n) -> p c n", c=2),
                     wd[layer, bass.ds(f0, FG), :].rearrange("(c p) n -> p c n", p=P))]

        for i in range(F_GROUPS):
            stream.add(up, i * FG, 2)
            stream.add(down, i * FG)

    for layer in range(DEPTH):
        if layer % 2 == 0:
            matrix(t["w_in_even"][0], EVEN_IN)
            stream.add(up_projections, 0, 2)
        else:
            matrix(t["w_in_odd"][0], ODD_IN)
        matrix(t["w_o"][layer], D)
        matrix(t["ple_gate_w"][layer], D)
        stream.add(ple_projection, layer)
        experts(layer)
    for layer in range(DEPTH):
        ffn(1, layer)
        matrix(t["w_in_2"][layer], IN_2, 2 * CONV_W)
        matrix(t["w_out_2"][layer], D)
        ffn(2, layer)


def build_program(nc, t, out):
    address = {}

    def sb(name, *dims, dtype=F32):
        made = nc.alloc_sbuf_tensor(name, [P, *dims], dtype)
        address[name] = nc.sbuf_base - int(np.prod(dims)) * (2 if dtype == BF16 else 4)
        return made

    ring = sb("weight_ring", WEIGHT_SLOTS, SLOT)
    x = sb("x", TILES, D)
    x_cols = sb("x_cols", DC, SEQ)
    mix_cols = sb("mix_cols", DC, SEQ)
    ln_params = sb("ln_params", 2, D)
    ident = sb("ident", P)
    chunk_masks = sb("chunk_masks", 4, P)
    rope_mla = sb("rope_mla", TILES, 2, ROPE_A // 2)
    rope_gqa = sb("rope_gqa", TILES, 2, HD // 2)
    causal = sb("causal", P)
    group_mean = sb("group_mean", P)
    zeros_bf = sb("zeros_bf", BANK, dtype=BF16)
    half_power = sb("half_power", 32)
    norm_cols = sb("norm_cols", DC)
    routers = sb("routers", DEPTH, DC, EXPERTS)
    stat = sb("stat", 128)
    arena_size = 18296
    arena = sb("arena", arena_size)

    def over(name, below, word, *dims):
        return nc.alloc_sbuf_tensor_at(name, [P, *dims], F32R, offset=address[below] + 4 * word)

    HALF = DC // 2 * BANK
    PARTS_AT, GATE_LOW_AT = (arena_size - 4 * HALF) // 8 * 8, (arena_size - DC * SEQ) // 8 * 8

    x_hi, x_lo = over("x_hi", "x_cols", 0, DC, SEQ), over("x_lo", "mix_cols", 0, DC, SEQ)
    gate_parts = over("gate_hi", "mix_cols", 0, DC, SEQ), over("gate_lo", "arena", GATE_LOW_AT, DC, SEQ)
    mix_lo = over("mix_lo", "arena", 4096, DC, SEQ)
    w_parts, gate_w_parts = (tuple(over(f"{name}_{part}", "arena", at + i * 2 * HALF, 2, HALF)
                                   for i, part in enumerate(("hi", "lo")))
                             for name, at in (("w", PARTS_AT), ("gate_w", 0)))
    ONE_HOT_AT, REST_AT, ROUTER_AT = 12544, 8192, 15712
    rows_hi, rows_lo = over("rows_hi", "x_cols", 0, TILES, D), over("rows_lo", "arena", REST_AT, TILES, D)
    router_hi, router_lo = (over(f"router_{part}", "arena", ROUTER_AT + i * DC * EXPERTS, DC, EXPERTS)
                            for i, part in enumerate(("hi", "lo")))
    one_hot = over("one_hot", "arena", ONE_HOT_AT, TILES, EXPERTS * CAP)
    up_hi, up_lo = over("up_hi", "arena", 0, 2, 2, DC, P), over("up_lo", "arena", 4096, 2, 2, DC, P)
    down_hi, down_lo = over("down_hi", "arena", 8192, 2, D), over("down_lo", "arena", 10240, 2, D)
    hid_hi, hid_lo = over("hid_hi", "arena", 12288, 2, SEQ), over("hid_lo", "arena", 12800, 2, SEQ)
    ps = nc.alloc_psum_tensor("psum", [P, 8, BANK], F32)

    signals = {}

    def signal(name):
        if name not in signals:
            signals[name] = Signal(nc, name)
        return signals[name]

    dve_chain, act_chain, pool_chain = (Chain(nc, n) for n in ("dve_chain", "act_chain", "pool_chain"))
    stream = WeightStream(nc, ring)
    plan_weights(nc, stream, t)
    params = signal("params_loaded")
    setup_loaded = signal("setup_loaded")
    routers_loaded = signal("routers_loaded")
    params_count = [0]

    class Arena:

        def __init__(self, at=0):
            self.at = at

        def take(self, *dims):
            n = int(np.prod(dims))
            assert self.at + n <= arena_size, (self.at, n)
            flat = arena[:, self.at:self.at + n]
            self.at += n
            if len(dims) == 1:
                return flat
            names = "abcd"[:len(dims)]
            spec = f"p ({' '.join(names)}) -> p {' '.join(names)}"
            return flat.rearrange(spec, **dict(zip(names[1:], dims[1:])))

    def load_params(sp, *pairs):
        for dst, src in pairs:
            sp.dma_start(dst, src, allow_slow_non_contiguous=True).then_inc(params.sem, 16)
            params_count[0] += 16

    def setup_ready(engine):
        engine.wait_ge(setup_loaded.sem, 32)

    def params_ready(engine):
        engine.wait_ge(params.sem, params_count[0])

    def spread(row):
        return row.partition_broadcast(P) if len(row.shape) == 1 else row.broadcast_to([P, row.shape[-1]])

    with nc.Block() as block:
        @block.sync
        def _(sp):
            sp.dma_start(ident[:, :], t["c_ident"]).then_inc(setup_loaded.sem, 16)
            sp.dma_start(x[:, :, :], t["x"][0].rearrange("(a p) d -> p a d", p=P)).then_inc(setup_loaded.sem, 16)

        @block.gpsimd
        def _(pool):
            pool.memset(zeros_bf[:, :], 0.0)
            pool.memset(half_power[:, :], -0.5)

    def load_constants(sp):
        load_params(
            sp,
            (chunk_masks[:, :, :], t["c_chunk_masks"]),
            (rope_mla[:, :, :, :], t["c_rope_mla"].rearrange("(a p) k f -> p a k f", p=P)),
            (rope_gqa[:, :, :, :], t["c_rope_gqa"].rearrange("(a p) k f -> p a k f", p=P)),
            (causal[:, :], t["c_causal"]),
            (group_mean[:, :], t["c_group_mean"]),
        )
        for layer in range(DEPTH):
            sp.dma_start(routers[:, layer], t["router_w"][layer].rearrange("(c p) e -> p c e", p=P)
                         ).then_inc(routers_loaded.sem, 16)

    def column_steps(src, high, low, gain=None, root_diag=None, roots_ready=None):
        turned, kept = signal("columns_turned"), signal("columns_high_kept")

        def turn(pe):
            setup_ready(pe)
            if roots_ready is not None:
                pe.wait_ge(roots_ready.sem, roots_ready.at(1))
            for c in range(DC):
                for a in range(TILES):
                    dst = ps[:, c // 2, (c % 2) * SEQ + a * P:(c % 2) * SEQ + (a + 1) * P]
                    rows = src[:, a, c * P:(c + 1) * P]
                    if roots_ready is None:
                        last = pe.transpose(dst, rows, ident[:, :])
                    else:
                        last = pe.matmul(dst, rows, root_diag[:, a, :], start=True, stop=True)
                if c % 2:
                    last.then_inc(turned.sem, 1)

        def keep_high(act):
            if gain is not None:
                params_ready(act)
            for b in range(DC // 2):
                act.wait_ge(turned.sem, turned.at(b + 1))
                if gain is None:
                    last = act.copy(high[:, 2 * b:2 * b + 2, :], ps[:, b, :].rearrange("p (c q) -> p c q", c=2))
                else:
                    for c in (2 * b, 2 * b + 1):
                        last = act.activation(high[:, c, :], ps[:, b, c % 2 * SEQ:c % 2 * SEQ + SEQ], ACT.Copy,
                                              scale=gain[:, c:c + 1])
                last.then_inc(kept.sem, 1)

        def keep_low(dve):
            for b in range(DC // 2):
                dve.wait_ge(kept.sem, kept.at(b + 1))
                both = slice(2 * b, 2 * b + 2)
                bank = ps[:, b, :].rearrange("p (c q) -> p c q", c=2)
                if gain is None:
                    dve.tensor_tensor(low[:, both, :], bank, high[:, both, :].bitcast(F32), ALU.subtract)
                else:
                    for c in (2 * b, 2 * b + 1):
                        dve.scalar_tensor_tensor(out=low[:, c, :], in0=ps[:, b, c % 2 * SEQ:c % 2 * SEQ + SEQ],
                                                 scalar=gain[:, c:c + 1], in1=high[:, c, :].bitcast(F32),
                                                 op0=ALU.mult, op1=ALU.subtract)

        return turn, keep_high, keep_low

    def close_columns():
        signal("columns_turned").advance(DC // 2), signal("columns_high_kept").advance(DC // 2)

    def to_columns(src, high, low, first_high, first_low=None, first_params=(), more_params=()):
        turn, keep_high, keep_low = column_steps(src, high, low)
        with nc.Block() as block:
            @block.sync
            def _(sp):
                load_params(sp, *first_params)
                stream.issue(sp)
                load_params(sp, *more_params)

            @block.tensor
            def _(pe):
                turn(pe)

            @block.scalar
            def _(act):
                keep_high(act)
                first_high(act)

            @block.vector
            def _(dve):
                keep_low(dve)
                if first_low is not None:
                    first_low(dve)
        close_columns()

    class PartedProducts:

        def __init__(self, first, n, x_high, x_low, banks, parts=w_parts, freed=None,
                     x_made=None):
            self.first, self.n, self.x_high, self.x_low, self.banks, self.freed = first, n, x_high, x_low, banks, freed
            self.w_hi, self.w_lo = parts
            self.x_made = x_made
            self.units = -(-n // BANK)
            self.high, self.low, self.done = (signal(s) for s in ("weights_high_kept", "weights_low_kept",
                                                                  "half_products_done"))

        def width(self, i):
            return min(BANK, self.n - i * BANK)

        def raw(self, i, half):
            n = DC // 2 * self.width(i)
            return stream.slot(self.first + i)[:, half * n:(half + 1) * n]

        def part_high(self, act, i, half):
            k = 2 * i + half
            if half == 0:
                stream.wait(act, self.first + i)
            if k >= 2:
                act.wait_ge(self.done.sem, self.done.at(k - 1))
            src = self.raw(i, half)
            act.copy(self.w_hi[:, half, 0:src.shape[-1]], src).then_inc(self.high.sem, 1)

        def part_low(self, dve, i, half):
            src = self.raw(i, half)
            dve.wait_ge(self.high.sem, self.high.at(2 * i + half + 1))
            dve.tensor_tensor(self.w_lo[:, half, 0:src.shape[-1]], src, self.w_hi[:, half, 0:src.shape[-1]].bitcast(F32),
                              ALU.subtract).then_inc(self.low.sem if half == 0 else stream.used, 1)

        def first_high(self, act):
            self.part_high(act, 0, 0), self.part_high(act, 0, 1)

        def products(self, pe, i, only=None):
            width = self.width(i)
            for half in (range(2) if only is None else (only,)):
                high, low = (w[:, half, 0:DC // 2 * width].rearrange("p (c n) -> p c n", c=DC // 2) for w in
                             (self.w_hi, self.w_lo))
                for w_part, x_parts in ((high, (self.x_high, self.x_low)), (low, (self.x_high,))):
                    if w_part is high:
                        pe.wait_ge(self.high.sem, self.high.at(2 * i + half + 1))
                        if self.x_made is not None and i == 0:
                            pe.wait_ge(self.x_made.sem, self.x_made.at(half + 1))
                    elif half == 0:
                        pe.wait_ge(self.low.sem, self.low.at(i + 1))
                    else:
                        pe.wait_ge(stream.used, self.first + i + 1)
                    for a in range(TILES):
                        k = TILES * i + a
                        if self.freed is not None and half == 0 and w_part is high and k >= len(self.banks):
                            pe.wait_ge(self.freed.sem, self.freed.at(k - len(self.banks) + 1))
                        for c in range(DC // 2):
                            cc = half * DC // 2 + c
                            for x_part in x_parts:
                                last = pe.matmul(ps[:, self.banks[k % len(self.banks)], 0:width],
                                                 x_part[:, cc, a * P:(a + 1) * P], w_part[:, c, :],
                                                 start=cc == 0 and w_part is high and x_part is self.x_high,
                                                 stop=cc == DC - 1 and w_part is low)
                last.then_inc(self.done.sem, 1)

        def wait(self, engine, i):
            engine.wait_ge(self.done.sem, self.done.at(2 * i + 2))

        def close(self):
            self.high.advance(2 * self.units), self.low.advance(self.units), self.done.advance(2 * self.units)

    def projection(n, banks=range(8)):
        return PartedProducts(stream.taken, n, x_hi, x_lo, banks, freed=signal("projection_kept"))

    def project(job, dst, leading=0, extra=None, activated=None, more_loads=None):
        n, units, banks, freed = job.n, job.units, job.banks, job.freed
        stream.take(units)
        extra, activated = extra or {}, activated or {}
        nothing = lambda engine, k: None
        with nc.Block() as block:
            @block.sync
            def _(sp):
                stream.issue(sp)
                if more_loads is not None:
                    more_loads(sp)

            @block.tensor
            def _(pe):
                for k in range(2 * units):
                    job.products(pe, k // 2, k % 2)
                    extra.get("tensor", nothing)(pe, k)

            @block.scalar
            def _(act):
                def keep(i):
                    job.wait(act, i)
                    n0 = i * BANK - leading if i * BANK >= leading else n - leading + i * BANK
                    for a in range(TILES):
                        bank = ps[:, banks[(TILES * i + a) % len(banks)], 0:job.width(i)]
                        split, function = activated.get(n0, (0, None))
                        if function is None:
                            last = act.copy(dst[:, a, n0:n0 + job.width(i)], bank)
                        else:
                            act.copy(dst[:, a, n0:n0 + split], bank[:, 0:split])
                            last = act.activation(dst[:, a, n0 + split:n0 + job.width(i)], bank[:, split:], function)
                        last.then_inc(freed.sem, 1)

                for k in range(2 * units):
                    if k % 2 and k > 1:
                        keep(k // 2 - 1)
                    if k > 1:
                        job.part_high(act, k // 2, k % 2)
                    extra.get("scalar", nothing)(act, k)
                keep(units - 1)

            @block.vector
            def _(dve):
                for k in range(2 * units):
                    job.part_low(dve, k // 2, k % 2)
                    extra.get("vector", nothing)(dve, k)

            if "gpsimd" in extra:
                @block.gpsimd
                def _(pool):
                    extra["gpsimd"](pool)
        job.close()
        freed.advance(units * TILES)

    def inverse_root(pool, dst, sums, count):
        n = dst.shape[-1]
        pool_chain.link(pool, pool.tensor_scalar(dst, sums, 1.0 / count, EPS, ALU.mult, ALU.add))
        return pool.tensor_tensor(dst, dst, half_power[:, 0:n], ALU.pow)

    def rotate(engine, first, second, cos, sin, scratch, chain=dve_chain):
        fs, sc, fc, ss = scratch
        engine.tensor_tensor(fc, first, cos, ALU.mult)
        engine.tensor_tensor(ss, second, sin, ALU.mult)
        engine.tensor_tensor(fs, first, sin, ALU.mult)
        chain.link(engine, engine.tensor_tensor(sc, second, cos, ALU.mult))
        engine.tensor_tensor(first, fc, ss, ALU.subtract)
        return engine.tensor_tensor(second, fs, sc, ALU.add)

    def norm_stats(dve, y, stats, h, a):
        return dve.bn_stats(stats[:, a, 6 * h:6 * h + 6], y[:, a, h * BANK:(h + 1) * BANK])

    def layer_norm_steps(dve, y, stats, wanted, got, centred, updated=None):
        for a in range(TILES):
            last = dve.bn_aggr(stats[:, a, 12:14], stats[:, a, 0:12])
        last.then_inc(wanted.sem, 1)
        dve.wait_ge(wanted.sem, wanted.at(1))
        dve.wait_ge(got.sem, got.at(1))
        dve_chain.link(dve, dve.tensor_scalar(y[:, 0, :], y[:, 0, :], stats[:, 0, 12:13], stats[:, 0, 14:15],
                                              ALU.subtract, ALU.mult))
        for a in range(TILES):
            if a == 1:
                dve.wait_ge(centred.sem, centred.at(1))
            dve_chain.link(dve, dve.tensor_tensor(y[:, a, :], y[:, a, :], ln_params[:, 0, :], ALU.mult))
            last = dve.tensor_tensor(x[:, a, :], y[:, a, :], ln_params[:, 1, :], ALU.add)
            if updated is not None:
                last.then_inc(updated.sem, 1)

    def layer_norm_root(pool, stats, wanted, got):
        pool.wait_ge(wanted.sem, wanted.at(1))
        root = stats[:, :, 14:15]
        pool_chain.link(pool, pool.tensor_scalar(root, stats[:, :, 13:14], 1.0, EPS, ALU.mult, ALU.add))
        pool_chain.link(pool, pool.tensor_tensor(root, root, half_power[:, 0:TILES].rearrange(
            "p (a u) -> p a u", u=1), ALU.pow))
        pool_chain.link(pool, pool.tensor_tensor(stats[:, :, 15:16], root, stats[:, :, 12:13], ALU.mult))
        pool.tensor_scalar(stats[:, :, 15:16], stats[:, :, 15:16], -1.0, None, ALU.mult).then_inc(got.sem, 1)

    def layer_norm_centre(act, y, stats, got, centred):
        act.wait_ge(got.sem, got.at(1))
        act.activation(y[:, 1, :], y[:, 1, :], ACT.Identity, scale=stats[:, 1, 14:15],
                       bias=stats[:, 1, 15:16]).then_inc(centred.sem, 1)

    def mix_products(job):
        def act_side(act):
            for k in range(4):
                job.part_high(act, k // 2, k % 2)

        def dve_side(dve):
            for k in range(4):
                if k < 2:
                    chunks = slice(4 * k, 4 * k + 4)
                    dve_chain.link(dve, dve.tensor_copy(x_hi[:, chunks, :], mix_cols[:, chunks, :]))
                    dve.tensor_tensor(mix_lo[:, chunks, :], mix_cols[:, chunks, :], x_hi[:, chunks, :].bitcast(F32),
                                      ALU.subtract).then_inc(job.x_made.sem, 1)
                job.part_low(dve, k // 2, k % 2)

        return act_side, dve_side

    def mix_out_norm():
        wanted, got, centred = (signal(s) for s in ("root_wanted", "root_ready", "tile_centred"))
        job = PartedProducts(stream.take(2), D, x_hi, mix_lo, range(4), x_made=signal("mix_parts_made"))
        act_side, dve_side = mix_products(job)
        y = Arena().take(TILES, D)
        stats = stat[:, 0:32].rearrange("p (a k) -> p a k", a=TILES)
        with nc.Block() as block:
            @block.sync
            def _(sp):
                stream.issue(sp)

            @block.tensor
            def _(pe):
                job.products(pe, 0), job.products(pe, 1)

            @block.scalar
            def _(act):
                act_side(act)
                layer_norm_centre(act, y, stats, got, centred)

            @block.vector
            def _(dve):
                dve_side(dve)
                params_ready(dve)
                for h in range(2):
                    job.wait(dve, h)
                    cols = slice(h * BANK, (h + 1) * BANK)
                    for a in range(TILES):
                        last = dve.scalar_tensor_tensor(out=y[:, a, cols], in0=x[:, a, cols], scalar=ALPHA,
                                                        in1=ps[:, 2 * h + a, :], op0=ALU.mult, op1=ALU.add)
                    dve_chain.link(dve, last)
                    for a in range(TILES):
                        last = norm_stats(dve, y, stats, h, a)
                dve_chain.link(dve, last)
                layer_norm_steps(dve, y, stats, wanted, got, centred)

            @block.gpsimd
            def _(pool):
                layer_norm_root(pool, stats, wanted, got)
        job.close()
        job.x_made.advance(2), wanted.advance(1), got.advance(1), centred.advance(1)

    def attention(heads, q_of, k_of, v_of, mix_head, scale, masked, mem, beside=None):
        deep = 4
        nothing = lambda engine, step: None
        on_tensor, on_vector, on_scalar = ((beside.tensor, beside.vector, beside.scalar) if beside else
                                           (nothing, nothing, nothing))
        scores, norm, turned, kept, summed, stored = (signal(s) for s in (
            "scores_ready", "probs_ready", "probs_turned", "turned_kept", "values_summed", "values_kept"))
        peak, expd = signal("peaks_ready"), signal("exps_ready")
        e_buf = mem.take(deep, TILES, SEQ)
        pt_buf = mem.take(2, TILES, SEQ)
        small = mem.take(deep, TILES, 4)

        def keys(a):
            return (a + 1) * P if masked else SEQ

        with nc.Block() as block:
            @block.sync
            def _(sp):
                stream.issue(sp)

            @block.tensor
            def _(pe):
                def score(h):
                    if h >= deep:
                        pe.wait_ge(expd.sem, expd.at(TILES * (h - deep + 1)))
                    for a in range(TILES):
                        last = pe.matmul(ps[:, h % deep, a * SEQ:a * SEQ + keys(a)], q_of(h)[:, a * P:(a + 1) * P],
                                         k_of(h)[:, 0:keys(a)], start=True, stop=True)
                    last.then_inc(scores.sem, 1)

                def turn(h):
                    pe.wait_ge(norm.sem, norm.at(h + 1))
                    if h >= 2:
                        pe.wait_ge(kept.sem, kept.at(h - 1))
                    for b in range(TILES):
                        for a in range(b if masked else 0, TILES):
                            last = pe.transpose(ps[:, deep + h % 2, b * SEQ + a * P:b * SEQ + (a + 1) * P],
                                                e_buf[:, h % deep, a, b * P:(b + 1) * P], ident[:, :])
                    last.then_inc(turned.sem, 1)

                def sum_values(h):
                    pe.wait_ge(kept.sem, kept.at(h + 1))
                    if h >= 4:
                        pe.wait_ge(stored.sem, stored.at(h // 2 - 1))
                    half = slice((h % 2) * HD, (h % 2) * HD + HD)
                    for b in range(TILES):
                        lo = b * P if masked else 0
                        last = pe.matmul(ps[half, 6 + h // 2 % 2, lo:SEQ], v_of(h, b),
                                         pt_buf[:, h % 2, b, lo:SEQ], start=b == 0, stop=b == TILES - 1)
                    last.then_inc(summed.sem, 1)

                on_tensor(pe, -1)
                for i in range(heads + 3):
                    if i < heads:
                        score(i)
                    on_tensor(pe, i)
                    if 2 <= i < heads + 2:
                        turn(i - 2)
                    if i >= 3:
                        sum_values(i - 3)
                on_tensor(pe, None)

            @block.vector
            def _(dve):
                def peaks(h):
                    dve.wait_ge(scores.sem, scores.at(h + 1))
                    src = ps[:, h % deep, :].rearrange("p (a k) -> p a k", a=TILES)
                    if masked:
                        if h >= deep:
                            dve.wait_ge(turned.sem, turned.at(h - deep + 1))
                        dve.tensor_copy(e_buf[:, h % deep, 1, 0:P], src[:, 1, 0:P])
                        for a in range(TILES):
                            last = dve.tensor_tensor(e_buf[:, h % deep, a, a * P:(a + 1) * P],
                                                     src[:, a, a * P:(a + 1) * P], causal[:, :], ALU.add)
                        dve_chain.link(dve, last)
                        for a in range(TILES):
                            last = dve.tensor_reduce(small[:, h % deep, a, 0:1], e_buf[:, h % deep, a, 0:keys(a)], AX,
                                                     ALU.max)
                    else:
                        last = dve.tensor_reduce(small[:, h % deep, :, 0:1], src, AX, ALU.max)
                    dve_chain.link(dve, last)
                    dve.tensor_scalar(small[:, h % deep, :, 1:2], small[:, h % deep, :, 0:1], -scale, None,
                                      ALU.mult).then_inc(peak.sem, 1)

                def normalise(h):
                    dve.wait_ge(expd.sem, expd.at(TILES * (h + 1)))
                    dve_chain.link(dve, dve.reciprocal(small[:, h % deep, :, 3:4], small[:, h % deep, :, 2:3]))
                    for a in range(TILES):
                        last = dve.tensor_scalar(e_buf[:, h % deep, a, 0:keys(a)], e_buf[:, h % deep, a, 0:keys(a)],
                                                 small[:, h % deep, a, 3:4], None, ALU.mult)
                    last.then_inc(norm.sem, 1)

                on_vector(dve, -1)
                for i in range(heads + 1):
                    if i < heads:
                        peaks(i)
                    on_vector(dve, i)
                    if i >= 1:
                        normalise(i - 1)

            @block.scalar
            def _(act):
                def exps(h):
                    act.wait_ge(peak.sem, peak.at(h + 1))
                    if h >= deep:
                        act.wait_ge(turned.sem, turned.at(h - deep + 1))
                    for a in range(TILES):
                        src = e_buf[:, h % deep, a, 0:keys(a)] if masked else ps[:, h % deep, a * SEQ:(a + 1) * SEQ]
                        act.activation(e_buf[:, h % deep, a, 0:keys(a)], src, ACT.Exp,
                                       bias=small[:, h % deep, a, 1:2], scale=scale,
                                       accum_out=small[:, h % deep, a, 2:3]).then_inc(expd.sem, 1)

                def keep(h):
                    act.wait_ge(turned.sem, turned.at(h + 1))
                    if h >= 2:
                        act.wait_ge(summed.sem, summed.at(h - 1))
                    if masked:
                        act.copy(pt_buf[:, h % 2, 0, :], ps[:, deep + h % 2, 0:SEQ])
                        last = act.copy(pt_buf[:, h % 2, 1, P:SEQ], ps[:, deep + h % 2, SEQ + P:2 * SEQ])
                    else:
                        last = act.copy(pt_buf[:, h % 2, :, :],
                                        ps[:, deep + h % 2, :].rearrange("p (b q) -> p b q", b=TILES))
                    last.then_inc(kept.sem, 1)

                def store(h):
                    act.wait_ge(summed.sem, summed.at(h + 1))
                    act.copy(mix_cols[:, (mix_head + h) // 2, :], ps[:, 6 + h // 2 % 2, 0:SEQ]).then_inc(stored.sem, 1)

                on_scalar(act, -1)
                for i in range(heads + 4):
                    if i < heads:
                        exps(i)
                    if 2 <= i < heads + 2:
                        keep(i - 2)
                    if i >= 4 and (i - 4) % 2 == 1:
                        store(i - 4)
                on_scalar(act, None)

            if beside:
                @block.gpsimd
                def _(pool):
                    beside.gpsimd(pool)
        for s in (scores, norm, turned, kept, summed, peak):
            s.advance(heads)
        expd.advance(TILES * heads)
        stored.advance(heads // 2)

    def even_mixer():
        mem = Arena()
        h = mem.take(TILES, EVEN_IN)
        load = [(norm_cols[:, 0:2], t["mla_q_norm"][0].rearrange("(c p) -> p c", p=P)),
                (norm_cols[:, 2:3], t["mla_kv_norm"][0].rearrange("(c p) -> p c", p=P)),
                (ln_params[:, 0, :], spread(t["ln1_g"][0])), (ln_params[:, 1, :], spread(t["ln1_b"][0]))]
        job = projection(EVEN_IN)
        to_columns(x, x_hi, x_lo, job.first_high)

        def more_loads(sp):
            load_params(sp, *load)
            load_constants(sp)

        project(job, h, more_loads=more_loads)
        base = mem.at

        q = mem.take(TILES, MLA_HEADS, MLA_QK)
        kv = mem.take(TILES, MLA_HEADS, NOPE + V_DIM)
        k = mem.take(TILES, MLA_HEADS, MLA_QK)
        q_cols = mem.take(MLA_HEADS, SEQ)
        k_cols = mem.take(MLA_HEADS, SEQ)
        mem_att = mem.at
        gla_mem = Arena(arena_size - 2000)
        gate_w = gla_mem.take(2 * GLA_WIDTH)
        gla_gain = gla_mem.take(DV)
        lr_cols = gla_mem.take(SEQ)
        log_a = gla_mem.take(TILES, 2 * GLA_WIDTH)
        soft = x_cols[:, 0:TILES * 2, :].rearrange("p (a c) q -> p a (c q)", a=TILES)
        latent = mem.take(TILES, Q_LORA + KV_LORA)
        latent_cols = mem.take(3, SEQ)
        scratch = mem.take(4, TILES * MLA_HEADS * ROPE_A // 2)
        sums = stat[:, 0:4]
        roots = stat[:, 4:8]
        unit = stream.take(1)
        squared, rooted, scaled, turned, taken, ready, kept, qk_made = (signal(s) for s in (
            "squares_summed", "root_ready", "latents_scaled", "columns_turned", "latents_turned", "up_projected",
            "up_kept", "qk_heads_ready"))
        cleared, lr_turned, lr_kept, gate_logits, logits_taken, soft_made = (signal(s) for s in (
            "gate_weights_cleared", "gate_inputs_turned", "gate_inputs_kept", "gate_logits", "gate_logits_taken",
            "soft_parts"))
        with nc.Block() as block:
            @block.sync
            def _(sp):
                sp.wait_ge(cleared.sem, cleared.at(1))
                load_params(sp, (gate_w[0:RANK, 0:GLA_WIDTH], t["gla_gate_w_fwd"][0]),
                            (gate_w[RANK:2 * RANK, GLA_WIDTH:], t["gla_gate_w_bwd"][0]),
                            (gate_w[2 * RANK:2 * RANK + 1, 0:GLA_WIDTH], t["gla_gate_b_fwd"]),
                            (gate_w[2 * RANK:2 * RANK + 1, GLA_WIDTH:], t["gla_gate_b_bwd"]),
                            (gla_gain, spread(t["gla_norm"][0])))
                stream.issue(sp)

            @block.scalar
            def _(act):
                for a in range(TILES):
                    act.activation(latent[:, a, 0:Q_LORA], h[:, a, O_CQ:O_CQ + Q_LORA], ACT.Square,
                                   accum_out=sums[:, a:a + 1])
                    last = act.activation(latent[:, a, Q_LORA:], h[:, a, O_CKV:O_CKV + KV_LORA], ACT.Square,
                                          accum_out=sums[:, 2 + a:3 + a])
                last.then_inc(squared.sem, 1)
                act.wait_ge(rooted.sem, rooted.at(1))
                act.wait_ge(squared.sem, squared.at(1))
                for a in range(TILES):
                    act.activation(latent[:, a, 0:Q_LORA], h[:, a, O_CQ:O_CQ + Q_LORA], ACT.Copy,
                                   scale=roots[:, a:a + 1])
                    last = act.activation(latent[:, a, Q_LORA:], h[:, a, O_CKV:O_CKV + KV_LORA], ACT.Copy,
                                          scale=roots[:, 2 + a:3 + a])
                last.then_inc(scaled.sem, 1)
                params_ready(act)
                for c in range(3):
                    act.wait_ge(turned.sem, turned.at(c + 1))
                    last = act.activation(latent_cols[:, c, :], ps[:, c, 0:SEQ], ACT.Copy,
                                          scale=norm_cols[:, c:c + 1])
                last.then_inc(taken.sem, 1)
                act.wait_ge(logits_taken.sem, logits_taken.at(1))
                act_chain.link(act, act.activation(soft, soft, ACT.Exp, scale=-1.0))
                act.activation(soft, soft, ACT.Ln, bias=1.0).then_inc(soft_made.sem, 1)
                for a in range(TILES):
                    if a == 0:
                        act.wait_ge(ready.sem, ready.at(1))
                    else:
                        act.wait_ge(stream.used, unit + 1)
                    width = MLA_HEADS * MLA_QK // 2
                    for i in range(2):
                        act.copy(q[:, a, 4 * i:4 * i + 4, :],
                                 ps[:, 4 * a + i, 0:width].rearrange("p (h d) -> p h d", d=MLA_QK))
                    for i in range(2):
                        last = act.copy(kv[:, a, 4 * i:4 * i + 4, :],
                                        ps[:, 4 * a + 2 + i, :].rearrange("p (h d) -> p h d", d=NOPE + V_DIM))
                    last.then_inc(kept.sem, 1)
                for g in range(MLA_HEADS):
                    act.wait_ge(turned.sem, turned.at(3 + g + 1))
                    dst = (q_cols if g < 4 else k_cols)[0:MLA_QK, 2 * (g % 4):2 * (g % 4) + 2, :]
                    act.copy(dst, ps[0:MLA_QK, g, :].rearrange("p (h q) -> p h q", h=2))

            @block.gpsimd
            def _(pool):
                pool.memset(gate_w, 0.0).then_inc(cleared.sem, 1)
                pool.wait_ge(cleared.sem, cleared.at(1))
                pool_chain.link(pool, pool.memset(lr_cols[2 * RANK:2 * RANK + 1, :], 1.0))
                pool.wait_ge(squared.sem, squared.at(1))
                inverse_root(pool, roots[:, 0:2], sums[:, 0:2], Q_LORA)
                inverse_root(pool, roots[:, 2:4], sums[:, 2:4], KV_LORA).then_inc(rooted.sem, 1)

            @block.tensor
            def _(pe):
                for a in range(TILES):
                    last = pe.transpose(ps[0:2 * RANK, 7, a * P:(a + 1) * P], h[:, a, O_LR:O_LR + 2 * RANK],
                                        ident[:, :])
                last.then_inc(lr_turned.sem, 1)
                pe.wait_ge(scaled.sem, scaled.at(1))
                for c in range(3):
                    for a in range(TILES):
                        last = pe.transpose(ps[:, c, a * P:(a + 1) * P], latent[:, a, c * P:(c + 1) * P],
                                            ident[:, :])
                    last.then_inc(turned.sem, 1)
                params_ready(pe)
                pe.wait_ge(lr_kept.sem, lr_kept.at(1))
                for a in range(TILES):
                    last = pe.matmul(ps[:, 5 + a, :], lr_cols[0:2 * RANK + 1, a * P:(a + 1) * P],
                                     gate_w[0:2 * RANK + 1, :], start=True, stop=True)
                last.then_inc(gate_logits.sem, 1)
                pe.wait_ge(taken.sem, taken.at(1))
                stream.wait(pe, unit)
                w = stream.slot(unit)
                uq = w[:, 0:2 * MLA_HEADS * MLA_QK].rearrange("p (c n) -> p c n", c=2)
                ukv = w[:, 2 * MLA_HEADS * MLA_QK:2 * MLA_HEADS * MLA_QK + D]
                width = MLA_HEADS * MLA_QK // 2
                for a in range(TILES):
                    if a == 1:
                        pe.wait_ge(logits_taken.sem, logits_taken.at(1))
                    for i in range(2):
                        for c in range(2):
                            pe.matmul(ps[:, 4 * a + i, 0:width], latent_cols[:, c, a * P:(a + 1) * P],
                                      uq[:, c, i * width:(i + 1) * width], start=c == 0, stop=c == 1)
                    for i in range(2):
                        last = pe.matmul(ps[:, 4 * a + 2 + i, :], latent_cols[:, 2, a * P:(a + 1) * P],
                                         ukv[:, i * BANK:(i + 1) * BANK], start=True, stop=True)
                    last.then_inc(ready.sem if a == 0 else stream.used, 1)
                pe.wait_ge(qk_made.sem, qk_made.at(1))
                for g in range(MLA_HEADS):
                    src = q if g < 4 else k
                    for i in range(4):
                        hd, a = 2 * (g % 4) + i // 2, i % 2
                        last = pe.transpose(ps[0:MLA_QK, g, i * P:(i + 1) * P], src[:, a, hd, :], ident[:, :])
                    last.then_inc(turned.sem, 1)

            @block.vector
            def _(dve):
                half = ROPE_A // 2
                kpe = h[:, :, O_KPE:O_KPE + ROPE_A]
                small = [scratch[:, i, 0:TILES * half].rearrange("p (a f) -> p a f", a=TILES) for i in range(4)]
                dve.wait_ge(lr_turned.sem, lr_turned.at(1))
                dve.tensor_copy(lr_cols[0:2 * RANK, :], ps[0:2 * RANK, 7, 0:SEQ]).then_inc(lr_kept.sem, 1)
                params_ready(dve)
                dve_chain.link(dve, rotate(dve, kpe[:, :, 0:half], kpe[:, :, half:], rope_mla[:, :, 0, :],
                                           rope_mla[:, :, 1, :], small))
                for a in range(TILES):
                    dve.tensor_copy(k[:, a, :, NOPE:], kpe[:, a, :].rearrange("p (u r) -> p u r", u=1)
                                    .broadcast_to([P, MLA_HEADS, ROPE_A]))
                dve.wait_ge(gate_logits.sem, gate_logits.at(1))
                logits = ps[:, 5:5 + TILES, :]
                dve_chain.link(dve, dve.tensor_scalar(log_a, logits, 0.0, None, ALU.min))
                dve.scalar_tensor_tensor(out=soft, in0=log_a, scalar=-2.0, in1=logits, op0=ALU.mult,
                                         op1=ALU.add).then_inc(logits_taken.sem, 1)
                dve.wait_ge(soft_made.sem, soft_made.at(1))
                dve.tensor_tensor(log_a, log_a, soft, ALU.subtract)
                dve.wait_ge(kept.sem, kept.at(TILES))
                for a in range(TILES):
                    dve.tensor_copy(k[:, a, :, 0:NOPE], kv[:, a, :, 0:NOPE])
                for a in range(TILES):
                    wide = [scratch[:, i, 0:MLA_HEADS * half].rearrange("p (h f) -> p h f", h=MLA_HEADS)
                            for i in range(4)]
                    cos, sin = (rope_mla[:, a, i:i + 1, :].broadcast_to([P, MLA_HEADS, half]) for i in range(2))
                    last = rotate(dve, q[:, a, :, NOPE:NOPE + half], q[:, a, :, NOPE + half:], cos, sin, wide)
                    if a == 0:
                        dve_chain.link(dve, last)
                last.then_inc(qk_made.sem, 1)
        squared.advance(1), rooted.advance(1), scaled.advance(1), turned.advance(3 + MLA_HEADS)
        taken.advance(1), ready.advance(1), kept.advance(TILES), qk_made.advance(1)
        for s in (cleared, lr_turned, lr_kept, gate_logits, logits_taken, soft_made):
            s.advance(1)

        attention(MLA_HEADS, lambda i: q_cols[0:MLA_QK, i, :], lambda i: k_cols[0:MLA_QK, i, :],
                  lambda i, b: kv[:, b, i, NOPE:], 0, MLA_QK ** -0.5, False, Arena(mem_att))
        return h, base, log_a, gla_gain

    def gla(h, base, log_a, gain):
        mem = Arena(base)
        width, pairs = GLA_WIDTH, GLA_HEADS // 2
        up = mem.take(2, pairs, SEQ)
        down = mem.take(2, pairs, SEQ)
        tail = mem.take(TILES, 2, width)
        qk_cols = mem.take(2, pairs, SEQ)
        q_up = mem.take(2, pairs, SEQ)
        state = mem.take(2, pairs, N_CHUNKS, DV)
        o = mem.take(TILES, GLA_HEADS * DV)
        scrap = mem.take(DV)
        gate = mem.take(TILES, GLA_HEADS * DV)
        att = x_cols[:, :, :].rearrange("p c q -> p (c q)").rearrange("p (g i l) -> p g i l", g=4, i=4)
        sums, roots = stat[:, 0:8], stat[:, 8:16]
        turned, taken, cums, exps, scaled, tails = (signal(s) for s in (
            "columns_turned", "columns_taken", "decays_summed", "decay_factors", "columns_decayed",
            "decayed_keys"))
        silus, gains, ups, states, atts, masked, outs, squares, rooted, normed, mixed = (signal(s) for s in (
            "gates_activated", "gates_scaled", "updates_ready", "states_ready", "chunk_scores", "chunk_scores_masked",
            "chunk_outputs", "squares_summed", "root_ready", "outputs_normed", "outputs_turned"))
        updates = [(d, pr, hh, n) for par in (1, 0) for d in range(2) for pr in range(pairs) for hh in range(2)
                   for n in range(par, N_CHUNKS, 2) if n != (N_CHUNKS - 1 if d == 0 else 0)]
        with nc.Block() as block:
            @block.sync
            def _(sp):
                stream.issue(sp)

            @block.tensor
            def _(pe):
                for i, off in enumerate((O_GQ, O_GK)):
                    for pr in range(pairs):
                        for a in range(TILES):
                            last = pe.transpose(ps[:, 1 + i, pr * SEQ + a * P:pr * SEQ + (a + 1) * P],
                                                h[:, a, off + pr * P:off + (pr + 1) * P], ident[:, :])
                last.then_inc(turned.sem, 1)
                for d in range(2):
                    for pr in range(pairs):
                        for a in range(TILES):
                            last = pe.matmul(ps[:, 5 + d, pr * SEQ + a * P:pr * SEQ + (a + 1) * P],
                                             log_a[:, a, d * width + pr * P:d * width + (pr + 1) * P],
                                             chunk_masks[:, d, :], start=True, stop=True)
                    last.then_inc(cums.sem, 1)
                for a in range(TILES):
                    for d in range(2):
                        last = pe.matmul(ps[:, 7 * a, d * width:(d + 1) * width], chunk_masks[:, 2 + d, :],
                                         log_a[:, a, d * width:(d + 1) * width], start=True, stop=True)
                last.then_inc(cums.sem, 1)
                for d in range(2):
                    pe.wait_ge(scaled.sem, scaled.at(d + 1))
                    if d == 0:
                        pe.wait_ge(exps.sem, exps.at(3))
                    for hh in range(2):
                        half = slice(hh * DK, (hh + 1) * DK)
                        for pr in range(pairs):
                            for a in range(TILES):
                                last = pe.matmul(ps[:, 2 * d + hh, (2 * pr + a) * P:(2 * pr + a + 1) * P],
                                                 down[half, d, pr, a * P:(a + 1) * P],
                                                 q_up[half, d, pr, a * P:(a + 1) * P], start=True, stop=True)
                        last.then_inc(atts.sem, 1)
                pe.wait_ge(tails.sem, tails.at(1))
                for i, (d, pr, hh, n) in enumerate(updates):
                    if i == len(updates) // 2:
                        pe.wait_ge(masked.sem, masked.at(4))
                    half = slice(n % 2 * CHUNK, n % 2 * CHUNK + CHUNK)
                    hd = 2 * pr + hh
                    last = pe.matmul(ps[hh * DK:(hh + 1) * DK, 2 * d + pr + 4 * (n % 2), n // 2 * DV:n // 2 * DV + DV],
                                     tail[half, n // 2, d, hd * DK:(hd + 1) * DK],
                                     h[half, n // 2, O_GV + hd * DV:O_GV + (hd + 1) * DV], start=True, stop=True)
                last.then_inc(ups.sem, 1)
                pe.wait_ge(states.sem, states.at(1))
                for a in range(TILES):
                    for hd in range(GLA_HEADS):
                        pr, hh = hd // 2, hd % 2
                        bank = 4 + 2 * a + hh
                        cols = slice(pr * DV, (pr + 1) * DV)
                        inter = [(d, n) for d in range(2) for n in (2 * a, 2 * a + 1)
                                 if n != (0 if d == 0 else N_CHUNKS - 1)]
                        for d in range(2):
                            pe.matmul(ps[:, bank, cols], att[:, 2 * d + hh, 2 * pr + a, :],
                                      h[:, a, O_GV + hd * DV:O_GV + (hd + 1) * DV], start=d == 0, stop=False,
                                      skip_group_check=True)
                        for d, n in inter:
                            last = pe.matmul(ps[n % 2 * CHUNK:n % 2 * CHUNK + CHUNK, bank, cols],
                                             q_up[hh * DK:(hh + 1) * DK, d, pr, n * CHUNK:(n + 1) * CHUNK],
                                             state[hh * DK:(hh + 1) * DK, d, pr, n, :], start=False,
                                             stop=(d, n) == inter[-1], skip_group_check=True)
                last.then_inc(outs.sem, 1)
                pe.wait_ge(normed.sem, normed.at(1))
                for c in range(GLA_HEADS):
                    for a in range(TILES):
                        last = pe.transpose(ps[:, c // 2, c % 2 * SEQ + a * P:c % 2 * SEQ + (a + 1) * P],
                                            o[:, a, c * P:(c + 1) * P], ident[:, :])
                last.then_inc(mixed.sem, 1)

            @block.scalar
            def _(act):
                act.activation(gate, h[:, :, O_GR:O_GR + GLA_HEADS * DV], ACT.Silu).then_inc(silus.sem, 1)
                act.wait_ge(turned.sem, turned.at(1))
                act.activation(qk_cols[:, 0], ps[:, 1, :].rearrange("p (c q) -> p c q", c=pairs), ACT.Copy,
                               scale=DK ** -0.5)
                act.copy(qk_cols[:, 1], ps[:, 2, :].rearrange("p (c q) -> p c q", c=pairs)).then_inc(taken.sem, 1)
                for d in range(2):
                    act.wait_ge(cums.sem, cums.at(d + 1))
                    cum = ps[:, 5 + d, :].rearrange("p (c q) -> p c q", c=pairs)
                    act.activation(up[:, d], cum, ACT.Exp, scale=1.0 / GATE_NORM)
                    act.activation(down[:, d], cum, ACT.Exp, scale=-1.0 / GATE_NORM).then_inc(exps.sem, 1)
                act.wait_ge(cums.sem, cums.at(3))
                for a in range(TILES):
                    last = act.activation(tail[:, a], ps[:, 7 * a, :].rearrange("p (d f) -> p d f", d=2), ACT.Exp,
                                          scale=1.0 / GATE_NORM)
                last.then_inc(exps.sem, 1)
                act.wait_ge(outs.sem, outs.at(1))
                for a in range(TILES):
                    for hd in range(GLA_HEADS):
                        last = act.activation(scrap, ps[:, 4 + 2 * a + hd % 2, hd // 2 * DV:hd // 2 * DV + DV],
                                              ACT.Square, accum_out=sums[:, GLA_HEADS * a + hd:GLA_HEADS * a + hd + 1])
                        act_chain.link(act, last)
                act.copy(sums[:, 0:1], sums[:, 0:1]).then_inc(squares.sem, 1)
                act.wait_ge(mixed.sem, mixed.at(1))
                for c in range(0, GLA_HEADS, 2):
                    act.copy(mix_cols[:, 4 + c:6 + c, :], ps[:, c // 2, :].rearrange("p (c q) -> p c q", c=2))

            @block.gpsimd
            def _(pool):
                pool.wait_ge(squares.sem, squares.at(1))
                inverse_root(pool, roots, sums, DV).then_inc(rooted.sem, 1)

            @block.vector
            def _(dve):
                params_ready(dve)
                dve.wait_ge(silus.sem, silus.at(1))
                for a in range(TILES):
                    view = gate[:, a, :].rearrange("p (h e) -> p h e", e=DV)
                    dve.tensor_tensor(view, view, gain.rearrange("p (u e) -> p u e", u=1)
                                      .broadcast_to([P, GLA_HEADS, DV]), ALU.mult)
                dve.wait_ge(taken.sem, taken.at(1))
                for d in range(2):
                    dve.wait_ge(exps.sem, exps.at(d + 1))
                    dve.tensor_tensor(q_up[:, d], qk_cols[:, 0], up[:, d], ALU.mult)
                    dve.tensor_tensor(down[:, d], qk_cols[:, 1], down[:, d], ALU.mult).then_inc(scaled.sem, 1)
                dve.wait_ge(exps.sem, exps.at(3))
                for a in range(TILES):
                    for d in range(2):
                        last = dve.tensor_tensor(tail[:, a, d, :], tail[:, a, d, :], h[:, a, O_GK:O_GK + width],
                                                 ALU.mult)
                last.then_inc(tails.sem, 1)
                for g in range(4):
                    dve.wait_ge(atts.sem, atts.at(g + 1))
                    mask = chunk_masks[:, g // 2:g // 2 + 1, :].broadcast_to([P, 4, P])
                    dve.tensor_tensor(att[:, g], ps[:, g, :].rearrange("p (i l) -> p i l", i=4), mask,
                                      ALU.mult).then_inc(masked.sem, 1)
                dve.wait_ge(ups.sem, ups.at(1))
                order = {0: range(0, N_CHUNKS - 1), 1: range(N_CHUNKS - 1, 0, -1)}
                for step in range(N_CHUNKS - 1):
                    for d in range(2):
                        n = order[d][step]
                        nxt, end = (n + 1, (n + 1) * CHUNK - 1) if d == 0 else (n - 1, n * CHUNK)
                        for pr in range(pairs):
                            update = ps[:, 2 * d + pr + 4 * (n % 2), n // 2 * DV:n // 2 * DV + DV]
                            if step == 0:
                                last = dve.tensor_copy(state[:, d, pr, nxt, :], update)
                            else:
                                last = dve.scalar_tensor_tensor(
                                    out=state[:, d, pr, nxt, :], in0=state[:, d, pr, n, :],
                                    scalar=up[:, d, pr, end:end + 1], in1=update, op0=ALU.mult, op1=ALU.add)
                    if step < N_CHUNKS - 2:
                        dve_chain.link(dve, last)
                last.then_inc(states.sem, 1)
                dve.wait_ge(rooted.sem, rooted.at(1))
                for a in range(TILES):
                    for hd in range(GLA_HEADS):
                        cols = slice(hd * DV, (hd + 1) * DV)
                        last = dve.scalar_tensor_tensor(
                            out=o[:, a, cols], in0=ps[:, 4 + 2 * a + hd % 2, hd // 2 * DV:hd // 2 * DV + DV],
                            scalar=roots[:, GLA_HEADS * a + hd:GLA_HEADS * a + hd + 1], in1=gate[:, a, cols],
                            op0=ALU.mult, op1=ALU.mult)
                last.then_inc(normed.sem, 1)
        scaled.advance(2), cums.advance(3), exps.advance(3)
        for s in (turned, taken, tails, silus, ups, states, outs, squares, rooted,
                  normed, mixed):
            s.advance(1)
        atts.advance(4), masked.advance(4)

    def odd_mixer():
        mem = Arena()
        h = mem.take(TILES, ODD_IN)
        n_heads = GQA_HEADS + KV_HEADS
        gains = mem.take(2, HD)
        job = projection(ODD_IN)
        to_columns(x, x_hi, x_lo, job.first_high, more_params=[(gains[:, 0, :], spread(t["gqa_q_norm"][0])),
                                               (gains[:, 1, :], spread(t["gqa_k_norm"][0])),
                                               (ln_params[:, 0, :], spread(t["ln1_g"][1])),
                                               (ln_params[:, 1, :], spread(t["ln1_b"][1]))])
        q_cols = mem.take(GQA_HEADS // 2, SEQ)
        k_cols = mem.take(KV_HEADS, SEQ)
        mem_att = mem.at
        group_heads = [BANK // HD, BANK // HD, KV_HEADS]
        most = max(group_heads)
        squares = mem.take(TILES * most * HD)
        scratch = mem.take(4, TILES * most * HD // 2)
        assert mem.at <= PARTS_AT
        k_twice = mem.take(TILES, KV_HEADS, 2, HD)
        squared, summed, rooted, doubled, turned = (signal(s) for s in (
            "squares_made", "squares_summed", "root_ready", "k_heads_doubled", "columns_turned"))
        kept = job.freed

        def heads_of(g, view):
            return view[:, :, g * BANK:g * BANK + group_heads[g] * HD].rearrange("p a (h d) -> p a h d", d=HD)

        def stat_of(g, base):
            n = TILES * group_heads[g]
            return stat[:, base + 16 * g:base + 16 * g + n]

        def square_heads(act, g):
            if g > 0:
                act.wait_ge(summed.sem, summed.at(g))
            n = TILES * group_heads[g] * HD
            act.activation(squares[:, 0:n].rearrange("p (a h d) -> p a h d", a=TILES, d=HD), heads_of(g, h),
                           ACT.Square).then_inc(squared.sem, 1)

        def sum_heads(dve, g):
            n = TILES * group_heads[g]
            dve.wait_ge(squared.sem, squared.at(g + 1))
            dve.tensor_reduce(stat_of(g, 0), squares[:, 0:n * HD].rearrange("p (h d) -> p h d", d=HD), AX,
                              ALU.add).then_inc(summed.sem, 1)

        def root_heads(pool, g):
            pool.wait_ge(summed.sem, summed.at(g + 1))
            inverse_root(pool, stat_of(g, 64), stat_of(g, 0), HD).then_inc(rooted.sem, 1)

        def rotate_heads(dve, g):
            heads, n = heads_of(g, h), group_heads[g]
            root = stat_of(g, 64).rearrange("p (a h u) -> p a h u", a=TILES, u=1)
            which = 1 if g == 2 else 0
            gain = gains[:, which:which + 1, :].rearrange("p (u v) d -> p u v d", u=1)
            dve.wait_ge(rooted.sem, rooted.at(g + 1))
            dve_chain.link(dve, dve.tensor_tensor(heads, heads, root.broadcast_to([P, TILES, n, HD]), ALU.mult))
            dve_chain.link(dve, dve.tensor_tensor(heads, heads, gain.broadcast_to([P, TILES, n, HD]), ALU.mult))
            wide = [scratch[:, i, 0:TILES * n * HD // 2].rearrange("p (a h f) -> p a h f", a=TILES, h=n)
                    for i in range(4)]
            cos, sin = (rope_gqa[:, :, i:i + 1, :].broadcast_to([P, TILES, n, HD // 2]) for i in range(2))
            last = rotate(dve, heads[:, :, :, 0:HD // 2], heads[:, :, :, HD // 2:], cos, sin, wide)
            dve_chain.link(dve, last)
            return last

        def heads_on_scalar(act, k):
            if k in (3, 5):
                act.wait_ge(kept.sem, kept.at(TILES * (k // 2)))
                square_heads(act, k // 2 - 1)

        def heads_on_vector(dve, k):
            if k == 4:
                sum_heads(dve, 0)
            if k == 5:
                params_ready(dve)
                sum_heads(dve, 1)
                rotate_heads(dve, 0)
                rotate_heads(dve, 1)

        def heads_on_gpsimd(pool):
            root_heads(pool, 0), root_heads(pool, 1)

        project(job, h, extra={"scalar": heads_on_scalar, "vector": heads_on_vector, "gpsimd": heads_on_gpsimd})

        with nc.Block() as block:
            @block.sync
            def _(sp):
                stream.issue(sp)

            @block.scalar
            def _(act):
                square_heads(act, 2)
                for b in range((GQA_HEADS // 2 + KV_HEADS) // 2):
                    act.wait_ge(turned.sem, turned.at(b + 1))
                    dst = q_cols[:, 2 * b:2 * b + 2, :] if b < GQA_HEADS // 4 else \
                        k_cols[:, 2 * b - GQA_HEADS // 2:2 * b - GQA_HEADS // 2 + 2, :]
                    act.copy(dst, ps[:, b, :].rearrange("p (c q) -> p c q", c=2))

            @block.vector
            def _(dve):
                sum_heads(dve, 2)
                rotate_heads(dve, 2)
                for a in range(TILES):
                    last = dve.tensor_copy(k_twice[:, a], heads_of(2, h)[:, a].rearrange("p h (u d) -> p h u d", u=1)
                                           .broadcast_to([P, KV_HEADS, 2, HD]))
                last.then_inc(doubled.sem, 1)

            @block.gpsimd
            def _(pool):
                root_heads(pool, 2)

            @block.tensor
            def _(pe):
                for b in range((GQA_HEADS // 2 + KV_HEADS) // 2):
                    if b == GQA_HEADS // 4:
                        pe.wait_ge(doubled.sem, doubled.at(1))
                    for i in range(2):
                        c = 2 * b + i
                        for a in range(TILES):
                            src = h[:, a, c * P:(c + 1) * P] if c < GQA_HEADS // 2 else \
                                k_twice[:, a, c - GQA_HEADS // 2].rearrange("p u d -> p (u d)")
                            last = pe.transpose(ps[:, b, i * SEQ + a * P:i * SEQ + (a + 1) * P], src, ident[:, :])
                    last.then_inc(turned.sem, 1)
        for s in (squared, summed, rooted):
            s.advance(3)
        doubled.advance(1)
        turned.advance((GQA_HEADS // 2 + KV_HEADS) // 2)
        group = GQA_HEADS // KV_HEADS
        half = lambda i: slice(i % 2 * HD, i % 2 * HD + HD)
        attention(GQA_HEADS, lambda i: q_cols[half(i), i // 2, :], lambda i: k_cols[half(i), i // group, :],
                  lambda i, b: h[:, b, (n_heads + i // group) * HD:(n_heads + i // group + 1) * HD], 0, HD ** -0.5,
                  False, Arena(mem_att))

    rope_2 = sb("rope_2", TILES, 2, ROT_RET + ROT_MOBA)
    pos_i = sb("positions", TILES, dtype=I32)

    class PositionTables:

        def __init__(self, mem):
            n = ROT_RET + ROT_MOBA
            self.inv, self.pos_f = mem.take(n), mem.take(TILES)
            self.angle, self.turns, self.absolute = (mem.take(TILES, n) for _ in range(3))
            self.reduced = signal("angles_reduced")

        def load(self, sp):
            load_params(sp, (pos_i[:, :], t["positions_2"][0].rearrange("(a p) -> p a", p=P)),
                        (self.inv, spread(t["c_inv_freq"])))

        def reduce_angles(self, dve):
            two_pi = 2 * np.pi
            c1 = 6.28125
            c2 = float(np.float32(np.round((two_pi - c1) * 2 ** 20) / 2 ** 20))
            c3 = float(np.float32(two_pi - c1 - c2))
            magic = 1.5 * 2 ** 23
            angle, turns, pos_f = self.angle, self.turns, self.pos_f
            params_ready(dve)
            dve_chain.link(dve, dve.tensor_copy(pos_f, pos_i[:, :]))
            for a in range(TILES):
                last = dve.tensor_scalar(angle[:, a, :], self.inv, pos_f[:, a:a + 1], None, ALU.mult)
            dve_chain.link(dve, last)
            dve_chain.link(dve, dve.tensor_scalar(turns, angle, 1.0 / two_pi, magic, ALU.mult, ALU.add))
            dve_chain.link(dve, dve.tensor_scalar(turns, turns, -magic, None, ALU.add))
            for c in (c1, c2, c3):
                dve_chain.link(dve, dve.scalar_tensor_tensor(out=angle, in0=turns, scalar=-c, in1=angle,
                                                             op0=ALU.mult, op1=ALU.add))
            dve.tensor_scalar(angle, angle, 3.1415925, -3.1415925, ALU.min, ALU.max).then_inc(self.reduced.sem, 1)

        def sines(self, act):
            act.wait_ge(self.reduced.sem, self.reduced.at(1))
            act_chain.link(act, act.activation(self.absolute, self.angle, ACT.Abs))
            act.activation(rope_2[:, :, 1, :], self.angle, ACT.Sin)
            act.activation(rope_2[:, :, 0, :], self.absolute, ACT.Sin, scale=-1.0, bias=float(np.pi / 2))

    def experts(layer):
        mem = Arena()
        picked_cols = mem.take(DC, EXPERTS, CAP)
        spread_back = mem.take(EXPERTS, SEQ)
        assert mem.at == REST_AT
        rest = mem.take(TILES, D)
        tokens_now = mem.take(DC, CAP)
        back_now = mem.take(SEQ)
        silu_g = mem.take(QW)
        hidden = mem.take(QW)
        hidden_cols = mem.take(2, P)
        partial = mem.take(D)
        loop_end = mem.at
        assert loop_end == ONE_HOT_AT
        mem.take(TILES, EXPERTS * CAP)
        p_tokens = mem.take(TILES, PLE_DIM)
        p_cols = mem.take(2, SEQ)
        router = routers[:, layer]
        slots = mem.take(CAP)
        aff = mem.take(TILES, EXPERTS)
        slot_tokens = mem.take(TILES, EXPERTS)
        ones = mem.take(SEQ)
        left = mem.take(SEQ)
        chosen = mem.take(SEQ)
        rank = mem.take(SEQ)
        assert mem.at == ROUTER_AT and ROUTER_AT + 2 * DC * EXPERTS <= GATE_LOW_AT
        bias = Arena(loop_end - D).take(D)
        tops = stat[:, 32:64]
        gate_hi, gate_lo = gate_parts
        four_hot = [mix_cols[:, :, :].rearrange("p c q -> p (c q)"), Arena(GATE_LOW_AT).take(DC * SEQ)]
        four_hot = [v.rearrange("p (e j s) -> p e j s", e=EXPERTS, j=QUADS) for v in four_hot]

        job = PartedProducts(stream.taken, D, gate_hi, gate_lo, range(4, 8), gate_w_parts)
        router_high = signal("router_high_kept")

        def first_high(act):
            act.wait_ge(routers_loaded.sem, 16 * DEPTH)
            act.copy(router_hi[:, :, :], router).then_inc(router_high.sem, 1)
            job.first_high(act)

        def router_low(dve):
            dve.wait_ge(router_high.sem, router_high.at(1))
            dve.tensor_tensor(router_lo[:, :, :], router, router_hi[:, :, :].bitcast(F32), ALU.subtract)

        to_columns(x, gate_hi, gate_lo, first_high, router_low, first_params=[
            (p_tokens, t["p"][layer, 0].rearrange("(a p) d -> p a d", p=P)),
            (slots, spread(t["c_slots"])),
            (bias, spread(t["ple_gate_b"][layer:layer + 1, :])),
            (ln_params[:, 0, :], spread(t["ln2_g"][layer])), (ln_params[:, 1, :], spread(t["ln2_b"][layer]))])
        router_high.advance(1)

        stream.take(2)
        ple_unit = stream.take(1)
        logits, affs, turned, ranked, turned_back, hot, gathered, kept, four, spread_s = (signal(s) for s in (
            "logits_ready", "affinities_ready", "affinities_turned", "slots_ranked", "slots_turned", "one_hot_ready",
            "tokens_gathered", "gathered_kept", "four_hot_ready", "one_hot_turned"))
        logit_rows, logit_kept = signal("logit_rows_ready"), signal("logit_rows_kept")
        exped, maxed = signal("router_exps"), signal("router_max")
        ple_p, ple_pk, biased, ple_s, ple_v = (signal(s) for s in (
            "ple_inputs_turned", "ple_inputs_kept", "ple_gates_biased", "ple_gates_activated", "ple_values_ready"))
        rows_high = signal("rows_high_kept")
        spread_kept, ones_made = signal("one_hot_kept"), signal("ones_made")
        with nc.Block() as block:
            @block.sync
            def _(sp):
                stream.issue(sp)

            @block.tensor
            def _(pe):
                passes = ((router_hi, gate_hi), (router_hi, gate_lo), (router_lo, gate_hi))
                for c in range(DC):
                    for k, (w_part, x_part) in enumerate(passes):
                        last = pe.matmul(ps[0:EXPERTS, 0, 0:SEQ], w_part[:, c, :], x_part[:, c, :],
                                         start=c == 0 and k == 0, stop=c == DC - 1 and k == len(passes) - 1)
                last.then_inc(logit_rows.sem, 1)
                pe.wait_ge(logit_kept.sem, logit_kept.at(1))
                for a in range(TILES):
                    last = pe.transpose(ps[:, 3, a * EXPERTS:(a + 1) * EXPERTS], left[0:EXPERTS, a * P:(a + 1) * P],
                                        ident[0:EXPERTS, 0:EXPERTS])
                last.then_inc(logits.sem, 1)
                params_ready(pe)
                for c in range(2):
                    for a in range(TILES):
                        last = pe.transpose(ps[:, 1, c * SEQ + a * P:c * SEQ + (a + 1) * P],
                                            p_tokens[:, a, c * P:(c + 1) * P], ident[:, :])
                last.then_inc(ple_p.sem, 1)
                job.products(pe, 0, 0)
                pe.wait_ge(affs.sem, affs.at(1))
                for a in range(TILES):
                    last = pe.transpose(ps[0:EXPERTS, 2, a * P:(a + 1) * P], aff[:, a, :], ident[:, :])
                last.then_inc(turned.sem, 1)
                job.products(pe, 0, 1)
                job.products(pe, 1, 0)
                pe.wait_ge(ranked.sem, ranked.at(1))
                for a in range(TILES):
                    last = pe.transpose(ps[:, 3, a * EXPERTS:(a + 1) * EXPERTS], rank[0:EXPERTS, a * P:(a + 1) * P],
                                        ident[0:EXPERTS, 0:EXPERTS])
                last.then_inc(turned_back.sem, 1)
                job.products(pe, 1, 1)
                pe.wait_ge(hot.sem, hot.at(1))
                for c in range(DC):
                    if c >= 4:
                        pe.wait_ge(kept.sem, kept.at(c - 3))
                    for a in range(TILES):
                        for part in (rows_hi, rows_lo):
                            last = pe.matmul(ps[:, c % 4, :], part[:, a, c * P:(c + 1) * P], one_hot[:, a, :],
                                             start=a == 0 and part is rows_hi,
                                             stop=a == TILES - 1 and part is rows_lo)
                    last.then_inc(gathered.sem, 1)
                pe.wait_ge(four.sem, four.at(2))
                for g in range(EXPERTS // 2):
                    if g < 4:
                        pe.wait_ge(kept.sem, kept.at(DC - 3 + g))
                    else:
                        pe.wait_ge(spread_kept.sem, spread_kept.at(g - 3))
                    for i in range(2):
                        for a in range(TILES):
                            last = pe.transpose(ps[:, g % 4, i * SEQ + a * P:i * SEQ + (a + 1) * P],
                                                four_hot[a][:, 2 * g + i].rearrange("p j s -> p (j s)"), ident[:, :])
                    last.then_inc(spread_s.sem, 1)
                stream.wait(pe, ple_unit)
                pe.wait_ge(ple_pk.sem, ple_pk.at(1))
                w = stream.slot(ple_unit)[:, 0:2 * D].rearrange("p (c n) -> p c n", c=2)
                for h in range(2):
                    for a in range(TILES):
                        pe.wait_ge(biased.sem, biased.at(2 * h + a + 1))
                        for c in range(2):
                            last = pe.matmul(ps[:, 4 + 2 * h + a, :], p_cols[:, c, a * P:(a + 1) * P],
                                             w[:, c, h * BANK:(h + 1) * BANK], start=c == 0, stop=c == 1)
                        last.then_inc(stream.used if (h, a) == (1, 1) else ple_v.sem, 1)

            @block.scalar
            def _(act):
                act.copy(rows_hi[:, :, :], x[:, :, :]).then_inc(rows_high.sem, 1)
                act.wait_ge(maxed.sem, maxed.at(1))
                act.activation(aff, aff, ACT.Exp).then_inc(exped.sem, 1)
                act.wait_ge(ple_p.sem, ple_p.at(1))
                act.copy(p_cols, ps[:, 1, :].rearrange("p (c q) -> p c q", c=2)).then_inc(ple_pk.sem, 1)
                for half in range(2):
                    job.part_high(act, 1, half)
                for c in range(DC):
                    act.wait_ge(gathered.sem, gathered.at(c + 1))
                    act.copy(picked_cols[:, c], ps[:, c % 4, :].rearrange("p (e s) -> p e s", e=EXPERTS)
                             ).then_inc(kept.sem, 1)
                for g in range(EXPERTS // 2):
                    act.wait_ge(spread_s.sem, spread_s.at(g + 1))
                    act.copy(spread_back[:, 2 * g:2 * g + 2, :], ps[:, g % 4, :].rearrange("p (e q) -> p e q", e=2)
                             ).then_inc(spread_kept.sem, 1)
                for h in range(2):
                    for a in range(TILES):
                        act.wait_ge(biased.sem, biased.at(2 * h + a + 1))
                        cols = slice(h * BANK, (h + 1) * BANK)
                        act.activation(rest[:, a, cols], rest[:, a, cols], ACT.Sigmoid).then_inc(ple_s.sem, 1)

            @block.vector
            def _(dve):
                job.part_low(dve, 0, 0)
                dve.wait_ge(logit_rows.sem, logit_rows.at(1))
                dve.tensor_copy(left[0:EXPERTS, :], ps[0:EXPERTS, 0, 0:SEQ]).then_inc(logit_kept.sem, 1)
                dve.wait_ge(logits.sem, logits.at(1))
                lg = ps[:, 3, 0:TILES * EXPERTS].rearrange("p (a e) -> p a e", a=TILES)
                top, total = tops[:, 0:TILES], tops[:, TILES:2 * TILES]
                wide = lambda v: v.rearrange("p (a u) -> p a u", u=1).broadcast_to([P, TILES, EXPERTS])
                dve_chain.link(dve, dve.tensor_reduce(top, lg, AX, ALU.max))
                dve.tensor_tensor(aff, lg, wide(top), ALU.subtract).then_inc(maxed.sem, 1)
                dve.wait_ge(exped.sem, exped.at(1))
                dve_chain.link(dve, dve.tensor_reduce(total, aff, AX, ALU.add))
                dve_chain.link(dve, dve.reciprocal(total, total))
                dve.tensor_tensor(aff, aff, wide(total), ALU.mult).then_inc(affs.sem, 1)
                job.part_low(dve, 0, 1)
                dve.wait_ge(rows_high.sem, rows_high.at(1))
                dve.tensor_tensor(rows_lo[:, :, :], x[:, :, :], rows_hi[:, :, :].bitcast(F32), ALU.subtract)
                job.part_low(dve, 1, 0)
                dve.wait_ge(turned.sem, turned.at(1))
                dve_chain.link(dve, dve.tensor_copy(left[0:EXPERTS, :], ps[0:EXPERTS, 2, 0:SEQ]))
                for r in range(CAP // 8):
                    dve_chain.link(dve, dve.max(tops[0:EXPERTS, 8:16], left[0:EXPERTS, :]))
                    dve_chain.link(dve, dve.match_replace(out=left[0:EXPERTS, :], in_to_replace=tops[0:EXPERTS, 8:16],
                                                          in_values=left[0:EXPERTS, :], imm_value=-1.0))
                dve_chain.link(dve, dve.tensor_scalar(chosen[0:EXPERTS, :], left[0:EXPERTS, :], 0.0, None, ALU.is_lt))
                dve.wait_ge(ones_made.sem, ones_made.at(1))
                dve_chain.link(dve, dve.tensor_tensor_scan(rank[0:EXPERTS, :], ones[0:EXPERTS, :],
                                                           chosen[0:EXPERTS, :], 0.0, ALU.mult, ALU.add))
                dve.tensor_tensor(rank[0:EXPERTS, :], rank[0:EXPERTS, :], chosen[0:EXPERTS, :],
                                  ALU.mult).then_inc(ranked.sem, 1)
                job.part_low(dve, 1, 1)
                params_ready(dve)
                dve.wait_ge(turned_back.sem, turned_back.at(1))
                dve_chain.link(dve, dve.tensor_copy(
                    slot_tokens, ps[:, 3, 0:TILES * EXPERTS].rearrange("p (a e) -> p a e", a=TILES)))
                for a in range(TILES):
                    last = dve.tensor_tensor(one_hot[:, a, :].rearrange("p (e s) -> p e s", e=EXPERTS),
                                             slot_tokens[:, a].rearrange("p (e u) -> p e u", u=1)
                                             .broadcast_to([P, EXPERTS, CAP]),
                                             slots.rearrange("p (u s) -> p u s", u=1).broadcast_to([P, EXPERTS, CAP]),
                                             ALU.is_equal)
                last.then_inc(hot.sem, 1)
                dve.wait_ge(hot.sem, hot.at(1))
                job.wait(dve, 1)
                for a in range(TILES):
                    dve.tensor_tensor(four_hot[a],
                                      one_hot[:, a, :].bitcast(F32).rearrange("p (e u s) -> p e u s", e=EXPERTS, u=1)
                                      .broadcast_to([P, EXPERTS, QUADS, CAP]),
                                      aff[:, a].rearrange("p (e u v) -> p e u v", u=1, v=1)
                                      .broadcast_to([P, EXPERTS, QUADS, CAP]), ALU.mult).then_inc(four.sem, 1)
                dve.wait_ge(gathered.sem, gathered.at(DC))
                for h in range(2):
                    for a in range(TILES):
                        cols = slice(h * BANK, (h + 1) * BANK)
                        dve.tensor_tensor(rest[:, a, cols], bias[:, cols], ps[:, 4 + 2 * h + a, :],
                                          ALU.add).then_inc(biased.sem, 1)
                for h in range(2):
                    for a in range(TILES):
                        dve.wait_ge(ple_s.sem, ple_s.at(2 * h + a + 1))
                        if (h, a) == (1, 1):
                            dve.wait_ge(stream.used, ple_unit + 1)
                        else:
                            dve.wait_ge(ple_v.sem, ple_v.at(2 * h + a + 1))
                        last = dve.tensor_tensor(rest[:, a, h * BANK:(h + 1) * BANK],
                                                 rest[:, a, h * BANK:(h + 1) * BANK], ps[:, 4 + 2 * h + a, :], ALU.mult)

            @block.gpsimd
            def _(pool):
                pool.memset(ones, 1.0).then_inc(ones_made.sem, 1)
        for s in (logits, affs, turned, ranked, turned_back, hot, exped, ple_p, ple_pk, logit_rows, logit_kept):
            s.advance(1)
        job.close()
        rows_high.advance(1), maxed.advance(1), ones_made.advance(1), four.advance(2)
        biased.advance(4), ple_s.advance(4), ple_v.advance(3)
        gathered.advance(DC), kept.advance(DC), spread_s.advance(EXPERTS // 2), spread_kept.advance(EXPERTS // 2)

        first = stream.take(6 * EXPERTS)
        assert stream.issued == first + WEIGHT_SLOTS
        token_set, back_set, silued, hid, h_turned, h_kept, part_0, part_1 = (signal(s) for s in (
            "expert_tokens_set", "scatter_rows_set", "expert_gates_activated", "expert_hidden_ready",
            "expert_hidden_turned", "expert_hidden_kept", "partial_0_kept", "partial_1_kept"))
        used = stream.used
        hc = hidden_cols
        tables = PositionTables(Arena(loop_end)) if layer == 0 else None
        with nc.Block() as block:
            @block.sync
            def _(sp):
                if tables:
                    tables.load(sp)
                with sp.Fori(0, EXPERTS - 1) as e:
                    for k in range(6):
                        sp.wait_ge(used, e * 6 + (first + k + 1))
                        stream.load(sp, first + k, e + 1)
                stream.issued = first + 6 * EXPERTS
                stream.issue(sp)

            @block.tensor
            def _(pe):
                for b in range(4):
                    pe.matmul(ps[:, b, :], zeros_bf[:, 0:P], zeros_bf[:, :], start=True, stop=False,
                              skip_group_check=True)
                with pe.Fori(0, EXPERTS) as e:
                    pe.wait_ge(token_set.sem, e + token_set.at(1))
                    for k in range(4):
                        u = first + k
                        w = stream.slot(u).rearrange("p (c f) -> p c f", c=DC // 2)
                        pe.wait_ge(stream.arrived[u % WEIGHT_SLOTS], e * 16 + stream.value[u])
                        for c in range(DC // 2):
                            cc = k % 2 * DC // 2 + c
                            for j in range(QUADS):
                                last = pe.matmul(ps[j * CAP:(j + 1) * CAP, 4 + k // 2, 0:QW], tokens_now[:, cc, :],
                                                 w[:, c, j * QW:(j + 1) * QW], start=cc == 0, stop=cc == DC - 1)
                        last.then_inc(used, 1)
                    pe.wait_ge(hid.sem, e + hid.at(1))
                    for i in range(2):
                        last = pe.transpose(ps[:, 4, i * P:(i + 1) * P], hidden[:, i * P:(i + 1) * P], ident[:, :])
                    last.then_inc(h_turned.sem, 1)
                    pe.wait_ge(h_kept.sem, e + h_kept.at(1))
                    for h in range(2):
                        u = first + 4 + h
                        w = stream.slot(u).rearrange("p (c f) -> p c f", c=DC)
                        pe.wait_ge(stream.arrived[u % WEIGHT_SLOTS], e * 16 + stream.value[u])
                        for i in range(2):
                            for j in range(QUADS):
                                last = pe.matmul(ps[j * CAP:(j + 1) * CAP, 6 + h, :], hc[:, i, j * CAP:(j + 1) * CAP],
                                                 w[:, 2 * j + i, :], start=i == 0, stop=i == 1)
                        last.then_inc(used, 1)
                    pe.wait_ge(back_set.sem, e + back_set.at(1))
                    for h, part in enumerate((part_0, part_1)):
                        pe.wait_ge(part.sem, e + part.at(1))
                        for a in range(TILES):
                            pe.matmul(ps[:, 2 * h + a, :], back_now[:, a * P:(a + 1) * P],
                                             partial[:, h * BANK:(h + 1) * BANK], start=False, stop=False,
                                             skip_group_check=True)

            @block.scalar
            def _(act):
                if tables:
                    tables.sines(act)
                with act.Fori(0, EXPERTS) as e:
                    act.wait_ge(used, e * 6 + (first + 2))
                    act.activation(silu_g, ps[:, 4, 0:QW], ACT.Silu).then_inc(silued.sem, 1)
                    act.wait_ge(h_turned.sem, e + h_turned.at(1))
                    act.copy(hc, ps[:, 4, 0:2 * P].rearrange("p (i q) -> p i q", i=2)).then_inc(h_kept.sem, 1)
                    act.wait_ge(used, e * 6 + (first + 5))
                    act.copy(partial[:, 0:BANK], ps[:, 6, :]).then_inc(part_0.sem, 1)

            @block.vector
            def _(dve):
                for a in range(TILES):
                    dve.scalar_tensor_tensor(out=rest[:, a, :], in0=x[:, a, :], scalar=ALPHA, in1=rest[:, a, :],
                                             op0=ALU.mult, op1=ALU.add)
                if tables:
                    tables.reduce_angles(dve)
                with dve.Fori(0, EXPERTS) as e:
                    dve.wait_ge(silued.sem, e + silued.at(1))
                    dve.wait_ge(used, e * 6 + (first + 4))
                    dve.tensor_tensor(hidden, silu_g, ps[:, 5, 0:QW], ALU.mult).then_inc(hid.sem, 1)
                    dve.wait_ge(used, e * 6 + (first + 6))
                    dve.tensor_copy(partial[:, BANK:], ps[:, 7, :]).then_inc(part_1.sem, 1)

            @block.gpsimd
            def _(pool):
                with pool.Fori(0, EXPERTS) as e:
                    pool.wait_ge(used, e * 6 + (first - 2))
                    pool.tensor_copy(tokens_now.rearrange("p c (u s) -> p c u s", u=1),
                                     picked_cols[:, :, bass.ds(e, 1), :]).then_inc(token_set.sem, 1)
                    pool.wait_ge(used, e * 6 + (first + 1))
                    pool.tensor_copy(back_now.rearrange("p (u q) -> p u q", u=1),
                                     spread_back[:, bass.ds(e, 1), :]).then_inc(back_set.sem, 1)
        for s in (token_set, back_set, silued, hid, h_turned, h_kept, part_0, part_1):
            s.advance(EXPERTS)

        if tables:
            tables.reduced.advance(1)

        wanted, got, centred = signal("root_wanted"), signal("root_ready"), signal("tile_centred")
        updated = signal("tiles_updated") if layer == DEPTH - 1 else None
        stats = stat[:, 0:32].rearrange("p (a k) -> p a k", a=TILES)
        with nc.Block() as block:
            @block.sync
            def _(sp):
                stream.issue(sp)

            @block.vector
            def _(dve):
                params_ready(dve)
                for h in range(2):
                    for a in range(TILES):
                        cols = slice(h * BANK, (h + 1) * BANK)
                        last = dve.tensor_tensor(rest[:, a, cols], rest[:, a, cols], ps[:, 2 * h + a, :], ALU.add)
                dve_chain.link(dve, last)
                for h in range(2):
                    for a in range(TILES):
                        last = norm_stats(dve, rest, stats, h, a)
                dve_chain.link(dve, last)
                layer_norm_steps(dve, rest, stats, wanted, got, centred, updated)

            @block.scalar
            def _(act):
                layer_norm_centre(act, rest, stats, got, centred)
                if updated is not None:
                    sum_squares(act, updated)

            @block.gpsimd
            def _(pool):
                layer_norm_root(pool, stats, wanted, got)
        wanted.advance(1), got.advance(1), centred.advance(1)
        if updated is not None:
            updated.advance(TILES)

    square_sums, square_roots = stat[:, 112:112 + TILES], stat[:, 114:114 + TILES]

    def sum_squares(act, updated):
        for a in range(TILES):
            act.wait_ge(updated.sem, updated.at(a + 1))
            act.activation(Arena(a * D).take(D), x[:, a, :], ACT.Square, accum_out=square_sums[:, a:a + 1])

    def rms_columns(gain_row, diag_at, first_high, more_params=()):
        root_diag = Arena(diag_at).take(TILES, P)
        rooted, spread_out = signal("root_ready"), signal("root_diagonals_ready")
        turn, keep_high, keep_low = column_steps(x, x_hi, x_lo, gain=norm_cols, root_diag=root_diag,
                                               roots_ready=spread_out)
        with nc.Block() as block:
            @block.sync
            def _(sp):
                load_params(sp, (norm_cols[:, :], gain_row.rearrange("(c p) -> p c", p=P)), *more_params)
                stream.issue(sp)

            @block.tensor
            def _(pe):
                turn(pe)

            @block.scalar
            def _(act):
                first_high(act)
                keep_high(act)

            @block.vector
            def _(dve):
                dve.wait_ge(rooted.sem, rooted.at(1))
                for a in range(TILES):
                    last = dve.tensor_scalar(root_diag[:, a, :], ident[:, :], square_roots[:, a:a + 1], None, ALU.mult)
                last.then_inc(spread_out.sem, 1)
                keep_low(dve)

            @block.gpsimd
            def _(pool):
                inverse_root(pool, square_roots, square_sums, D).then_inc(rooted.sem, 1)
        rooted.advance(1), spread_out.advance(1)
        close_columns()

    def ffn(gain_row):
        mem = Arena(13312)
        silu_g = mem.take(2, SEQ)
        hidden = mem.take(2, SEQ)
        steps_total = 2 * F_GROUPS
        first = stream.taken
        used = stream.used
        updated = signal("tiles_updated")
        names = ("up_high_kept", "up_low_kept", "down_high_kept", "down_low_kept", "up_products_ready",
                 "down_products_done", "ffn_gates_activated", "hidden_parts_made")
        hi_up, lo_up, hi_down, lo_down, up_done, down_done, silued, made = (signal(n) for n in names)
        body = WEIGHT_SLOTS
        trips = (steps_total - 4) // body
        assert trips * body == steps_total - 4

        def shifted(r, per_trip, value):
            return value if isinstance(r, int) else r * per_trip + value

        def up_weights(k):
            slot = stream.slot(first + k // 2 * 2).rearrange("p (h c f) -> p h c f", h=2, c=DC)
            return slot[:, :, :, k % 2 * P:k % 2 * P + P]

        def down_weights(k):
            return stream.slot(first + k // 2 * 2 + 1)[:, k % 2 * D:(k % 2 + 1) * D]

        def arrived(engine, u, r):
            value = stream.value[u]
            step = stream.value[u + WEIGHT_SLOTS] - value if u + WEIGHT_SLOTS < first + 2 * F_GROUPS else 0
            engine.wait_ge(stream.arrived[u % WEIGHT_SLOTS], shifted(r, step, value))

        def first_high(act):
            stream.wait(act, first)
            act.copy(up_hi[:, 0], up_weights(0)).then_inc(hi_up.sem, 1)

        rms_columns(gain_row, arena_size - TILES * P, first_high)
        stream.take(2 * F_GROUPS)
        assert stream.issued == first + WEIGHT_SLOTS

        def all_steps(engine, step, last):
            step(0, 0), step(1, 0)
            with engine.Fori(0, trips) as r:
                for k in range(2, 2 + body):
                    step(k, r)
            for k in range(2 + trips * body, last):
                step(k, 0)

        with nc.Block() as block:
            @block.sync
            def _(sp):
                def reload(u, r):
                    sp.wait_ge(used, r * WEIGHT_SLOTS + (u - WEIGHT_SLOTS + 1))
                    for dst, src in stream.units[u][0](stream.slot(u), r * (WEIGHT_SLOTS // 2 * FG) + stream.units[u][1]):
                        sp.dma_start(dst, src).then_inc(stream.arrived[u % WEIGHT_SLOTS], 16)

                loads = (2 * F_GROUPS - WEIGHT_SLOTS) // WEIGHT_SLOTS
                with sp.Fori(0, loads) as r:
                    for k in range(WEIGHT_SLOTS):
                        reload(first + WEIGHT_SLOTS + k, r)
                stream.issued = first + WEIGHT_SLOTS * (loads + 1)
                stream.issue(sp)

            @block.tensor
            def _(pe):
                for b in range(4):
                    pe.matmul(ps[:, b, :], zeros_bf[:, 0:P], zeros_bf[:, :], start=True, stop=False,
                              skip_group_check=True)

                def down(k, r):
                    f = k % 2
                    if f == 0:
                        pe.wait_ge(lo_down.sem, shifted(r, body // 2, lo_down.at(k // 2 + 1)))
                    else:
                        pe.wait_ge(used, shifted(r, body, first + k // 2 * 2 + 2))
                    pe.wait_ge(made.sem, shifted(r, 3 * body, made.at(3 * k + 3)))
                    for a in range(TILES):
                        rows = slice(a * P, (a + 1) * P)
                        for x_part, w_part in ((hid_hi, down_hi), (hid_hi, down_lo), (hid_lo, down_hi)):
                            for h in range(2):
                                last = pe.matmul(ps[:, 2 * h + a, :], x_part[:, f, rows],
                                                 w_part[:, f, h * BANK:(h + 1) * BANK], start=False, stop=False,
                                                 skip_group_check=True)
                    last.then_inc(down_done.sem, 1)

                def up(k, r):
                    f = k % 2
                    pe.wait_ge(hi_up.sem, shifted(r, body, hi_up.at(k + 1)))
                    if k >= 2:
                        pe.wait_ge(made.sem, shifted(r, 3 * body, made.at(3 * k - 5)))
                    for h in range(2):
                        for w_part, x_parts in ((up_hi, (x_hi, x_lo)), (up_lo, (x_hi,))):
                            if w_part is up_lo and h == 0:
                                if f == 0:
                                    pe.wait_ge(lo_up.sem, shifted(r, body // 2, lo_up.at(k // 2 + 1)))
                                else:
                                    pe.wait_ge(used, shifted(r, body, first + k // 2 * 2 + 1))
                            for c in range(DC):
                                for x_part in x_parts:
                                    last = pe.matmul(ps[:, 4 + f, h * SEQ:(h + 1) * SEQ], w_part[:, f, h, c, :],
                                                     x_part[:, c, :],
                                                     start=c == 0 and w_part is up_hi and x_part is x_hi,
                                                     stop=c == DC - 1 and w_part is up_lo)
                    last.then_inc(up_done.sem, 1)

                def step(k, r):
                    if k >= 2:
                        down(k - 2, r)
                    if k < steps_total:
                        up(k, r)

                all_steps(pe, step, steps_total + 2)

            @block.scalar
            def _(act):
                def high_up(k, r):
                    if k % 2 == 0:
                        arrived(act, first + k // 2 * 2, r)
                    if k >= 2:
                        act.wait_ge(up_done.sem, shifted(r, body, up_done.at(k - 1)))
                    act.copy(up_hi[:, k % 2], up_weights(k)).then_inc(hi_up.sem, 1)

                def high_down(k, r):
                    if k % 2 == 0:
                        arrived(act, first + k // 2 * 2 + 1, r)
                    if k >= 2:
                        act.wait_ge(down_done.sem, shifted(r, body, down_done.at(k - 1)))
                    act.copy(down_hi[:, k % 2], down_weights(k)).then_inc(hi_down.sem, 1)

                def step(k, r):
                    if k >= 1:
                        high_down(k - 1, r)
                    if k + 1 < steps_total:
                        high_up(k + 1, r)
                    if k < steps_total:
                        act.wait_ge(up_done.sem, shifted(r, body, up_done.at(k + 1)))
                        if k >= 2:
                            act.wait_ge(made.sem, shifted(r, 3 * body, made.at(3 * k - 5)))
                        act.activation(silu_g[:, k % 2, :], ps[:, 4 + k % 2, 0:SEQ], ACT.Silu).then_inc(silued.sem, 1)

                all_steps(act, step, steps_total + 1)
                sum_squares(act, updated)

            @block.vector
            def _(dve):
                def low_up(k, r):
                    dve.wait_ge(hi_up.sem, shifted(r, body, hi_up.at(k + 1)))
                    dve.tensor_tensor(up_lo[:, k % 2], up_weights(k), up_hi[:, k % 2].bitcast(F32), ALU.subtract
                                      ).then_inc(lo_up.sem if k % 2 == 0 else used, 1)

                def low_down(k, r):
                    dve.wait_ge(hi_down.sem, shifted(r, body, hi_down.at(k + 1)))
                    dve.tensor_tensor(down_lo[:, k % 2], down_weights(k), down_hi[:, k % 2].bitcast(F32), ALU.subtract
                                      ).then_inc(lo_down.sem if k % 2 == 0 else used, 1)

                def hidden_parts(k, r):
                    f = k % 2
                    dve.wait_ge(silued.sem, shifted(r, body, silued.at(k + 1)))
                    dve.tensor_tensor(hidden[:, f, :], silu_g[:, f, :], ps[:, 4 + f, SEQ:2 * SEQ],
                                      ALU.mult).then_inc(made.sem, 1)
                    if k >= 2:
                        dve.wait_ge(down_done.sem, shifted(r, body, down_done.at(k - 1)))
                    dve.wait_ge(made.sem, shifted(r, 3 * body, made.at(3 * k + 1)))
                    dve.tensor_copy(hid_hi[:, f, :], hidden[:, f, :]).then_inc(made.sem, 1)
                    dve.wait_ge(made.sem, shifted(r, 3 * body, made.at(3 * k + 2)))
                    dve.tensor_tensor(hid_lo[:, f, :], hidden[:, f, :], hid_hi[:, f, :].bitcast(F32),
                                      ALU.subtract).then_inc(made.sem, 1)

                def step(k, r):
                    if k >= 1:
                        low_down(k - 1, r)
                    if k + 1 < steps_total:
                        low_up(k + 1, r)
                    if k < steps_total:
                        hidden_parts(k, r)

                low_up(0, 0)
                all_steps(dve, step, steps_total + 1)
                dve.wait_ge(down_done.sem, down_done.at(steps_total))
                for a in range(TILES):
                    for h in range(2):
                        cols = slice(h * BANK, (h + 1) * BANK)
                        last = dve.scalar_tensor_tensor(out=x[:, a, cols], in0=ps[:, 2 * h + a, :], scalar=0.5,
                                                        in1=x[:, a, cols], op0=ALU.mult, op1=ALU.add)
                    last.then_inc(updated.sem, 1)
        for s in (hi_up, hi_down, up_done, down_done, silued):
            s.advance(steps_total)
        updated.advance(TILES)
        lo_up.advance(F_GROUPS), lo_down.advance(F_GROUPS), made.advance(3 * steps_total)

    def second_mixer(layer):
        mem = Arena()
        z = mem.take(TILES, IN_2)
        conv_mem = Arena(mem.at)
        decay = mem.take(RET_HEADS, TILES, SEQ)
        acc = mem.take(2, SEQ)
        conv_norm = mem.take(2, 2)
        assert mem.at <= PARTS_AT
        conv_pad = conv_mem.take(2, KERNEL - 1 + SEQ)
        taps = conv_mem.take(CONV_W)
        tap_cols = conv_mem.take(2, KERNEL + 1)
        qk_cols = mem.take(4 * RW // P, SEQ)
        after = mem.at
        scratch = mem.take(4, 2 * RET_HEADS * ROT_RET)
        moba_scratch = mem.take(TILES, 4, 2 * MOBA_HEADS * ROT_MOBA)
        square = mem.take(2, SEQ)
        centred = Arena(arena_size - 2 * SEQ).take(2, SEQ)
        assert mem.at <= arena_size - 2 * SEQ
        conv_root = acc
        o_rq, o_rv, o_rg = 0, 2 * RW, 3 * RW
        o_mq = 4 * RW
        o_mv = o_mq + 2 * MW
        o_ca, o_cg = o_mv + MW, o_mv + MW + CONV_W
        n_chunks = 4 * RW // P
        starts = [o_rq + i * P for i in range(2 * RW // P)] + [o_mq + i * P for i in range(2 * MW // P)]
        gated, conv_turned, conv_kept, padded, tapped = (signal(s) for s in (
            "conv_gated", "conv_inputs_turned", "conv_inputs_kept", "conv_padding_cleared", "taps_added"))
        freed = signal("projection_kept")

        def conv_on_tensor(pe, k):
            if k != 2:
                return
            params_ready(pe)
            for c in range(2):
                pe.transpose(ps[:, 7, c * (KERNEL + 1):(c + 1) * (KERNEL + 1)],
                             taps[0:KERNEL + 1, c * P:(c + 1) * P], ident[0:KERNEL + 1, 0:KERNEL + 1])
            pe.wait_ge(gated.sem, gated.at(1))
            for c in range(2):
                for a in range(TILES):
                    last = pe.transpose(ps[:, 6, c * SEQ + a * P:c * SEQ + (a + 1) * P],
                                        z[:, a, o_ca + c * P:o_ca + (c + 1) * P], ident[:, :])
            last.then_inc(conv_turned.sem, 1)

        def conv_on_scalar(act, k):
            if k == 3:
                act.wait_ge(padded.sem, padded.at(1))
                act.wait_ge(conv_turned.sem, conv_turned.at(1))
                act.copy(tap_cols, ps[:, 7, 0:2 * (KERNEL + 1)].rearrange("p (c k) -> p c k", c=2))
                act.copy(conv_pad[:, :, KERNEL - 1:],
                         ps[:, 6, :].rearrange("p (c q) -> p c q", c=2)).then_inc(conv_kept.sem, 1)

        def conv_on_gpsimd(pool):
            pool.memset(conv_pad[:, :, 0:KERNEL - 1], 0.0).then_inc(padded.sem, 1)
            pool.wait_ge(freed.sem, freed.at(TILES))
            pool.tensor_tensor(z[:, :, o_ca:o_ca + CONV_W], z[:, :, o_ca:o_ca + CONV_W],
                               z[:, :, o_cg:o_cg + CONV_W], ALU.mult).then_inc(gated.sem, 1)

        def add_tap(dve, j):
            for c in range(2):
                if j > 0:
                    dve.wait_ge(tapped.sem, tapped.at(2 * j + c - 1))
                window = conv_pad[:, c, j:j + SEQ]
                if j == 0:
                    last = dve.tensor_scalar(acc[:, c, :], window, tap_cols[:, c, 0:1],
                                             tap_cols[:, c, KERNEL:KERNEL + 1], ALU.mult, ALU.add)
                else:
                    last = dve.scalar_tensor_tensor(out=acc[:, c, :], in0=window, scalar=tap_cols[:, c, j:j + 1],
                                                    in1=acc[:, c, :], op0=ALU.mult, op1=ALU.add)
                last.then_inc(tapped.sem, 1)

        def conv_on_vector(dve, k):
            per_half = 4
            if k == 4:
                dve.wait_ge(conv_kept.sem, conv_kept.at(1))
            for j in range(max(k - 4, 0) * per_half, min((k - 3) * per_half, KERNEL)):
                add_tap(dve, j)

        job = projection(IN_2, range(6))
        rms_columns(t["mix_norm_2"][layer], 0, job.first_high, more_params=[
            (taps[0:KERNEL, :], t["conv_w_2"][layer]),
            (taps[KERNEL:KERNEL + 1, :], t["conv_b_2"][layer:layer + 1, :]),
            (conv_norm[:, 0, :], t["conv_ln_g_2"][layer].rearrange("(c p) -> p c", p=P)),
            (conv_norm[:, 1, :], t["conv_ln_b_2"][layer].rearrange("(c p) -> p c", p=P))])
        project(job, z, leading=2 * CONV_W, extra={"tensor": conv_on_tensor, "scalar": conv_on_scalar, "vector": conv_on_vector,
                   "gpsimd": conv_on_gpsimd},
            activated={o_ca: (CONV_W, ACT.Sigmoid), o_rg // BANK * BANK: (o_rg % BANK, ACT.Silu)})
        tapped.advance(2 * KERNEL)
        for s in (gated, conv_turned, conv_kept, padded):
            s.advance(1)

        turned, rotated_ret, rotated_moba = (signal(s) for s in (
            "columns_turned", "retention_heads_rotated", "block_heads_rotated"))
        means, centre_ready, sq, variances, rooted, scaled = (signal(s) for s in (
            "means_ready", "centred_ready", "squares_made", "variances_ready", "root_ready", "tokens_scaled"))
        with nc.Block() as block:
            @block.sync
            def _(sp):
                load_params(sp, (decay, t["c_decay"].rearrange("h a p q -> p h a q")))
                stream.issue(sp)

            def rotate_heads(engine, chain, a, offset, scratch, f0, n):
                nh = 2 * RET_HEADS
                view = z[:, a, offset:offset + nh * HD].rearrange("p (h d) -> p h d", d=HD)
                wide = [scratch[:, i, :].rearrange("p (h f) -> p h f", h=nh) for i in range(4)]
                cos, sin = (rope_2[:, a, i:i + 1, f0:f0 + n].broadcast_to([P, nh, n]) for i in range(2))
                return rotate(engine, view[:, :, 0:n], view[:, :, n:2 * n], cos, sin, wide, chain)

            @block.scalar
            def _(act):
                act.wait_ge(centre_ready.sem, centre_ready.at(1))
                act.activation(square, centred, ACT.Square).then_inc(sq.sem, 1)
                act.wait_ge(variances.sem, variances.at(1))
                act.activation(conv_root, ps[:, 7, :].rearrange("p (c q) -> p c q", c=2), ACT.Sqrt,
                               bias=EPS).then_inc(rooted.sem, 1)
                for g in range(n_chunks // 2):
                    act.wait_ge(turned.sem, turned.at(g + 1))
                    act.copy(qk_cols[:, 2 * g:2 * g + 2, :], ps[:, g, :].rearrange("p (c q) -> p c q", c=2))

            @block.vector
            def _(dve):
                dve.wait_ge(means.sem, means.at(1))
                dve.tensor_tensor(centred, acc, ps[:, 6, :].rearrange("p (c q) -> p c q", c=2),
                                  ALU.subtract).then_inc(centre_ready.sem, 1)
                for a in range(TILES):
                    last = rotate_heads(dve, dve_chain, a, o_rq, scratch, 0, ROT_RET)
                    if a + 1 < TILES:
                        dve_chain.link(dve, last)
                last.then_inc(rotated_ret.sem, 1)

            @block.gpsimd
            def _(pool):
                for a in range(TILES):
                    last = rotate_heads(pool, pool_chain, a, o_mq, moba_scratch[:, a], ROT_RET, ROT_MOBA)
                last.then_inc(rotated_moba.sem, 1)

            @block.tensor
            def _(pe):
                pe.matmul(ps[:, 6, :], group_mean[:, :], acc.rearrange("p c q -> p (c q)"), start=True,
                          stop=True).then_inc(means.sem, 1)
                pe.wait_ge(sq.sem, sq.at(1))
                pe.matmul(ps[:, 7, :], group_mean[:, :], square.rearrange("p c q -> p (c q)"), start=True,
                          stop=True).then_inc(variances.sem, 1)
                for g in range(n_chunks // 2):
                    if g == 0:
                        pe.wait_ge(rotated_ret.sem, rotated_ret.at(1))
                    if g == 2 * RW // P // 2:
                        pe.wait_ge(rotated_moba.sem, rotated_moba.at(1))
                    for i in range(2):
                        off = starts[2 * g + i]
                        for a in range(TILES):
                            last = pe.transpose(ps[:, g, i * SEQ + a * P:i * SEQ + (a + 1) * P],
                                                z[:, a, off:off + P], ident[:, :])
                    last.then_inc(turned.sem, 1)
        turned.advance(n_chunks // 2)
        for s in (rotated_ret, rotated_moba, means, centre_ready, sq, variances, rooted):
            s.advance(1)

        mem = Arena(after)
        y = mem.take(TILES, RW)
        squares = mem.take(TILES, RW)
        beside_mem = mem.at
        deep = 4
        s_buf = Arena(beside_mem).take(deep, TILES, SEQ)
        sums, roots = stat[:, 64:64 + TILES * RET_HEADS], stat[:, 80:80 + TILES * RET_HEADS]
        ret_scores, decayed, outs, outs_kept, summed, rooted, normed, mixed = (signal(s) for s in (
            "retention_scores", "scores_decayed", "outputs_ready", "outputs_kept", "squares_summed",
            "root_ready", "outputs_normed", "outputs_turned"))
        rc = RW // P

        class Retention:

            @staticmethod
            def tensor(pe, step):
                def score(h):
                    half = slice(h % 2 * HD, h % 2 * HD + HD)
                    if h >= deep:
                        pe.wait_ge(decayed.sem, decayed.at(h - deep + 1))
                    for b in range(TILES):
                        last = pe.matmul(ps[:, h % deep, b * SEQ + b * P:(b + 1) * SEQ],
                                         qk_cols[half, rc + h // 2, b * P:(b + 1) * P],
                                         qk_cols[half, h // 2, b * P:SEQ], start=True, stop=True)
                    last.then_inc(ret_scores.sem, 1)

                def sum_values(h):
                    pe.wait_ge(decayed.sem, decayed.at(h + 1))
                    for a in range(TILES):
                        for b in range(a + 1):
                            last = pe.matmul(ps[:, 4 + a, h * HD:(h + 1) * HD], s_buf[:, h % deep, b, a * P:(a + 1) * P],
                                             z[:, b, o_rv + h * HD:o_rv + (h + 1) * HD], start=b == 0, stop=b == a)
                    last.then_inc(outs.sem, 1)

                if step == -1:
                    for i in range(RET_HEADS + 2):
                        if i < RET_HEADS:
                            score(i)
                        if i >= 2:
                            sum_values(i - 2)
                elif step == 1:
                    pe.wait_ge(outs_kept.sem, outs_kept.at(1))
                elif step is None:
                    pe.wait_ge(normed.sem, normed.at(1))
                    for c in range(rc):
                        for a in range(TILES):
                            last = pe.transpose(ps[:, c // 2, c % 2 * SEQ + a * P:c % 2 * SEQ + (a + 1) * P],
                                                y[:, a, c * P:(c + 1) * P], ident[:, :])
                    last.then_inc(mixed.sem, 1)

            @staticmethod
            def vector(dve, step):
                if step == -1:
                    params_ready(dve)
                    for h in range(RET_HEADS):
                        if h == deep:
                            dve_chain.link(dve, dve.reciprocal(conv_root, conv_root))
                            dve.tensor_tensor(centred, centred, conv_root, ALU.mult).then_inc(scaled.sem, 1)
                        dve.wait_ge(ret_scores.sem, ret_scores.at(h + 1))
                        if h >= deep:
                            dve.wait_ge(outs.sem, outs.at(h - deep + 1))
                        for b in range(TILES):
                            last = dve.tensor_tensor(s_buf[:, h % deep, b, b * P:],
                                                     ps[:, h % deep, b * SEQ + b * P:(b + 1) * SEQ],
                                                     decay[:, h, b, b * P:], ALU.mult)
                        last.then_inc(decayed.sem, 1)
                elif step == 1:
                    dve.wait_ge(outs_kept.sem, outs_kept.at(1))
                    dve.tensor_reduce(sums.rearrange("p (a h) -> p a h", a=TILES),
                                      squares.rearrange("p a (h d) -> p a h d", d=HD), AX,
                                      ALU.add).then_inc(summed.sem, 1)
                elif step == 3:
                    dve.wait_ge(rooted.sem, rooted.at(1))
                    for a in range(TILES):
                        root = roots[:, a * RET_HEADS:(a + 1) * RET_HEADS].rearrange("p (h u) -> p h u", u=1)
                        view = y[:, a, :].rearrange("p (h d) -> p h d", d=HD)
                        last = dve.tensor_tensor(view, view, root.broadcast_to([P, RET_HEADS, HD]), ALU.mult)
                    dve_chain.link(dve, last)
                    dve.tensor_tensor(y, y, z[:, :, o_rg:o_rg + RW], ALU.mult).then_inc(normed.sem, 1)

            @staticmethod
            def scalar(act, step):
                if step == -1:
                    params_ready(act)
                    act.wait_ge(scaled.sem, scaled.at(1))
                    for c in range(2):
                        act.activation(mix_cols[:, 2 * rc + c, :], centred[:, c, :], ACT.Silu,
                                       scale=conv_norm[:, 0, c:c + 1], bias=conv_norm[:, 1, c:c + 1])
                    act.wait_ge(outs.sem, outs.at(RET_HEADS))
                    act.copy(y, ps[:, 4:4 + TILES, 0:RW])
                    act.activation(squares, ps[:, 4:4 + TILES, 0:RW], ACT.Square).then_inc(outs_kept.sem, 1)
                elif step is None:
                    act.wait_ge(mixed.sem, mixed.at(1))
                    act.copy(mix_cols[:, 0:2, :], ps[:, 0, :].rearrange("p (c q) -> p c q", c=2))
                    act.copy(mix_cols[:, 2, :], ps[:, 1, 0:SEQ])

            @staticmethod
            def gpsimd(pool):
                pool.wait_ge(summed.sem, summed.at(1))
                inverse_root(pool, roots, sums, HD).then_inc(rooted.sem, 1)

        half = lambda i: slice(i % 2 * HD, i % 2 * HD + HD)
        attention(MOBA_HEADS, lambda i: qk_cols[half(i), 2 * rc + i // 2, :],
                  lambda i: qk_cols[half(i), 3 * rc + i // 2, :],
                  lambda i, b: z[:, b, o_mv + i * HD:o_mv + (i + 1) * HD], RET_HEADS, HD ** -0.5, True,
                  Arena(beside_mem), beside=Retention)
        ret_scores.advance(RET_HEADS), decayed.advance(RET_HEADS), outs.advance(RET_HEADS)
        for s in (scaled, outs_kept, summed, rooted, normed, mixed):
            s.advance(1)

        job = PartedProducts(stream.take(2), D, x_hi, mix_lo, range(4), x_made=signal("mix_parts_made"))
        act_side, dve_side = mix_products(job)
        updated = signal("tiles_updated")
        with nc.Block() as block:
            @block.sync
            def _(sp):
                stream.issue(sp)

            @block.tensor
            def _(pe):
                job.products(pe, 0), job.products(pe, 1)

            @block.scalar
            def _(act):
                act_side(act)
                sum_squares(act, updated)

            @block.vector
            def _(dve):
                dve_side(dve)
                for h in range(2):
                    job.wait(dve, h)
                    for a in range(TILES):
                        cols = slice(h * BANK, (h + 1) * BANK)
                        last = dve.tensor_tensor(x[:, a, cols], x[:, a, cols], ps[:, 2 * h + a, :], ALU.add)
                        if h == 1:
                            last.then_inc(updated.sem, 1)
        job.close()
        job.x_made.advance(2), updated.advance(TILES)

    def final_norm():
        normed = Arena().take(TILES, D)
        roots = square_roots
        rooted, done, stored = (signal(s) for s in ("root_ready", "tokens_scaled", "output_stored"))
        with nc.Block() as block:
            @block.sync
            def _(sp):
                load_params(sp, (ln_params[:, 0, :], spread(t["final_norm_2"])))
                for a in range(TILES):
                    sp.wait_ge(done.sem, done.at(a + 1))
                    sp.dma_start(out[0, a * P:(a + 1) * P, :], normed[:, a, :]).then_inc(stored.sem, 16)
                sp.wait_ge(stored.sem, 16 * TILES)

            @block.gpsimd
            def _(pool):
                inverse_root(pool, roots, square_sums, D).then_inc(rooted.sem, 1)

            @block.vector
            def _(dve):
                params_ready(dve)
                dve.wait_ge(rooted.sem, rooted.at(1))
                for a in range(TILES):
                    dve.scalar_tensor_tensor(out=normed[:, a, :], in0=x[:, a, :], scalar=roots[:, a:a + 1],
                                             in1=ln_params[:, 0, :], op0=ALU.mult, op1=ALU.mult).then_inc(done.sem, 1)

    h, base, log_decays, gla_gain = even_mixer()
    gla(h, base, log_decays, gla_gain)
    mix_out_norm()
    experts(0)
    odd_mixer()
    mix_out_norm()
    experts(1)
    for layer in range(DEPTH):
        ffn(t["ffn1_norm_2"][layer])
        second_mixer(layer)
        ffn(t["ffn2_norm_2"][layer])
    final_norm()


INPUTS = ["x", "p", "w_in_even", "mla_q_norm", "w_uq", "mla_kv_norm", "w_ukv", "gla_gate_w_fwd", "gla_gate_b_fwd",
          "gla_gate_w_bwd", "gla_gate_b_bwd", "gla_norm", "w_in_odd", "gqa_q_norm", "gqa_k_norm", "w_o", "ln1_g",
          "ln1_b", "router_w", "w1", "w3", "w2", "ple_gate_w", "ple_gate_b", "ple_w", "ln2_g", "ln2_b",
          "positions_2", "ffn1_norm_2", "ffn1_wg_2", "ffn1_wu_2", "ffn1_wd_2", "mix_norm_2", "w_in_2", "conv_w_2",
          "conv_b_2", "conv_ln_g_2", "conv_ln_b_2", "w_out_2", "ffn2_norm_2", "ffn2_wg_2", "ffn2_wu_2", "ffn2_wd_2",
          "final_norm_2"]


def kernel(**inputs):
    import concourse.bacc as bacc
    from concourse.bass_utils import run_bass_kernel_spmd

    nc = bacc.Bacc("TRN2", target_bir_lowering=False, num_devices=1)
    arrays = {name: np.ascontiguousarray(inputs[name]) for name in INPUTS}
    arrays.update(shape_constants())
    tensors = {name: nc.dram_tensor(f"in_{name}", a.shape, mybir.dt.from_np(a.dtype), kind="ExternalInput").ap()
               for name, a in arrays.items()}
    out = nc.dram_tensor("out", (1, SEQ, D), F32, kind="ExternalOutput").ap()
    build_program(nc, tensors, out)
    result = run_bass_kernel_spmd(nc, [{f"in_{name}": a for name, a in arrays.items()}], core_ids=[0])
    return result.results[0]["out"]
```
